# Optimizing a Trainium2 kernel written in Bass

```python
import math
import jax, jax.numpy as jnp
from jax import lax
import numpy as np

D_MODEL = 1024
BATCH = 1
SEQ = 256
DEPTH = 1

MEM_LEN = 256
RMS_EPS = 1e-6
NEG_INF = -1e30
FORCE = 1e6

POOL_WINDOWS = (2, 4, 8, 16)
POOL_GROUPS = len(POOL_WINDOWS)
POOL_GROUP_DIM = D_MODEL // 8
POOL_WIDTH = POOL_GROUPS * POOL_GROUP_DIM

NSA_HEADS = 16
NSA_KV_HEADS = 4
NSA_GROUP = NSA_HEADS // NSA_KV_HEADS
HEAD_DIM = 64
NSA_WIDTH = NSA_HEADS * HEAD_DIM
KV_WIDTH = NSA_KV_HEADS * HEAD_DIM
CMP_LEN = 32
CMP_STRIDE = 16
SEL_BLOCK = 64
N_SELECT = 16
WINDOW = 512
NSA_Q_BLOCK = 64

X_HEADS = 4
X_HEAD_DIM = 128
X_WIDTH = X_HEADS * X_HEAD_DIM

N_BUCKETS = 32
MAX_DISTANCE = 128

PEER_HEADS = 8
N_KEYS = 128
N_EXPERTS = N_KEYS * N_KEYS
PEER_QDIM = 256
PEER_HALF = PEER_QDIM // 2
PEER_TOPK = 16
PEER_TOKEN_BLOCK = 128

N_BRANCHES = 3
IN_WIDTHS = (POOL_WIDTH, NSA_WIDTH, 6 * KV_WIDTH, 3 * NSA_HEADS, X_WIDTH, N_BRANCHES * D_MODEL)
IN_SPLITS = tuple(int(s) for s in np.cumsum(IN_WIDTHS)[:-1])
D_IN = int(sum(IN_WIDTHS))


def rms_norm(x, g):
    xf = x.astype(jnp.float32)
    y = xf * lax.rsqrt(jnp.mean(xf * xf, axis=-1, keepdims=True) + RMS_EPS)
    return (y * g.astype(jnp.float32)).astype(x.dtype)

def masked_softmax(s, mask):
    return jax.nn.softmax(jnp.where(mask, s, NEG_INF), axis=-1)

def t5_bucket(dist):
    n = jnp.maximum(dist, 0)
    max_exact = N_BUCKETS // 2
    nf = jnp.maximum(n, 1).astype(jnp.float32)
    large = max_exact + (jnp.log(nf / max_exact) / math.log(MAX_DISTANCE / max_exact)
                         * (N_BUCKETS - max_exact)).astype(jnp.int32)
    large = jnp.minimum(large, N_BUCKETS - 1)
    return jnp.where(n < max_exact, n, large)

def pool_mixer(u, w_grp, scale):
    B, T, _ = u.shape
    c = jnp.cumsum(u.astype(jnp.float32), axis=1)
    t_idx = jnp.arange(T)
    outs = []
    for g, w in enumerate(POOL_WINDOWS):
        sl = slice(g * POOL_GROUP_DIM, (g + 1) * POOL_GROUP_DIM)
        cg = c[..., sl]
        shifted = jnp.pad(cg, ((0, 0), (w, 0), (0, 0)))[:, :T]
        cnt = jnp.minimum(t_idx + 1, w).astype(jnp.float32)[None, :, None]
        outs.append((cg - shifted) / cnt - u[..., sl].astype(jnp.float32))
    pooled = jnp.stack(outs, axis=2)
    mixed = jnp.einsum('btgc,gcd->btgd', pooled, w_grp.astype(jnp.float32))
    return (mixed.reshape(B, T, POOL_WIDTH) * scale.astype(jnp.float32)).astype(u.dtype)

def nsa_attention(q, k_cmp_tok, v_cmp_tok, k_sel, v_sel, k_win, v_win,
                  w_cmp_k, w_cmp_v, pe_k, pe_v, rel_bias):
    B, T = q.shape[:2]
    G, R, dh = NSA_KV_HEADS, NSA_GROUP, HEAD_DIM
    QB = NSA_Q_BLOCK
    n_cmp = (T - CMP_LEN) // CMP_STRIDE + 1
    n_sel = T // SEL_BLOCK
    n_top = min(N_SELECT, n_sel)

    cmp_start = jnp.arange(n_cmp) * CMP_STRIDE
    cmp_end = cmp_start + CMP_LEN - 1
    tok_idx = cmp_start[:, None] + jnp.arange(CMP_LEN)[None, :]

    def compress(tok, pe, w):
        blk = tok[:, tok_idx] + pe[None, None, :, None, :]
        blk = blk.transpose(0, 1, 3, 2, 4).reshape(B, n_cmp, G, CMP_LEN * dh)
        return blk @ w

    kc = compress(k_cmp_tok, pe_k, w_cmp_k)
    vc = compress(v_cmp_tok, pe_v, w_cmp_v)

    sel_start = jnp.arange(n_sel) * SEL_BLOCK
    overlap = ((cmp_start[:, None] < sel_start[None, :] + SEL_BLOCK) &
               (cmp_start[:, None] + CMP_LEN > sel_start[None, :])).astype(jnp.float32)

    ks_blk = k_sel.reshape(B, n_sel, SEL_BLOCK, G, dh).transpose(0, 3, 1, 2, 4)
    vs_blk = v_sel.reshape(B, n_sel, SEL_BLOCK, G, dh).transpose(0, 3, 1, 2, 4)
    kw_pad = jnp.pad(k_win, ((0, 0), (WINDOW, 0), (0, 0), (0, 0)))
    vw_pad = jnp.pad(v_win, ((0, 0), (WINDOW, 0), (0, 0), (0, 0)))

    qg = q.reshape(B, T, G, R, dh) * (dh ** -0.5)
    table_gr = rel_bias.astype(jnp.float32).reshape(N_BUCKETS, G, R)
    bi = jnp.arange(B)[:, None, None, None]
    gi = jnp.arange(G)[None, :, None, None]
    gi5 = jnp.arange(G)[None, :, None, None, None]
    sel_ids = jnp.arange(n_sel)
    win_off = jnp.arange(WINDOW + QB)

    def head_bias(dist):
        return table_gr[t5_bucket(dist)].transpose(2, 3, 0, 1)

    def block(t0):
        qb = lax.dynamic_slice_in_dim(qg, t0, QB, axis=1)
        tq = t0 + jnp.arange(QB)

        dist_c = tq[:, None] - cmp_end[None, :]
        mask_c = dist_c >= 0
        s_c = jnp.einsum('bqgrd,bcgd->bgrqc', qb, kc).astype(jnp.float32) + head_bias(dist_c)
        has = jnp.any(mask_c, axis=-1).astype(jnp.float32)
        p_c = masked_softmax(s_c, mask_c) * has[None, None, None, :, None]
        o_c = jnp.einsum('bgrqc,bcgd->bqgrd', p_c.astype(vc.dtype), vc)

        imp = jnp.einsum('bgrqc,cs->bgqs', p_c, overlap)
        blk_q = tq // SEL_BLOCK
        forced = ((sel_ids[None, :] == 0) | (sel_ids[None, :] == blk_q[:, None]) |
                  (sel_ids[None, :] == blk_q[:, None] - 1))
        causal_blk = sel_ids[None, :] <= blk_q[:, None]
        imp = jnp.where(forced, FORCE, jnp.where(causal_blk, imp, -FORCE))
        _, idx = lax.top_k(imp, n_top)

        k_g = ks_blk[bi, gi, idx]
        v_g = vs_blk[bi, gi, idx]
        pos = idx[..., None] * SEL_BLOCK + jnp.arange(SEL_BLOCK)
        dist_s = tq[None, None, :, None, None] - pos
        bias_s = jnp.moveaxis(table_gr[t5_bucket(dist_s), gi5], -1, 2)
        nk = n_top * SEL_BLOCK
        s_s = jnp.einsum('bqgrd,bgqkld->bgrqkl', qb, k_g).astype(jnp.float32) + bias_s
        s_s = s_s.reshape(B, G, R, QB, nk)
        mask_s = (dist_s >= 0).reshape(B, G, 1, QB, nk)
        p_s = masked_softmax(s_s, mask_s)
        o_s = jnp.einsum('bgrqn,bgqnd->bqgrd', p_s.astype(v_g.dtype), v_g.reshape(B, G, QB, nk, dh))

        k_w = lax.dynamic_slice_in_dim(kw_pad, t0, WINDOW + QB, axis=1)
        v_w = lax.dynamic_slice_in_dim(vw_pad, t0, WINDOW + QB, axis=1)
        pos_w = t0 - WINDOW + win_off
        dist_w = tq[:, None] - pos_w[None, :]
        mask_w = (dist_w >= 0) & (dist_w < WINDOW) & (pos_w[None, :] >= 0)
        s_w = jnp.einsum('bqgrd,bkgd->bgrqk', qb, k_w).astype(jnp.float32) + head_bias(dist_w)
        p_w = masked_softmax(s_w, mask_w)
        o_w = jnp.einsum('bgrqk,bkgd->bqgrd', p_w.astype(v_w.dtype), v_w)
        return (o_c, o_s, o_w)

    o_c, o_s, o_w = lax.map(block, jnp.arange(T // QB) * QB)

    def unblock(o):
        return o.transpose(1, 0, 2, 3, 4, 5).reshape(B, T, NSA_HEADS, dh).astype(q.dtype)

    return unblock(o_c), unblock(o_s), unblock(o_w)

def memory_cross_attention(q_x, mem, g_mem, w_mem_kv):
    B, T, _ = q_x.shape
    M = mem.shape[1]
    kv = rms_norm(mem, g_mem) @ w_mem_kv
    k, v = jnp.split(kv, 2, axis=-1)
    q = q_x.reshape(B, T, X_HEADS, X_HEAD_DIM) * (X_HEAD_DIM ** -0.5)
    k = k.reshape(B, M, X_HEADS, X_HEAD_DIM)
    v = v.reshape(B, M, X_HEADS, X_HEAD_DIM)
    s = jnp.einsum('bthd,bmhd->bhtm', q, k).astype(jnp.float32)
    p = jax.nn.softmax(s, axis=-1).astype(v.dtype)
    return jnp.einsum('bhtm,bmhd->bthd', p, v).reshape(B, T, X_WIDTH)

def peer_ffn(h, w_q, sub_keys, u, v):
    B, T, D = h.shape
    tokens = h.reshape(-1, D)
    blocks = tokens.reshape(-1, PEER_TOKEN_BLOCK, D)
    n = PEER_TOKEN_BLOCK

    def block(xb):
        q = (xb @ w_q).reshape(n, PEER_HEADS, 2, PEER_HALF)
        s = jnp.einsum('nhpc,hpkc->nhpk', q, sub_keys).astype(jnp.float32)
        s_top, i_top = lax.top_k(s, PEER_TOPK)
        cand_s = (s_top[:, :, 0, :, None] + s_top[:, :, 1, None, :]).reshape(n, PEER_HEADS, -1)
        cand_i = (i_top[:, :, 0, :, None] * N_KEYS + i_top[:, :, 1, None, :]).reshape(n, PEER_HEADS, -1)
        best_s, best_pos = lax.top_k(cand_s, PEER_TOPK)
        ids = jnp.take_along_axis(cand_i, best_pos, axis=-1)
        gate = jax.nn.softmax(best_s, axis=-1)
        u_e = u[ids]
        act = jax.nn.gelu(jnp.einsum('nd,nhkd->nhk', xb, u_e).astype(jnp.float32), approximate=False)
        wgt = (gate * act).astype(xb.dtype)
        return jnp.einsum('nhk,nhkd->nd', wgt, v[ids])

    return lax.map(block, blocks).reshape(B, T, D)

def first_inputs(seed: int = 0) -> dict:
    key = jax.random.key(seed)
    ks = jax.random.split(key, 24)

    def nrm(k, shape, scale):
        return jax.random.normal(k, shape, jnp.float32) * scale

    D = D_MODEL
    return {
        "x": nrm(ks[0], (BATCH, SEQ, D), 1.0),
        "mem": nrm(ks[1], (BATCH, MEM_LEN, D), 1.0),
        "rel_bias": nrm(ks[2], (N_BUCKETS, NSA_HEADS), 0.5),
        "g_mix": 1.0 + nrm(ks[3], (DEPTH, D), 0.05),
        "w_in": nrm(ks[4], (DEPTH, D, D_IN), D ** -0.5),
        "w_pool_grp": nrm(ks[5], (DEPTH, POOL_GROUPS, POOL_GROUP_DIM, POOL_GROUP_DIM), POOL_GROUP_DIM ** -0.5),
        "pool_scale": 1.0 + nrm(ks[6], (DEPTH, POOL_WIDTH), 0.1),
        "w_pool_out": nrm(ks[7], (DEPTH, POOL_WIDTH, D), POOL_WIDTH ** -0.5),
        "w_cmp_k": nrm(ks[8], (DEPTH, CMP_LEN * HEAD_DIM, HEAD_DIM), (CMP_LEN * HEAD_DIM) ** -0.5),
        "w_cmp_v": nrm(ks[9], (DEPTH, CMP_LEN * HEAD_DIM, HEAD_DIM), (CMP_LEN * HEAD_DIM) ** -0.5),
        "pe_k": nrm(ks[10], (DEPTH, CMP_LEN, HEAD_DIM), 0.5),
        "pe_v": nrm(ks[11], (DEPTH, CMP_LEN, HEAD_DIM), 0.5),
        "w_nsa_out": nrm(ks[12], (DEPTH, NSA_WIDTH, D), NSA_WIDTH ** -0.5),
        "g_mem": 1.0 + nrm(ks[13], (DEPTH, D), 0.05),
        "w_mem_kv": nrm(ks[14], (DEPTH, D, 2 * X_WIDTH), D ** -0.5),
        "w_x_out": nrm(ks[15], (DEPTH, X_WIDTH, D), X_WIDTH ** -0.5),
        "w_o": nrm(ks[16], (DEPTH, D, D), D ** -0.5),
        "g_ffn": 1.0 + nrm(ks[17], (DEPTH, D), 0.05),
        "w_peer_q": nrm(ks[18], (DEPTH, D, PEER_HEADS * PEER_QDIM), D ** -0.5),
        "peer_sub_keys": nrm(ks[19], (DEPTH, PEER_HEADS, 2, N_KEYS, PEER_HALF), PEER_HALF ** -0.5),
        "peer_u": nrm(ks[20], (DEPTH, N_EXPERTS, D), D ** -0.5),
        "peer_v": nrm(ks[21], (DEPTH, N_EXPERTS, D), 0.1),
        "g_final": 1.0 + nrm(ks[22], (D,), 0.05),
    }

def first_block(x, mem, rel_bias, g_mix, w_in, w_pool_grp, pool_scale, w_pool_out,
              w_cmp_k, w_cmp_v, pe_k, pe_v, w_nsa_out, g_mem, w_mem_kv, w_x_out, w_o,
              g_ffn, w_peer_q, peer_sub_keys, peer_u, peer_v, g_final):
    B, T, D = x.shape
    for l in range(DEPTH):
        hn = rms_norm(x, g_mix[l])
        z = hn @ w_in[l]
        u_pool, q_nsa, kv_nsa, g_nsa, q_x, g_merge = jnp.split(z, IN_SPLITS, axis=-1)

        y_pool = pool_mixer(u_pool, w_pool_grp[l], pool_scale[l]) @ w_pool_out[l]

        kv = kv_nsa.reshape(B, T, 6, NSA_KV_HEADS, HEAD_DIM)
        o_c, o_s, o_w = nsa_attention(q_nsa.reshape(B, T, NSA_HEADS, HEAD_DIM),
                                      kv[:, :, 0], kv[:, :, 1], kv[:, :, 2], kv[:, :, 3],
                                      kv[:, :, 4], kv[:, :, 5],
                                      w_cmp_k[l], w_cmp_v[l], pe_k[l], pe_v[l], rel_bias)
        bg = jax.nn.sigmoid(g_nsa.reshape(B, T, 3, NSA_HEADS))[..., None]
        o_nsa = (bg[:, :, 0] * o_c + bg[:, :, 1] * o_s + bg[:, :, 2] * o_w).reshape(B, T, NSA_WIDTH)
        y_nsa = o_nsa @ w_nsa_out[l]

        y_mem = memory_cross_attention(q_x, mem, g_mem[l], w_mem_kv[l]) @ w_x_out[l]

        gm = jax.nn.sigmoid(g_merge.reshape(B, T, N_BRANCHES, D))
        merged = gm[:, :, 0] * y_pool + gm[:, :, 1] * y_nsa + gm[:, :, 2] * y_mem
        x = x + merged @ w_o[l]

        x = x + peer_ffn(rms_norm(x, g_ffn[l]), w_peer_q[l], peer_sub_keys[l], peer_u[l], peer_v[l])
    return rms_norm(x, g_final)


DEPTH_2 = 2

CHUNK = 64
Q_BLOCK = 128
N_MIXERS = 2
N_MLA_LAYERS = (DEPTH_2 + 1) // 2
N_FOX_LAYERS = DEPTH_2 // 2
D_FF = 256 * ((8 * D_MODEL // 3 + 255) // 256)
PLE_DIM = 256
MLA_HEADS = 8
MLA_NOPE = 128
MLA_ROPE = 64
MLA_V = 128
MLA_Q_LORA = 256
MLA_KV_LORA = 128
ROPE_THETA = 10000.0
FOX_HEADS = 8
FOX_HEAD_DIM = 128
NORM_EPS = 1e-6
NEG_INF_2 = -1e30


def rms_norm_2(x, g):
    xf = x.astype(jnp.float32)
    y = xf * lax.rsqrt(jnp.mean(xf * xf, axis=-1, keepdims=True) + NORM_EPS)
    return (y * g.astype(jnp.float32)).astype(x.dtype)

def swiglu(x, w_in, w_out):
    gate, up = jnp.split(x @ w_in, 2, axis=-1)
    return (jax.nn.silu(gate) * up) @ w_out

def apply_rope(x, cos, sin):
    x1, x2 = jnp.split(x, 2, axis=-1)
    return jnp.concatenate([x1 * cos - x2 * sin, x2 * cos + x1 * sin], axis=-1)

def causal_block_attention(scores_fn, v, chunk_causal):
    seq = v.shape[1]
    outs = []
    for q0 in range(0, seq, Q_BLOCK):
        q1 = q0 + Q_BLOCK
        s = scores_fn(q0, q1)
        q_pos = jnp.arange(q0, q1)
        k_pos = jnp.arange(q1)
        if chunk_causal:
            allowed = (k_pos[None, :] // CHUNK) <= (q_pos[:, None] // CHUNK)
        else:
            allowed = k_pos[None, :] <= q_pos[:, None]
        s = jnp.where(allowed, s, NEG_INF_2)
        probs = jax.nn.softmax(s, axis=-1).astype(v.dtype)
        outs.append(jnp.einsum('bhqk,bkhd->bqhd', probs, v[:, :q1]))
    return jnp.concatenate(outs, axis=1)

def mla_mixer(u, cos, sin, w_down, q_norm, w_uq, kv_norm, w_ukv, w_o):
    b, s, _ = u.shape
    c = u @ w_down
    c_q, c_kv, k_rope = jnp.split(c, [MLA_Q_LORA, MLA_Q_LORA + MLA_KV_LORA], axis=-1)
    q = (rms_norm_2(c_q, q_norm) @ w_uq).reshape(b, s, MLA_HEADS, MLA_NOPE + MLA_ROPE)
    q_nope, q_rope = jnp.split(q, [MLA_NOPE], axis=-1)
    q_rope = apply_rope(q_rope, cos[:, :, None, :], sin[:, :, None, :])
    k_rope = apply_rope(k_rope, cos, sin)
    kv = (rms_norm_2(c_kv, kv_norm) @ w_ukv).reshape(b, s, MLA_HEADS, MLA_NOPE + MLA_V)
    k_nope, v = jnp.split(kv, [MLA_NOPE], axis=-1)
    scale = (MLA_NOPE + MLA_ROPE) ** -0.5

    def scores(q0, q1):
        sc = (jnp.einsum('bqhd,bkhd->bhqk', q_nope[:, q0:q1], k_nope[:, :q1])
              + jnp.einsum('bqhr,bkr->bhqk', q_rope[:, q0:q1], k_rope[:, :q1]))
        return sc.astype(jnp.float32) * scale

    o = causal_block_attention(scores, v, chunk_causal=True)
    return o.reshape(b, s, MLA_HEADS * MLA_V) @ w_o

def fox_mixer(u, w_in, b_f, w_o):
    b, s, _ = u.shape
    hd = FOX_HEADS * FOX_HEAD_DIM
    proj = u @ w_in
    q, k, v, f_logit = jnp.split(proj, [hd, 2 * hd, 3 * hd], axis=-1)
    q = q.reshape(b, s, FOX_HEADS, FOX_HEAD_DIM)
    k = k.reshape(b, s, FOX_HEADS, FOX_HEAD_DIM)
    v = v.reshape(b, s, FOX_HEADS, FOX_HEAD_DIM)
    log_f = jax.nn.log_sigmoid(f_logit.astype(jnp.float32) + b_f.astype(jnp.float32))
    cum = jnp.cumsum(log_f, axis=1).transpose(0, 2, 1)
    scale = FOX_HEAD_DIM ** -0.5

    def scores(q0, q1):
        sc = jnp.einsum('bqhd,bkhd->bhqk', q[:, q0:q1], k[:, :q1]).astype(jnp.float32) * scale
        return sc + cum[:, :, q0:q1, None] - cum[:, :, None, :q1]

    o = causal_block_attention(scores, v, chunk_causal=False)
    return o.reshape(b, s, hd) @ w_o

def second_inputs(seed: int = 0) -> dict:
    key = jax.random.key(seed)
    ks = jax.random.split(key, 20)
    f32 = jnp.float32

    def dense(k, shape, fan_in):
        return jax.random.normal(k, shape, f32) * (fan_in ** -0.5)

    def gain(k, shape):
        return 1.0 + 0.05 * jax.random.normal(k, shape, f32)

    x = jax.random.normal(ks[0], (BATCH, SEQ, D_MODEL), f32)
    p = jax.random.normal(ks[1], (DEPTH_2, BATCH, SEQ, PLE_DIM), f32)
    offset = jax.random.randint(ks[2], (BATCH, 1), 0, 4096, dtype=jnp.int32)
    positions = (offset + jnp.arange(SEQ, dtype=jnp.int32)[None, :]).astype(jnp.int32)

    ffn_norm = gain(ks[3], (DEPTH_2, 2, D_MODEL))
    ffn_w_in = dense(ks[4], (DEPTH_2, 2, D_MODEL, 2 * D_FF), D_MODEL)
    ffn_w_out = dense(ks[5], (DEPTH_2, 2, D_FF, D_MODEL), D_FF)
    mix_norm = gain(ks[6], (DEPTH_2, D_MODEL))

    mla_w_down = dense(ks[7], (N_MLA_LAYERS, D_MODEL, MLA_Q_LORA + MLA_KV_LORA + MLA_ROPE), D_MODEL)
    mla_q_norm = gain(ks[8], (N_MLA_LAYERS, MLA_Q_LORA))
    mla_w_uq = dense(ks[9], (N_MLA_LAYERS, MLA_Q_LORA, MLA_HEADS * (MLA_NOPE + MLA_ROPE)), MLA_Q_LORA)
    mla_kv_norm = gain(ks[10], (N_MLA_LAYERS, MLA_KV_LORA))
    mla_w_ukv = dense(ks[11], (N_MLA_LAYERS, MLA_KV_LORA, MLA_HEADS * (MLA_NOPE + MLA_V)), MLA_KV_LORA)
    mla_w_o = dense(ks[12], (N_MLA_LAYERS, MLA_HEADS * MLA_V, D_MODEL), MLA_HEADS * MLA_V)

    fox_hd = FOX_HEADS * FOX_HEAD_DIM
    fox_w_in = dense(ks[13], (N_FOX_LAYERS, D_MODEL, 3 * fox_hd + FOX_HEADS), D_MODEL)
    fox_w_in = fox_w_in.at[..., 3 * fox_hd:].multiply(0.1)
    fox_b_f = jax.random.uniform(ks[14], (N_FOX_LAYERS, FOX_HEADS), f32, minval=1.0, maxval=6.0)
    fox_w_o = dense(ks[15], (N_FOX_LAYERS, fox_hd, D_MODEL), fox_hd)

    ple_norm = gain(ks[16], (DEPTH_2, D_MODEL))
    ple_w_gate = dense(ks[17], (DEPTH_2, D_MODEL, D_MODEL), D_MODEL)
    ple_w_proj = dense(ks[18], (DEPTH_2, PLE_DIM, D_MODEL), PLE_DIM)
    final_norm = gain(ks[19], (D_MODEL,))

    return {"x": x, "p": p, "positions": positions,
            "ffn_norm": ffn_norm, "ffn_w_in": ffn_w_in, "ffn_w_out": ffn_w_out,
            "mix_norm": mix_norm,
            "mla_w_down": mla_w_down, "mla_q_norm": mla_q_norm, "mla_w_uq": mla_w_uq,
            "mla_kv_norm": mla_kv_norm, "mla_w_ukv": mla_w_ukv, "mla_w_o": mla_w_o,
            "fox_w_in": fox_w_in, "fox_b_f": fox_b_f, "fox_w_o": fox_w_o,
            "ple_norm": ple_norm, "ple_w_gate": ple_w_gate, "ple_w_proj": ple_w_proj,
            "final_norm": final_norm}

def second_block(x, p, positions, ffn_norm, ffn_w_in, ffn_w_out, mix_norm,
              mla_w_down, mla_q_norm, mla_w_uq, mla_kv_norm, mla_w_ukv, mla_w_o,
              fox_w_in, fox_b_f, fox_w_o, ple_norm, ple_w_gate, ple_w_proj, final_norm):
    inv_freq = ROPE_THETA ** (-jnp.arange(0, MLA_ROPE, 2, dtype=jnp.float32) / MLA_ROPE)
    ang = positions.astype(jnp.float32)[..., None] * inv_freq
    cos = jnp.cos(ang).astype(x.dtype)
    sin = jnp.sin(ang).astype(x.dtype)

    h = x
    for i in range(DEPTH_2):
        h = h + 0.5 * swiglu(rms_norm_2(h, ffn_norm[i, 0]), ffn_w_in[i, 0], ffn_w_out[i, 0])
        u = rms_norm_2(h, mix_norm[i])
        j = i // N_MIXERS
        if i % N_MIXERS == 0:
            h = h + mla_mixer(u, cos, sin, mla_w_down[j], mla_q_norm[j], mla_w_uq[j],
                              mla_kv_norm[j], mla_w_ukv[j], mla_w_o[j])
        else:
            h = h + fox_mixer(u, fox_w_in[j], fox_b_f[j], fox_w_o[j])
        h = h + 0.5 * swiglu(rms_norm_2(h, ffn_norm[i, 1]), ffn_w_in[i, 1], ffn_w_out[i, 1])
        gate = jax.nn.sigmoid(rms_norm_2(h, ple_norm[i]) @ ple_w_gate[i])
        h = h + gate * (p[i] @ ple_w_proj[i])
    return rms_norm_2(h, final_norm)


def setup_inputs(seed=0):
    out = dict(first_inputs(seed))
    for name, value in second_inputs(seed + 1).items():
        if name != "x":
            out[name + "_2"] = value
    return out


def reference(
    x, mem, rel_bias, g_mix, w_in, w_pool_grp, pool_scale, w_pool_out, w_cmp_k, w_cmp_v, pe_k,
    pe_v, w_nsa_out, g_mem, w_mem_kv, w_x_out, w_o, g_ffn, w_peer_q, peer_sub_keys, peer_u,
    peer_v, g_final, p_2, positions_2, ffn_norm_2, ffn_w_in_2, ffn_w_out_2, mix_norm_2,
    mla_w_down_2, mla_q_norm_2, mla_w_uq_2, mla_kv_norm_2, mla_w_ukv_2, mla_w_o_2, fox_w_in_2,
    fox_b_f_2, fox_w_o_2, ple_norm_2, ple_w_gate_2, ple_w_proj_2, final_norm_2,
):
    x = first_block(
        x, mem, rel_bias, g_mix, w_in, w_pool_grp, pool_scale, w_pool_out, w_cmp_k, w_cmp_v,
        pe_k, pe_v, w_nsa_out, g_mem, w_mem_kv, w_x_out, w_o, g_ffn, w_peer_q, peer_sub_keys,
        peer_u, peer_v, g_final,
    )
    return second_block(
        x, p_2, positions_2, ffn_norm_2, ffn_w_in_2, ffn_w_out_2, mix_norm_2, mla_w_down_2,
        mla_q_norm_2, mla_w_uq_2, mla_kv_norm_2, mla_w_ukv_2, mla_w_o_2, fox_w_in_2, fox_b_f_2,
        fox_w_o_2, ple_norm_2, ple_w_gate_2, ple_w_proj_2, final_norm_2,
    )


_drawn_inputs = setup_inputs


def setup_inputs(seed=0):
    import zlib

    import numpy as np

    out = dict(_drawn_inputs(seed))
    spreads = {}
    factors = {'pe_k': 64.0,
     'g_mem': 8.0,
     'g_ffn': 5.171,
     'mix_norm_2': 2.75,
     'mla_q_norm_2': 8.0,
     'mla_kv_norm_2': 4.76,
     'ple_norm_2': 21.655}
    for name, (base, spread) in spreads.items():
        noise = np.random.default_rng([zlib.crc32(name.encode()), seed]).standard_normal(out[name].shape)
        drawn = base * np.exp(spread * noise) if base else spread * noise
        out[name] = __import__('jax').numpy.asarray(drawn.astype(out[name].dtype))
    for name, factor in factors.items():
        out[name] = (out[name] * factor).astype(out[name].dtype)
    return out
```

```python
import math
from contextlib import ExitStack

import concourse.bass as bass
from concourse import mybir

ALU = mybir.AluOpType
ACT = mybir.ActivationFunctionType
F32 = mybir.dt.float32
U32 = mybir.dt.uint32
F32R = mybir.dt.float32r
I32 = mybir.dt.int32
AX_X = mybir.AxisListType.X

P = 128
T = 256
TT = T // P
D = 1024
DC = D // P
POOL_W, NSA_W, KV_W = 512, 1024, 256
NSA_HEADS, NSA_GROUPS, HEAD = 16, 4, 64
HEADS_PER_GROUP = NSA_HEADS // NSA_GROUPS
CMP_LEN, CMP_STRIDE = 32, 16
N_CMP = (T - CMP_LEN) // CMP_STRIDE + 1
CMP_SLOT = 32
LP = CMP_LEN // 2
X_HEADS = 4
BUCKETS = 32
PEER_HEADS, KEYS, TOPK = 8, 128, 16
SLOTS = PEER_HEADS * TOPK
D_FF = 2816
FC = D_FF // P
MLA_HEADS, ROPE = 8, 64
FOX_HEADS = 8
NEG = -1e30
EPS = 1e-6
MAGIC = 1.5 * 2.0 ** 23
TWO_PI_PARTS = (6.28125, 0.00193500518798828125, 2 * math.pi - 6.28125 - 0.00193500518798828125)
INV_TWO_PI = 0.15915494309189535

Z_POOL, Z_Q, Z_KV = 0, POOL_W, POOL_W + NSA_W
Z_GATE = Z_KV + 6 * KV_W
Z_QX = Z_GATE + 3 * NSA_HEADS
Z_MERGE = Z_QX + X_HEADS * P

GAINS = [("g_mix", 8), ("g_mem", 8), ("g_ffn", 8), ("g_final", 8), ("ffn_norm_2", 32), ("mix_norm_2", 16),
         ("ple_norm_2", 16), ("final_norm_2", 8), ("mla_q_norm_2", 2), ("mla_kv_norm_2", 1), ("pool_scale", 4)]
GAIN_AT = {}
for _name, _n in GAINS:
    GAIN_AT[_name] = sum(n for _, n in GAINS[:len(GAIN_AT)])
N_GAINS = sum(n for _, n in GAINS)

RING = 4
PANEL = FC * P
GATHERS = 8
LAG = 3


class Job:

    def __init__(self, name, panels, kind, weight, rows, cols, width, act):
        self.name, self.panels, self.kind = name, panels, kind
        self.weight, self.rows, self.cols, self.width, self.act = weight, rows, cols, width, act
        self.first = 0
        self.split = None
        self.split_first = 0


class Step:

    def __init__(self, first, j, turn, per):
        self.j, self.turn, self.per, self.origin = j, turn, per, first
        self.slot = (first + j) % RING
        self.uses = (first + j) // RING + turn
        self.number = first + j + (turn * RING if per else 0)

    def at(self, f):
        if not self.per:
            return f(self.j)
        return f(self.j) + self.turn * (f(self.j + RING) - f(self.j))


def panels_of(eng, job, body, ahead=0):
    turns = (job.panels - ahead) // RING
    done = 0
    if turns >= 2 and job.first >= RING:
        with eng.Fori(0, turns) as i:
            for j in range(RING):
                body(Step(job.first, j, i, True))
        done = turns * RING
    for j in range(done, job.panels):
        body(Step(job.first, j, 0, False))


def over_partitions(row, n):
    return bass.AP(row.tensor, row.offset, [[0, n], [1, row.shape[-1]]])


def build(nc, a, out, onehot, inv_freq):
    ctx = ExitStack()
    with ctx:
        def sb(name, shape, dt=F32):
            return ctx.enter_context(nc.sbuf_tensor(name, shape, dt))

        sems = {}

        def sem(name):
            if name not in sems:
                sems[name] = ctx.enter_context(nc.semaphore(name))
            return sems[name]

        xT = sb("xT", [P, DC, T])
        nT = sb("nT", [P, DC, T])
        ring = sb("ring", [P, RING, PANEL])
        work = sb("work", [P, 3, LAG, 512])
        soft, prob, probT = work[:, 0], work[:, 1], work[:, 2]
        squares = work[:, :, :, :].rearrange("p n a b -> p (n a b)")
        ident = sb("ident", [P, P])
        ones = sb("ones", [P, P])
        causal = sb("causal", [P, 3 * P])
        chunked = sb("chunked", [P, 3 * P])
        zeros = sb("zeros", [P, 512])
        tri = sb("tri", [P, TT, T])
        gains = sb("gains", [P, N_GAINS])
        root = sb("root", [P, T])
        rstd = sb("rstd", [P, T])
        nmax = sb("nmax", [P, LAG, TT])
        sums = sb("sums", [P, LAG, TT])
        inv = sb("inv", [P, LAG, TT])
        coef = sb("coef", [P, LAG, TT])
        has = sb("has", [P, 1])
        eps = sb("eps", [P, 1])
        iota16 = sb("iota16", [P, 16])[:, :]
        arena_byte = nc.sbuf_base
        arena = sb("arena", [P, 30208])
        spot = [0]

        def parts_at(name, shape, at):
            return nc.alloc_sbuf_tensor_at(name, [P] + shape, F32R, offset=arena_byte + 4 * at)

        def part(n, at=None):
            if at is None:
                at = spot[0]
                spot[0] += n
                assert spot[0] <= 30208, spot[0]
            return arena[:, at:at + n]

        merge = part(24 * T).rearrange("p (c t) -> p c t", c=24)
        tokk = part(1024, 0).rearrange("p (g t) -> p g t", g=4)
        tokv = part(1024, 1024).rearrange("p (g t) -> p g t", g=4)
        blkk = part(2048, 2048).rearrange("p (l g c) -> p l g c", l=LP, g=4)
        blkv = part(2048, 4096).rearrange("p (l g c) -> p l g c", l=LP, g=4)
        bias_at = spot[0]
        bias = part(NSA_HEADS * 384).rearrange("p (h k) -> p h k", h=NSA_HEADS)
        x_in = part(2048, bias_at).rearrange("p (t d) -> p t d", t=TT)
        mem_in = part(2048, bias_at + 2048).rearrange("p (t d) -> p t d", t=TT)
        rows_in = part(P, bias_at + 4096)
        pe_in = part(P, bias_at + 4224)
        q_at = spot[0]
        qT = part(2048).rearrange("p (c t) -> p c t", c=8)
        kselT = part(512).rearrange("p (c t) -> p c t", c=2)
        kwinT = part(512).rearrange("p (c t) -> p c t", c=2)
        vsel = part(512).rearrange("p (t d) -> p t d", t=2)
        vwin = part(512).rearrange("p (t d) -> p t d", t=2)
        o_at = spot[0]
        o_nsa = part(2048).rearrange("p (t d) -> p t d", t=2)
        memT = part(2048, o_at).rearrange("p (c t) -> p c t", c=8)
        w_cmp = part(2 * 1024).rearrange("p (k l d) -> p k l d", k=2, l=LP)
        w_grp = part(512).rearrange("p (g d) -> p g d", g=4)
        qxT = part(1024).rearrange("p (c t) -> p c t", c=4)
        kxT = part(1024).rearrange("p (c t) -> p c t", c=4)
        vx = part(1024).rearrange("p (t d) -> p t d", t=2)
        uT = part(1024).rearrange("p (c t) -> p c t", c=4)
        mixT = part(1024).rearrange("p (c t) -> p c t", c=4)
        o_x = part(1024, spot[0]).rearrange("p (t d) -> p t d", t=2)
        pcmp = part(1024).rearrange("p (t r g c) -> p t r g c", t=2, r=4, g=4)
        pcmpT = part(1024).rearrange("p (t r q) -> p t r q", t=2, r=4)
        scmp = part(480).rearrange("p (n c) -> p n c", c=N_CMP)
        bcmp = part(512).rearrange("p (n c) -> p n c", c=16)
        kcT = part(2 * N_CMP).rearrange("p (s c) -> p s c", s=2)
        vc = part(HEAD)
        cstat = part(4 * 32).rearrange("p (k n) -> p k n", k=4)
        gate_nsa = part(TT * 48).rearrange("p (t n) -> p t n", t=TT)
        peT = part(32)
        table = part(384, q_at)
        rel = part(16, q_at + 384)
        hot = part(256, q_at + 400)
        icount = part(16)
        oxT = uT[:, :, :]
        spot[0] = 0
        gath = part(GATHERS * D).rearrange("p (k d) -> p k d", k=GATHERS)
        qpT = part(16 * T).rearrange("p (c t) -> p c t", c=16)
        sub_in = part(2048).rearrange("p (c k) -> p c k", c=16)
        eq = sub_in.rearrange("p c k -> p (c k)")
        hrow = part(2048).rearrange("p (t d) -> p t d", t=TT)
        subT = part(2048).rearrange("p (c k) -> p c k", c=16)
        cand = part(2048).rearrange("p (h a b) -> p h a b", h=8, a=16)
        cand2 = part(2048).rearrange("p (h n) -> p h n", h=8)
        yacc = part(2048).rearrange("p (t d) -> p t d", t=TT)
        stop_ = part(2 * P)
        ktop = part(256).rearrange("p (h s k) -> p h s k", h=8, s=2)
        kidx = part(256).rearrange("p (h s k) -> p h s k", h=8, s=2)
        kidf = part(256).rearrange("p (h s k) -> p h s k", h=8, s=2)
        best = part(P).rearrange("p (h k) -> p h k", h=8)
        bpos = part(P).rearrange("p (h k) -> p h k", h=8)
        bhalf = part(2 * P).rearrange("p (s n) -> p s n", s=2)
        bhalff = part(2 * P).rearrange("p (s n) -> p s n", s=2)
        which = part(2 * P).rearrange("p (s n) -> p s n", s=2)
        idf = part(P)
        ids = part(TT * P).rearrange("p (t n) -> p t n", t=TT)
        idcol = part(GATHERS)
        gate = part(TT * P).rearrange("p (t n) -> p t n", t=TT)
        dots = part(TT * P).rearrange("p (t n) -> p t n", t=TT)
        wgt = part(TT * P).rearrange("p (t n) -> p t n", t=TT)
        dcol = part(GATHERS)
        gsum = part(8)
        w_high = parts_at("w_high", [2, PANEL], 0)
        w_low = parts_at("w_low", [2, PANEL], 2 * PANEL)
        h_high = parts_at("h_high", [FC, T], 4 * PANEL)
        h_low = parts_at("h_low", [FC, T], 4 * PANEL + FC * T)
        spot[0] = 4 * PANEL + 2 * FC * T
        n_high = parts_at("n_high", [DC, T], spot[0])
        n_low = parts_at("n_low", [DC, T], spot[0] + DC * T)
        spot[0] += 2 * DC * T
        sgate = part(1024).rearrange("p (k n) -> p k n", k=2)
        p_in = part(4 * 256).rearrange("p (i t d) -> p i t d", i=2, t=2)
        pT = part(4 * 256).rearrange("p (i c t) -> p i c t", i=2, c=2)
        fbias = part(8)
        freq = part(1)
        posi = part(256)
        spot[0] = 0
        q2T = part(2048).rearrange("p (c t) -> p c t", c=8)
        qrT = part(2048).rearrange("p (c t) -> p c t", c=8)
        k2T = part(2048).rearrange("p (c t) -> p c t", c=8)
        v2 = part(2048).rearrange("p (t d) -> p t d", t=2)
        o2 = part(2048).rearrange("p (t d) -> p t d", t=2)
        cqT = part(512).rearrange("p (c t) -> p c t", c=2)
        ckvT = part(256).rearrange("p (c t) -> p c t", c=1)
        krT = part(256)
        rope_in = part(256)
        rope_sw = part(256)
        cosT = part(256)
        sinT = part(256)
        ncum = part(8 * 384).rearrange("p (h k) -> p h k", h=8)
        ftmp = part(6 * 16).rearrange("p (k n) -> p k n", k=6)
        logf = part(16).rearrange("p (t h) -> p t h", t=2)
        logf_wide = part(2048).rearrange("p (t n) -> p t n", t=2)
        cumq = part(16).rearrange("p (t h) -> p t h", t=2)
        posf = part(256)
        ang = part(3 * 256).rearrange("p (k t) -> p k t", k=3)
        assert spot[0] <= 4 * PANEL + 2 * FC * T
        xrow = part(2048, 0).rearrange("p (t d) -> p t d", t=TT)

        bank = [ctx.enter_context(nc.psum_tensor(f"bank{i}", [P, 512], F32)) for i in range(RING)]
        psS = [ctx.enter_context(nc.psum_tensor(f"psS{i}", [P, 512], F32)) for i in range(2)]
        psP = ctx.enter_context(nc.psum_tensor("psP", [P, 512], F32))
        psO = ctx.enter_context(nc.psum_tensor("psO", [P, 512], F32))
        toeplitz = nc.dram_tensor("toeplitz", (NSA_HEADS, P, 384), F32, kind="Internal")

        w_in = a["w_in"][0]
        L = range(2)

        def wv(ap):
            return ap.rearrange("(c p) n -> p c n", p=P)

        def job(name, panels, kind, weight, cols, width, act, chunks=DC):
            return Job(name, panels, kind, lambda j: wv(weight), lambda j: chunks, cols, width, lambda j: act)

        jobs = [job("kv", 6, None, w_in, lambda j: Z_KV + 256 * j, 256, nT)]
        jobs[0].kind = lambda j: "T" if j in (3, 5) else "F"
        jobs += [
            job("q", 4, "F", w_in, lambda j: Z_Q + 256 * j, 256, nT),
            job("gate_nsa", 1, "T", w_in, lambda j: Z_GATE, 48, nT),
            job("qx", 2, "F", w_in, lambda j: Z_QX + 256 * j, 256, nT),
            job("pool", 2, "F", w_in, lambda j: Z_POOL + 256 * j, 256, nT),
            job("kx", 2, "F", a["w_mem_kv"][0], lambda j: 256 * j, 256, memT),
            job("vx", 2, "T", a["w_mem_kv"][0], lambda j: 512 + 256 * j, 256, memT),
            job("merge", 12, "F", w_in, lambda j: Z_MERGE + 256 * j, 256, nT),
            job("pool_out", 4, "F", a["w_pool_out"][0], lambda j: 256 * j, 256, mixT, 4),
            job("x_out", 4, "F", a["w_x_out"][0], lambda j: 256 * j, 256, oxT, 4),
            job("nsa_out", 4, "F", a["w_nsa_out"][0], lambda j: 256 * j, 256, nT),
            job("w_o", 4, "F", a["w_o"][0], lambda j: 256 * j, 256, merge),
            job("peer_q", 8, "F", a["w_peer_q"][0], lambda j: 256 * j, 256, nT),
        ]

        def ffn_jobs(i, s):
            w = a["ffn_w_in_2"][i, s]
            j1 = job(f"ffn_in{i}{s}", FC, "F", w, lambda j: (j % 2) * D_FF + 256 * (j // 2), 256, None)
            j2 = job(f"ffn_out{i}{s}", DC, "F", a["ffn_w_out_2"][i, s], lambda j: 128 * j, 128, None, FC)
            j1.split, j2.split = (n_high, n_low), (h_high, h_low)
            return [j1, j2]

        def ple_job(i):
            g, w = a["ple_w_gate_2"][i], a["ple_w_proj_2"][i]
            return [Job(f"ple{i}", 8, "F", lambda j: wv(w if j % 2 else g), lambda j: 2 if j % 2 else DC,
                        lambda j: 256 * (j // 2), 256, lambda j: pT[:, i] if j % 2 else nT)]

        jobs += ffn_jobs(0, 0) + [
            job("cq", 1, "F", a["mla_w_down_2"][0], lambda j: 0, 256, nT),
            job("ckv", 1, "F", a["mla_w_down_2"][0], lambda j: 256, 192, nT),
            job("uq", 8, "F", a["mla_w_uq_2"][0], lambda j: 192 * j, 192, cqT, 2),
            job("ukv", 8, "FT", a["mla_w_ukv_2"][0], lambda j: 256 * j, 256, ckvT, 1),
            job("mla_o", 4, "F", a["mla_w_o_2"][0], lambda j: 256 * j, 256, nT),
        ] + ffn_jobs(0, 1) + ple_job(0) + ffn_jobs(1, 0) + [
            job("fq", 4, "F", a["fox_w_in_2"][0], lambda j: 256 * j, 256, nT),
            job("fk", 4, "F", a["fox_w_in_2"][0], lambda j: D + 256 * j, 256, nT),
            job("fv", 4, "T", a["fox_w_in_2"][0], lambda j: 2 * D + 256 * j, 256, nT),
            job("ff", 1, "T", a["fox_w_in_2"][0], lambda j: 3 * D, FOX_HEADS, nT),
            job("fox_o", 4, "F", a["fox_w_o_2"][0], lambda j: 256 * j, 256, nT),
        ] + ffn_jobs(1, 1) + ple_job(1)
        at = 0
        by_name = {}
        n_split = 0
        for j_ in jobs:
            j_.first, j_.split_first = at, n_split
            if j_.split:
                n_split += j_.panels
            at += j_.panels
            by_name[j_.name] = j_
        landed = [sem(f"landed{k}") for k in range(RING)]
        multiplied = sem("multiplied")
        emptied = [sem(f"emptied{k}") for k in range(RING)]
        high = sem("high")
        low = sem("low")

        def after(st, n):
            return Step(st.origin, st.j + n, st.turn, st.per)

        def split_no(job_, st):
            return st.number - job_.first + job_.split_first

        def halved(job_, st):
            return (job_.split_first + st.j) % 2, job_.rows(st.j) * job_.width

        def unit(lhs, rhs, scale, mask, width, v, outs, kind, extra=None):
            return dict(lhs=lhs, rhs=rhs, scale=scale, mask=mask, width=width, v=v, outs=outs, kind=kind, extra=extra)

        SEGS = {384: [(0, [(0, 0)]), (1, [(1, 0), (2, 1)])],
                512: [(0, [(0, 0), (1, 1)]), (1, [(2, 0), (3, 1)])]}

        def tok(ap, t):
            return ap[:, t * P:(t + 1) * P]

        nsa_units = []
        for b, (kT_, v_) in enumerate(((kselT, vsel), (kwinT, vwin))):
            for h in range(NSA_HEADS):
                g = h // HEADS_PER_GROUP
                lo = HEAD * (g % 2)
                nsa_units.append(unit(
                    [qT[lo:lo + HEAD, (g // 2) * 4 + h % 4, :]], [kT_[lo:lo + HEAD, g // 2, :]], 1.0, bias[:, h, :], 384,
                    [v_[:, k, g * HEAD:(g + 1) * HEAD] for k in range(TT)],
                    [o_nsa[:, t, h * HEAD:(h + 1) * HEAD] for t in range(TT)],
                    "gated", gate_nsa[:, :, (b + 1) * NSA_HEADS + h]))
        x_units = [unit([qxT[:, h, :]], [kxT[:, h, :]], float(P) ** -0.5, zeros[:, :], 512,
                        [vx[:, k, h * P:(h + 1) * P] for k in range(TT)],
                        [o_x[:, t, h * P:(h + 1) * P] for t in range(TT)], "plain") for h in range(X_HEADS)]
        mla_units = [unit([q2T[:, h, :], qrT[0:ROPE, h, :]], [k2T[:, h, :], krT[0:ROPE, :]], float(P + ROPE) ** -0.5,
                          chunked[:, :], 384, [v2[:, k, h * P:(h + 1) * P] for k in range(TT)],
                          [o2[:, t, h * P:(h + 1) * P] for t in range(TT)], "plain") for h in range(MLA_HEADS)]
        fox_units = [unit([q2T[:, h, :]], [k2T[:, h, :]], float(P) ** -0.5, ncum[:, h, :], 384,
                          [v2[:, k, h * P:(h + 1) * P] for k in range(TT)],
                          [o2[:, t, h * P:(h + 1) * P] for t in range(TT)], "fox", cumq[:, :, h]) for h in range(FOX_HEADS)]
        unit_base = {}
        n_ = 0
        for key, us in (("nsa", nsa_units), ("x", x_units), ("mla", mla_units), ("fox", fox_units)):
            unit_base[key] = (n_, us)
            n_ += len(us)
        biased = sem("biased")
        exped = sem("exped")
        probs_up = sem("probs_up")

        class Channel:

            def __init__(self, name, depth):
                self.full, self.free, self.depth = sem(name + "_full"), sem(name + "_free"), depth
                self.put = self.got = 0

            def claim(self, pe):
                if self.put >= self.depth:
                    pe.wait_ge(self.free, self.put - self.depth + 1)
                self.put += 1
                return (self.put - 1) % self.depth

            def take(self, eng):
                self.got += 1
                eng.wait_ge(self.full, self.got)
                return (self.got - 1) % self.depth

        chS, chP, chO = Channel("S", 2), Channel("P", 1), Channel("O", 1)

        norms = {}

        def norm(name, src, dst, gain, chunks):
            norms[name] = (len(norms), src, dst, GAIN_AT[gain[0]] + gain[1], chunks)

        norm("mix", xT, nT, ("g_mix", 0), DC)
        norm("mem", memT, memT, ("g_mem", 0), DC)
        norm("peer", xT, nT, ("g_ffn", 0), DC)
        norm("first", xT, xT, ("g_final", 0), DC)
        norm("ffn00", xT, nT, ("ffn_norm_2", 0), DC)
        norm("mix0", xT, nT, ("mix_norm_2", 0), DC)
        norm("cq", cqT, cqT, ("mla_q_norm_2", 0), 2)
        norm("ckv", ckvT, ckvT, ("mla_kv_norm_2", 0), 1)
        norm("ffn01", xT, nT, ("ffn_norm_2", 8), DC)
        norm("ple0", xT, nT, ("ple_norm_2", 0), DC)
        norm("ffn10", xT, nT, ("ffn_norm_2", 16), DC)
        norm("mix1", xT, nT, ("mix_norm_2", 8), DC)
        norm("ffn11", xT, nT, ("ffn_norm_2", 24), DC)
        norm("ple1", xT, nT, ("ple_norm_2", 8), DC)
        norm("final", xT, xT, ("final_norm_2", 0), DC)
        squared_v, squared_s = sem("squared_v"), sem("squared_s")
        rooted, normed = sem("rooted"), sem("normed")
        src_ready = sem("src_ready")

        block = ctx.enter_context(nc.Block())

        @block.sync
        def _(sp):
            for jb in jobs:
                def load(st):
                    if not (isinstance(st.number, int) and st.number < RING):
                        sp.wait_ge(emptied[st.slot], st.uses)
                    c = jb.rows(st.j)
                    src = jb.weight(st.j)
                    cols = st.at(jb.cols)
                    src = src[:, :, bass.ds(cols, jb.width)] if st.per else src[:, :, cols:cols + jb.width]
                    dst = ring[:, st.slot, 0:c * jb.width].rearrange("p (c n) -> p c n", c=c)
                    sp.dma_start(dst, src).then_inc(landed[st.slot], 16)
                panels_of(sp, jb, load)
            sp.wait_ge(sem("out_rows"), 4)
            sp.dma_start(out.rearrange("b (t p) d -> p (b t) d", p=P), xrow[:, :, :]).then_inc(sem("stored"), 16)
            sp.wait_ge(sem("stored"), 16)

        @block.gpsimd
        def _(pool):
            chain = [0]

            def link(ins):
                ins.then_inc(sem("pool_chain"), 1)
                chain[0] += 1
                pool.wait_ge(sem("pool_chain"), chain[0])

            def fill(ap, value, keep, base, pattern, mult):
                return pool.affine_select(out=ap, in_=ap, compare_op=keep, fill=value, base=base, pattern=pattern,
                                          channel_multiplier=mult)

            link(pool.memset(ident[:, :], 0.0))
            link(fill(ident[:, :], 1.0, ALU.not_equal, 0, [[-1, P]], 1))
            link(pool.memset(ones[:, :], 1.0))
            link(pool.memset(eps[:, :], EPS))
            link(pool.memset(has[:, :], 1.0))
            link(fill(has[:, :], 0.0, ALU.is_ge, -(CMP_LEN - 1), [[0, 1]], 1))
            link(pool.memset(zeros[:, :], 0.0))
            link(pool.memset(causal[:, :], 0.0))
            link(pool.memset(chunked[:, :], 0.0))
            for lo in (0, 2 * P):
                link(fill(causal[:, lo:lo + P], NEG, ALU.is_ge, 0, [[-1, P]], 1))
            for lo in (HEAD, 2 * P + HEAD):
                link(pool.memset(chunked[0:64, lo:lo + 64], NEG))
            link(pool.memset(tri[:, :, :], 1.0))
            link(fill(tri[:, :, :], 0.0, ALU.is_ge, 0, [[-P, TT], [1, T]], -1))
            link(pool.memset(pcmp, 0.0))
            link(pool.memset(blkv, 0.0))
            link(pool.memset(bcmp, NEG))
            link(pool.memset(table, NEG))
            link(pool.iota(icount, pattern=[[1, 16]], base=1, channel_multiplier=0, allow_small_or_imprecise_dtypes=True))
            link(pool.iota(iota16, pattern=[[1, 16]], base=0, channel_multiplier=0, allow_small_or_imprecise_dtypes=True))
            pool.sem_inc(sem("consts"), 1)

            for t in range(TT):
                for ph, rows in enumerate(("peer_u", "peer_v")):
                    pool.wait_ge(sem("ids_ready"), t + 1)
                    src = a[rows][0]
                    numbers = ids.bitcast(U32)
                    n = (t * 2 + ph) * SLOTS

                    with pool.Fori(0, SLOTS // GATHERS) as i:
                        for k in range(GATHERS):
                            pool.wait_ge(sem("rows_used"), i * GATHERS + (n + k + 1))
                            pool.sem_inc(sem("gather_turn"), 1)
                            pool.tensor_copy(idcol[:, k:k + 1].bitcast(U32),
                                             numbers[:, t, bass.ds(i * GATHERS + k, 1)]).then_inc(sem("idcol_ready"), 1)
                            pool.wait_ge(sem("idcol_ready"), i * GATHERS + (n + k + 1))
                            pool.sem_inc(sem("gather_turn"), 1)
                            pool.indirect_dma_start(
                                gath[:, k, :], None, src,
                                bass.IndirectOffsetOnAxis(ap=idcol[:, k:k + 1].bitcast(U32), axis=0)
                            ).then_inc(sem(f"rows_in{k}"), 16)

        @block.scalar
        def _(act):
            chain = [0]

            def link(ins):
                ins.then_inc(sem("act_chain"), 1)
                chain[0] += 1
                act.wait_ge(sem("act_chain"), chain[0])

            act.dma_start(x_in, a["x"][0].rearrange("(t p) d -> p t d", p=P)).then_inc(sem("x_in"), 16)
            for name, n in GAINS:
                src = a[name]
                if len(src.shape) > 1:
                    src = src.rearrange("a b c -> (a b c)" if len(src.shape) > 2 else "a b -> (a b)")
                act.dma_start(rows_in[GAIN_AT[name]:GAIN_AT[name] + n, :], src.rearrange("(r p) -> r p", p=P)).then_inc(sem("gains_in"), 16)
            for k, name in enumerate(("pe_k", "pe_v")):
                act.dma_start(pe_in[16 * k:16 * k + 16, :], a[name][0].rearrange("(l e) d -> l (e d)", e=2)).then_inc(sem("pe_in"), 16)
            act.dma_start(mem_in, a["mem"][0].rearrange("(t p) d -> p t d", p=P)).then_inc(sem("mem_in"), 16)
            act.dma_start(rel[0:BUCKETS, :], a["rel_bias"]).then_inc(sem("rel_in"), 16)
            act.dma_start(hot[0:BUCKETS, :], onehot).then_inc(sem("rel_in"), 16)
            for k, name in enumerate(("w_cmp_k", "w_cmp_v")):
                act.dma_start(w_cmp[:, k], a[name][0].rearrange("(l p) d -> p l d", p=P)).then_inc(sem("cmp_in"), 16)
            act.dma_start(w_grp, a["w_pool_grp"][0].rearrange("g c d -> c g d")).then_inc(sem("grp_in"), 16)

            def copy_out(dst, src):
                return act.activation(dst, src, ACT.Copy)

            def from_P(dst, cols=slice(0, 512), rows=slice(0, P), name="turned"):
                chP.take(act)
                copy_out(dst, psP[rows, cols]).then_inc(chP.free, 1)

            def quads(ap):
                return ap.rearrange("p (c t) -> p c t", c=4)

            def norm_root(name):
                n, src, dst, g, c = norms[name]
                act.wait_ge(src_ready, n + 1)
                act.activation(squares[:, 0:c * T].rearrange("p (c t) -> p c t", c=c)[:, :, P:T], src[:, 0:c, P:T],
                               ACT.Square).then_inc(squared_s, 1)
                chP.take(act)
                if n > 0:
                    act.wait_ge(normed, n)
                act.activation(root[:, :], psP[:, 0:T], ACT.Sqrt, scale=1.0 / (P * c), bias=eps[:, 0:1]).then_inc(rooted, 1)
                act.wait_ge(rooted, n + 1)
                act.sem_inc(chP.free, 1)

            def empties(name, body):
                jb = by_name[name]

                def one(st):
                    act.wait_ge(multiplied, st.number + 1)
                    if st.per:
                        act.sem_inc(sem("act_turn"), 1)
                    body(st, bank[st.slot]).then_inc(emptied[st.slot], 1)
                panels_of(act, jb, one)

            def high_part(jb, st, free=True):
                par, n = halved(jb, st)
                act.wait_ge(landed[st.slot], st.uses * 16 + 16)
                if free:
                    act.wait_ge(multiplied, st.number - 1)
                copy_out(w_high[:, par, 0:n], ring[:, st.slot, 0:n]).then_inc(high, 1)

            def attention(key):
                base, us = unit_base[key]
                n = len(us)
                for s in range(n + 2):
                    if s < n:
                        u, gu, w = us[s], base + s, us[s]["width"]
                        act.wait_ge(biased, gu + 1)
                        half = w - 2 * P
                        for t, (lo, hi) in enumerate(((0, half), (half, w))):
                            ins = act.activation(prob[:, gu % LAG, lo:hi], soft[:, gu % LAG, lo:hi], ACT.Exp,
                                                 bias=nmax[:, gu % LAG, t:t + 1], accum_out=sums[:, gu % LAG, t:t + 1])
                        ins.then_inc(exped, 1)
                    if s >= 2:
                        gu, w = base + s - 2, us[s - 2]["width"]
                        if gu >= LAG:
                            act.wait_ge(chO.full, gu - LAG + 1)
                        chP.take(act)
                        copy_out(probT[:, gu % LAG, 0:w], psP[:, 0:w]).then_inc(chP.free, 1)
                        act.wait_ge(chP.free, chP.got)
                        act.sem_inc(probs_up, 1)

            act.wait_ge(sem("consts"), 1)
            from_P(gains[:, :], slice(0, N_GAINS))
            from_P(peT, slice(0, 32))
            for dst in (xT, memT):
                for t in range(TT):
                    for h in range(2):
                        chP.take(act)
                        copy_out(dst[:, 4 * h:4 * h + 4, t * P:(t + 1) * P], quads(psP[:, :])).then_inc(chP.free, 1)
            act.wait_ge(chP.free, 10)
            act.sem_inc(sem("inputs_T"), 1)
            chP.take(act)
            copy_out(table[0:NSA_HEADS, 0:T], psP[0:NSA_HEADS, 0:T]).then_inc(chP.free, 1)
            act.wait_ge(chP.free, chP.got)
            row = table[0:NSA_HEADS, :]
            act.dma_start(toeplitz[:, :, :], bass.AP(row.tensor, row.offset, [list(row.ap[0]), [0, P], [1, 384]]))\
                .then_inc(sem("table_out"), 16)
            act.wait_ge(sem("table_out"), 16)
            line = toeplitz[:, :, :]
            wide = bass.AP(line.tensor, P - 1, [[383, P], [P * 384, NSA_HEADS], [1, T]])
            diag = bass.AP(line.tensor, 2 * P - 1, [[383, P], [P * 384, NSA_HEADS], [1, P]])
            act.dma_start(bias[:, :, P:3 * P], wide).then_inc(sem("bias_in"), 16)
            act.dma_start(bias[:, :, 0:P], diag).then_inc(sem("bias_in"), 16)

            norm_root("mix")
            norm_root("mem")

            def kv_out(st, bk):
                j = st.j
                if j < 2:
                    dst = (tokk, tokv)[j]
                    for par in range(2):
                        src = bk[64 * par:64 * par + 64, :].rearrange("p (c t) -> p c t", c=2)
                        copy_out(dst[0:64, par::2, :], src)
                        ins = copy_out(dst[64:128, par::2, 0:T - 1], src[:, :, 1:T])
                    return ins
                dst = (kselT, vsel, kwinT, vwin)[j - 2]
                return copy_out(dst, bk[:, :].rearrange("p (c t) -> p c t", c=2))

            empties("kv", kv_out)

            def q_out(st, bk):
                g = st.j
                for par in range(2):
                    ins = act.activation(
                        qT[64 * (g % 2):64 * (g % 2) + 64, (g // 2) * 4 + par:(g // 2) * 4 + 4:2, :],
                        bk[64 * par:64 * par + 64, :].rearrange("p (c t) -> p c t", c=2), ACT.Copy, scale=HEAD ** -0.5)
                return ins

            empties("q", q_out)
            empties("gate_nsa", lambda st, bk: act.activation(
                gate_nsa, bk[:, :].rearrange("p (t n) -> p t n", t=TT)[:, :, 0:48], ACT.Sigmoid))

            def pairs(dst):
                return lambda st, bk: copy_out(dst[:, 2 * st.j:2 * st.j + 2, :], bk[:, :].rearrange("p (c t) -> p c t", c=2))

            def tokens(dst):
                return lambda st, bk: copy_out(dst[:, :, 256 * st.j:256 * st.j + 256], bk[:, :].rearrange("p (t n) -> p t n", t=2))

            empties("qx", pairs(qxT))
            empties("pool", pairs(uT))
            empties("kx", pairs(kxT))
            empties("vx", tokens(vx))
            chP.take(act)
            for par in range(2):
                ins = copy_out(kcT[64 * par:64 * par + 64, :, :],
                               psP[0:64, 0:4 * N_CMP].rearrange("p (g c) -> p g c", g=4)[:, par::2, :])
            ins.then_inc(chP.free, 1)
            chP.take(act)
            copy_out(vc, psP[:, 0:HEAD]).then_inc(chP.free, 1)
            act.wait_ge(chP.free, chP.got)
            act.sem_inc(sem("kc_ready"), 1)
            act.wait_ge(sem("cmp_scores"), 1)
            act.activation(scmp, scmp, ACT.Exp).then_inc(sem("cmp_exp"), 1)
            for t in range(TT):
                chP.take(act)
                copy_out(pcmpT[:, t], quads(psP[:, :])).then_inc(chP.free, 1)
            act.wait_ge(chP.free, chP.got)
            act.sem_inc(sem("pcmp_T"), 1)
            attention("nsa")
            attention("x")

            def turn_back(dst, quarters):
                for t in range(TT):
                    for h in range(quarters):
                        chP.take(act)
                        copy_out(dst[:, 4 * h:4 * h + 4, t * P:(t + 1) * P], quads(psP[:, :])).then_inc(chP.free, 1)
                act.wait_ge(chP.free, chP.got)
                act.sem_inc(sem("turned"), 1)

            turn_back(oxT, 1)
            empties("merge", lambda st, bk: act.activation(
                merge[:, bass.ds(st.at(lambda j: 2 * j), 2), :], bk[:, :].rearrange("p (c t) -> p c t", c=2), ACT.Sigmoid))
            turn_back(nT, 2)
            act.wait_ge(src_ready, norms["peer"][0] + 1)
            act.dma_start(sub_in, a["peer_sub_keys"][0].rearrange("h s k c -> k (h s) c")).then_inc(sem("sub_in"), 16)
            norm_root("peer")
            for q in range(4):
                chP.take(act)
                copy_out(subT[:, 4 * q:4 * q + 4, :], quads(psP[:, :])).then_inc(chP.free, 1)
            for t in range(TT):
                for h in range(2):
                    chP.take(act)
                    copy_out(hrow[:, t, 512 * h:512 * h + 512], psP[:, :]).then_inc(chP.free, 1)
            act.wait_ge(chP.free, chP.got)
            act.sem_inc(sem("sub_T"), 1)
            empties("peer_q", lambda st, bk: copy_out(
                qpT[:, bass.ds(st.at(lambda j: 2 * j), 2), :], bk[:, :].rearrange("p (c t) -> p c t", c=2)))
            for t in range(TT):
                act.wait_ge(sem("best_ready"), t + 1)
                act.activation(gate[:, t], gate[:, t], ACT.Exp).then_inc(sem("gate_exp"), 1)
            for t in range(TT):
                act.wait_ge(sem("dots_ready"), t + 1)
                act.activation(wgt[:, t], dots[:, t], ACT.Gelu).then_inc(sem("gelu_done"), 1)
            norm_root("first")
            act.wait_ge(normed, norms["first"][0] + 1)
            for i in L:
                act.dma_start(p_in[:, i], a["p_2"][i, 0].rearrange("(t p) d -> p t d", p=P)).then_inc(sem("p_in"), 16)
            act.dma_start(posi[0:ROPE, :].bitcast(I32), over_partitions(a["positions_2"], ROPE)).then_inc(sem("pos_in"), 16)
            act.dma_start(freq[0:ROPE, :], inv_freq).then_inc(sem("pos_in"), 16)
            act.dma_start(fbias, over_partitions(a["fox_b_f_2"], P)).then_inc(sem("pos_in"), 16)

            ffn_pairs = [0]

            def first_high(i, s_):
                jb = by_name[f"ffn_in{i}{s_}"]
                for j in range(2):
                    high_part(jb, Step(jb.first, j, 0, False), free=False)

            def norm_high():
                for q in range(2):
                    norms_split[0] += 1
                    act.wait_ge(sem("norm_half"), norms_split[0])
                    copy_out(n_high[:, 4 * q:4 * q + 4, :], nT[:, 4 * q:4 * q + 4, :]).then_inc(sem("n_high"), 1)

            norms_split = [0]

            def ffn_gates(i, s_):
                jb, jo = by_name[f"ffn_in{i}{s_}"], by_name[f"ffn_out{i}{s_}"]
                k0 = ffn_pairs[0]
                ffn_pairs[0] += FC // 2
                h0 = (2 * i + s_) * (FC // 2)

                def ahead(st):
                    if not st.per and st.j + 2 >= jb.panels:
                        high_part(jo, Step(jo.first, st.j + 2 - jb.panels, 0, False))
                    else:
                        high_part(jb, after(st, 2))

                def one(st):
                    pair = k0 + (st.j // 2) + (st.turn * 2 if st.per else 0)
                    if st.j % 2 == 0:
                        act.wait_ge(sem("sgate_free"), pair + 1)
                        if st.per:
                            act.sem_inc(sem("act_turn"), 1)
                        act.wait_ge(multiplied, st.number + 1)
                        act.activation(sgate[:, (st.j // 2 + k0) % 2, :], bank[st.slot][:, :], ACT.Silu)\
                            .then_inc(emptied[st.slot], 1)
                        ahead(st)
                    else:
                        ahead(st)
                        act.wait_ge(sem("hidden_pair"), h0 + st.j // 2 + 1 + (st.turn * 2 if st.per else 0))
                        if st.per:
                            act.sem_inc(sem("act_turn"), 1)
                        at_ = st.at(lambda j: 2 * (j // 2))
                        dst = h_high[:, bass.ds(at_, 2), :] if st.per else h_high[:, at_:at_ + 2, :]
                        copy_out(dst, sgate[:, (st.j // 2 + k0) % 2, :].rearrange("p (c t) -> p c t", c=2))\
                            .then_inc(sem("h_high"), 1)
                panels_of(act, jb, one, ahead=2)
                for j in range(DC - 2):
                    high_part(jo, Step(jo.first, j + 2, 0, False))

            first_high(0, 0)
            norm_root("ffn00")
            norm_high()
            ffn_gates(0, 0)
            norm_root("mix0")
            act.wait_ge(sem("angles"), 1)
            act.activation(cosT[0:ROPE, :], ang[0:ROPE, 0, :], ACT.Sin, scale=0.5).then_inc(sem("sines"), 1)
            act.activation(sinT[0:ROPE, :], ang[0:ROPE, 0, :], ACT.Sin).then_inc(sem("sines"), 1)
            norm_root("cq")
            norm_root("ckv")

            def swap(src):
                copy_out(rope_sw[0:32, :], src[32:64, :])
                return copy_out(rope_sw[32:64, :], src[0:32, :])

            act.wait_ge(sem("rope_go"), 1)
            swap(krT).then_inc(sem("swapped"), 1)

            def uq_out(st, bk):
                h = st.j
                act.wait_ge(sem("rope_go"), h + 2)
                copy_out(q2T[:, h, :], bk[:, 0:T])
                copy_out(rope_in[0:ROPE, :], bk[0:ROPE, T:2 * T])
                return swap(bk[:, T:2 * T])

            for h in range(MLA_HEADS):
                st = Step(by_name["uq"].first, h, 0, False)
                act.wait_ge(multiplied, st.number + 1)
                uq_out(st, bank[st.slot]).then_inc(emptied[st.slot], 1)
            for h in range(MLA_HEADS):
                st = Step(by_name["ukv"].first, h, 0, False)
                act.wait_ge(multiplied, st.number + 1)
                copy_out(k2T[:, h, :], bank[st.slot][:, 0:T])
                copy_out(v2[:, :, h * P:(h + 1) * P], bank[st.slot][:, T:2 * T].rearrange("p (t n) -> p t n", t=2))\
                    .then_inc(emptied[st.slot], 1)
            attention("mla")
            turn_back(nT, 2)
            first_high(0, 1)
            norm_root("ffn01")
            norm_high()
            ffn_gates(0, 1)
            for i in L:
                chP.take(act)
                copy_out(pT[:, i].rearrange("p c t -> p (c t)"), psP[:, :]).then_inc(chP.free, 1)
            act.wait_ge(chP.free, chP.got)
            act.sem_inc(sem("p_T"), 1)

            ple_pairs = [0]

            def ple_gates(name):
                jb = by_name[name]
                k0 = ffn_pairs[0]
                ffn_pairs[0] += 4

                def one(st):
                    if st.j % 2:
                        return
                    pair = k0 + (st.j // 2) + (st.turn * 2 if st.per else 0)
                    act.wait_ge(sem("sgate_free"), pair + 1)
                    if st.per:
                        act.sem_inc(sem("act_turn"), 1)
                    act.wait_ge(multiplied, st.number + 1)
                    act.activation(sgate[:, (st.j // 2 + k0) % 2, :], bank[st.slot][:, :], ACT.Sigmoid)\
                        .then_inc(emptied[st.slot], 1)
                panels_of(act, jb, one)

            norm_root("ple0")
            ple_gates("ple0")
            first_high(1, 0)
            norm_root("ffn10")
            norm_high()
            ffn_gates(1, 0)
            norm_root("mix1")
            empties("fq", pairs(q2T))
            empties("fk", pairs(k2T))
            empties("fv", tokens(v2))
            act.wait_ge(sem("forget"), 1)
            act.activation(ftmp[:, 1], ftmp[:, 1], ACT.Exp, scale=-1.0).then_inc(sem("fexp"), 1)
            act.wait_ge(sem("forget"), 2)
            act.activation(ftmp[:, 2], ftmp[:, 2], ACT.Ln).then_inc(sem("fexp"), 1)
            attention("fox")
            turn_back(nT, 2)
            first_high(1, 1)
            norm_root("ffn11")
            norm_high()
            ffn_gates(1, 1)
            norm_root("ple1")
            ple_gates("ple1")
            norm_root("final")
            for t in range(TT):
                for h in range(2):
                    chP.take(act)
                    copy_out(xrow[:, t, 512 * h:512 * h + 512], psP[:, :]).then_inc(sem("out_rows"), 1)
                    act.wait_ge(sem("out_rows"), 2 * t + h + 1)
                    act.sem_inc(chP.free, 1)

        @block.tensor
        def _(pe):
            def products(name, ready=None):
                jb = by_name[name]
                if ready is not None:
                    pe.wait_ge(*ready)

                def one(st):
                    if jb.split:
                        pe.wait_ge(low, split_no(jb, st) + 1)
                    else:
                        pe.wait_ge(landed[st.slot], st.uses * 16 + 16)
                    if not (isinstance(st.uses, int) and st.uses == 0):
                        pe.wait_ge(emptied[st.slot], st.uses)
                    c, w, act_ = jb.rows(st.j), jb.width, jb.act(st.j)
                    if jb.split:
                        par, n = halved(jb, st)
                        wh, wl = (x[:, par, 0:n].rearrange("p (c n) -> p c n", c=c) for x in (w_high, w_low))
                        ah, al = jb.split
                        for m in range(0, w, P):
                            dst = bank[st.slot][:, (m // P) * T:(m // P) * T + T]
                            for k in range(c):
                                for n_, (x, y) in enumerate(((wh, al), (wl, ah), (wh, ah))):
                                    mm = pe.matmul(dst, x[:, k, m:m + P], y[:, k, :], start=(k == 0 and n_ == 0),
                                                   stop=(k == c - 1 and n_ == 2))
                        mm.then_inc(multiplied, 1)
                        return
                    wt = ring[:, st.slot, 0:c * w].rearrange("p (c n) -> p c n", c=c)
                    kind = jb.kind(st.j) if callable(jb.kind) else jb.kind
                    bk = bank[st.slot]
                    groups = []
                    if kind == "F":
                        for m in range(0, w, P):
                            mw = min(P, w - m)
                            o = (m // P) * T
                            groups.append((bk[0:mw, o:o + T], lambda k, m=m, mw=mw: (wt[:, k, m:m + mw], act_[:, k, :])))
                    else:
                        lo = 0
                        if kind == "FT":
                            groups.append((bk[:, 0:T], lambda k: (wt[:, k, 0:P], act_[:, k, :])))
                            lo = P
                        for t in range(TT):
                            o = T + t * P if kind == "FT" else t * T
                            groups.append((bk[:, o:o + w - lo],
                                           lambda k, t=t, lo=lo: (act_[:, k, t * P:(t + 1) * P], wt[:, k, lo:w])))
                    for dst, ops in groups:
                        for k in range(c):
                            lhs, rhs = ops(k)
                            mm = pe.matmul(dst, lhs, rhs, start=(k == 0), stop=(k == c - 1))
                    mm.then_inc(multiplied, 1)
                panels_of(pe, jb, one)

            def all_left(name):
                last = by_name[name].first + by_name[name].panels
                for k in range(RING):
                    pe.wait_ge(emptied[k], (last - 1 - k) // RING + 1)

            def turn(pieces):
                chP.claim(pe)
                for o, src in pieces:
                    n, m = src.shape[0], src.shape[1]
                    mm = pe.transpose(psP[0:m, o:o + n], src, ident[0:n, 0:n])
                mm.then_inc(chP.full, 1)

            def norm_sum(name):
                n, src, dst, g, c = norms[name]
                pe.wait_ge(squared_v, n + 1)
                pe.wait_ge(squared_s, n + 1)
                chP.claim(pe)
                for k in range(c):
                    mm = pe.matmul(psP[:, 0:T], ones[:, :], squares[:, k * T:(k + 1) * T], start=(k == 0), stop=(k == c - 1))
                mm.then_inc(chP.full, 1)

            def attention(key):
                base, us = unit_base[key]
                n = len(us)
                for s in range(n + LAG):
                    if s < n:
                        u = us[s]
                        ps = psS[chS.claim(pe)]
                        half = u["width"] - T
                        for t, (lo, hi) in enumerate(((0, half), (half, u["width"]))):
                            for k, (ql, kr) in enumerate(zip(u["lhs"], u["rhs"])):
                                mm = pe.matmul(ps[:, lo:hi], ql[:, t * P:(t + 1) * P], kr[:, 0:hi - lo],
                                               start=(k == 0), stop=(k == len(u["lhs"]) - 1))
                        mm.then_inc(chS.full, 1)
                    if 2 <= s < n + 2:
                        gu, w = base + s - 2, us[s - 2]["width"]
                        pe.wait_ge(exped, gu + 1)
                        turn([(o, prob[:, gu % LAG, o:o + P]) for o in range(0, w, P)])
                    if s >= LAG:
                        gu, u = base + s - LAG, us[s - LAG]
                        pe.wait_ge(probs_up, gu + 1)
                        lo = chO.claim(pe) * T
                        dv = u["v"][0].shape[1]
                        for t, pieces in SEGS[u["width"]]:
                            for k, (c, kt) in enumerate(pieces):
                                mm = pe.matmul(psO[:, lo + t * dv:lo + (t + 1) * dv], probT[:, gu % LAG, c * P:(c + 1) * P],
                                               u["v"][kt], start=(k == 0), stop=(k == len(pieces) - 1))
                        mm.then_inc(chO.full, 1)

            def rows_to_T(src, blocks):
                for t in range(TT):
                    for q in range(blocks // 4):
                        turn([(j * P, src[:, t, (4 * q + j) * P:(4 * q + j + 1) * P]) for j in range(4)])

            pe.wait_ge(sem("consts"), 1)
            pe.wait_ge(sem("gains_in"), 16 * len(GAINS))
            turn([(0, rows_in[0:N_GAINS, :])])
            pe.wait_ge(sem("pe_in"), 32)
            turn([(0, pe_in[0:32, :])])
            pe.wait_ge(sem("x_in"), 16)
            rows_to_T(x_in, 8)
            pe.wait_ge(sem("mem_in"), 16)
            rows_to_T(mem_in, 8)
            pe.wait_ge(sem("rel_in"), 32)
            chP.claim(pe)
            pe.matmul(psP[0:NSA_HEADS, 0:T], rel[0:BUCKETS, :], hot[0:BUCKETS, :], start=True, stop=True).then_inc(chP.full, 1)
            norm_sum("mix")
            norm_sum("mem")
            products("kv", (normed, norms["mix"][0] + 1))
            products("q")
            products("gate_nsa")
            products("qx")
            products("pool")
            products("kx", (normed, norms["mem"][0] + 1))
            products("vx")
            pe.wait_ge(sem("blocks"), 2)
            pe.wait_ge(sem("cmp_in"), 32)
            chP.claim(pe)
            for l in range(LP):
                mm = pe.matmul(psP[0:HEAD, 0:4 * N_CMP], w_cmp[:, 0, l, :], blkk[:, l, :, 0:N_CMP], start=(l == 0), stop=(l == LP - 1))
            mm.then_inc(chP.full, 1)
            chP.claim(pe)
            for l in range(LP):
                mm = pe.matmul(psP[:, 0:HEAD], blkv[:, l].rearrange("p g c -> p (g c)"), w_cmp[:, 1, l, :],
                               start=(l == 0), stop=(l == LP - 1))
            mm.then_inc(chP.full, 1)
            pe.wait_ge(sem("kc_ready"), 1)
            all_left("vx")
            for par in range(2):
                ps = psS[chS.claim(pe)]
                lo = HEAD * par
                for t in range(TT):
                    for g in (par, par + 2):
                        for r in range(HEADS_PER_GROUP):
                            o = (t * NSA_HEADS + g * HEADS_PER_GROUP + r) * 16
                            mm = pe.matmul(ps[:, o:o + N_CMP], qT[lo:lo + HEAD, (g // 2) * 4 + r, t * P:(t + 1) * P],
                                           kcT[lo:lo + HEAD, g // 2, :], start=True, stop=True)
                mm.then_inc(chS.full, 1)
            pe.wait_ge(sem("cmp_probs"), 1)
            for t in range(TT):
                turn([(r * P, pcmp[:, t, r].rearrange("p g c -> p (g c)")) for r in range(4)])
            pe.wait_ge(sem("pcmp_T"), 1)
            for g in range(NSA_GROUPS):
                ps = psS[chS.claim(pe)]
                lo = CMP_SLOT * g
                for t in range(TT):
                    for r in range(HEADS_PER_GROUP):
                        o = t * T + r * HEAD
                        mm = pe.matmul(ps[:, o:o + HEAD], pcmpT[lo:lo + N_CMP, t, r, :], vc[lo:lo + N_CMP, :],
                                       start=True, stop=True)
                mm.then_inc(chS.full, 1)
            pe.wait_ge(sem("pooled"), 1)
            pe.wait_ge(sem("grp_in"), 16)
            for half in range(2):
                ps = psS[chS.claim(pe)]
                for g in (2 * half, 2 * half + 1):
                    mm = pe.matmul(ps[:, (g % 2) * T:(g % 2 + 1) * T], w_grp[:, g, :], uT[:, g, :], start=True, stop=True)
                mm.then_inc(chS.full, 1)
            pe.wait_ge(sem("bias_in"), 32)
            attention("nsa")
            attention("x")
            pe.wait_ge(sem("attended"), 1)
            rows_to_T(o_x, 4)
            products("merge")
            rows_to_T(o_nsa, 8)
            products("pool_out", (sem("mixed"), 1))
            products("x_out", (sem("turned"), 1))
            products("nsa_out", (sem("turned"), 2))
            products("w_o", (sem("merged"), 1))
            norm_sum("peer")
            pe.wait_ge(sem("sub_in"), 16)
            for q in range(4):
                turn([(j * P, sub_in[:, 4 * q + j, :]) for j in range(4)])
            pe.wait_ge(normed, norms["peer"][0] + 1)
            for t in range(TT):
                for q in range(2):
                    turn([(j * P, nT[:, 4 * q + j, t * P:(t + 1) * P]) for j in range(4)])
            products("peer_q")
            pe.wait_ge(sem("sub_T"), 1)
            all_left("peer_q")
            for t in range(TT):
                for h2 in range(PEER_HEADS // 2):
                    ps = psS[chS.claim(pe)]
                    for j in range(4):
                        c = 4 * h2 + j
                        mm = pe.matmul(ps[:, j * P:(j + 1) * P], qpT[:, c, t * P:(t + 1) * P], subT[:, c, :], start=True, stop=True)
                    mm.then_inc(chS.full, 1)
            for t in range(TT):
                pe.wait_ge(sem("experts_done"), t + 1)
                for q in range(2):
                    ps = psS[chS.claim(pe)]
                    for j in range(4):
                        mm = pe.transpose(ps[:, j * P:(j + 1) * P], yacc[:, t, (4 * q + j) * P:(4 * q + j + 1) * P], ident[:, :])
                    mm.then_inc(chS.full, 1)
            norm_sum("first")

            def ffn(i, s):
                n = f"ffn{i}{s}"
                norm_sum(n)
                products(f"ffn_in{i}{s}", (sem("n_low"), 2 * (2 * i + s) + 2))
                products(f"ffn_out{i}{s}", (sem("h_low"), (2 * i + s + 1) * (FC // 2)))

            ffn(0, 0)
            norm_sum("mix0")
            products("cq", (normed, norms["mix0"][0] + 1))
            products("ckv")
            norm_sum("cq")
            norm_sum("ckv")
            products("uq", (normed, norms["cq"][0] + 1))
            products("ukv", (normed, norms["ckv"][0] + 1))

            all_left("ukv")
            pe.wait_ge(sem("rope_go"), 2 + MLA_HEADS)
            attention("mla")
            pe.wait_ge(sem("attended"), 2)
            rows_to_T(o2, 8)
            products("mla_o", (sem("turned"), 3))
            ffn(0, 1)
            pe.wait_ge(sem("p_in"), 32)
            for i in L:
                turn([(c * T + t * P, p_in[:, i, t, c * P:(c + 1) * P]) for c in range(2) for t in range(TT)])
            norm_sum("ple0")
            pe.wait_ge(sem("p_T"), 1)
            products("ple0", (normed, norms["ple0"][0] + 1))
            ffn(1, 0)
            norm_sum("mix1")
            products("fq", (normed, norms["mix1"][0] + 1))
            products("fk")
            products("fv")
            products("ff")
            pe.wait_ge(sem("forget"), 3)
            ps = psS[chS.claim(pe)]
            for t in range(TT):
                for j in range(t + 1):
                    mm = pe.matmul(ps[:, t * FOX_HEADS:(t + 1) * FOX_HEADS], tri[:, j, t * P:(t + 1) * P], logf[:, j, :],
                                   start=(j == 0), stop=(j == t))
            mm.then_inc(chS.full, 1)
            pe.wait_ge(sem("forget"), 4)
            for h2 in range(FOX_HEADS // 2):
                ps = psS[chS.claim(pe)]
                for j in range(2):
                    h = 2 * h2 + j
                    for t in range(TT):
                        mm = pe.matmul(ps[:, j * T:(j + 1) * T], logf_wide[:, t, h * P:(h + 1) * P], tri[:, t, :],
                                       start=(t == 0), stop=(t == TT - 1))
                mm.then_inc(chS.full, 1)
            all_left("ff")
            attention("fox")
            pe.wait_ge(sem("attended"), 3)
            rows_to_T(o2, 8)
            products("fox_o", (sem("turned"), 4))
            ffn(1, 1)
            norm_sum("ple1")
            products("ple1", (normed, norms["ple1"][0] + 1))
            norm_sum("final")
            pe.wait_ge(normed, norms["final"][0] + 1)
            for t in range(TT):
                for q in range(2):
                    turn([(j * P, xT[:, 4 * q + j, t * P:(t + 1) * P]) for j in range(4)])

        @block.vector
        def _(dve):
            chain = [0]

            def link(ins):
                ins.then_inc(sem("dve_chain"), 1)
                chain[0] += 1
                dve.wait_ge(sem("dve_chain"), chain[0])

            def tt(o, x, y, op):
                return dve.tensor_tensor(o, x, y, op)

            def ts(o, x, s1, op0, s2=None, op1=None):
                return dve.tensor_scalar(o, x, s1, s2, op0, op1) if op1 is not None else dve.tensor_scalar(o, x, s1, None, op0)

            def stt(o, x, s, y, op0, op1):
                return dve.scalar_tensor_tensor(out=o, in0=x, scalar=s, in1=y, op0=op0, op1=op1)

            def ready(name):
                dve.sem_inc(src_ready, 1)

            def do_norm(name):
                n, src, dst, g, c = norms[name]
                sq = squares[:, 0:c * T].rearrange("p (c t) -> p c t", c=c)
                dve.sem_inc(src_ready, 1)
                tt(sq[:, :, 0:P], src[:, 0:c, 0:P], src[:, 0:c, 0:P], ALU.mult).then_inc(squared_v, 1)
                dve.wait_ge(rooted, n + 1)
                link(dve.reciprocal(rstd[:, :], root[:, :]))
                for k in range(c):
                    ins = stt(dst[:, k, :], src[:, k, :], gains[:, g + k:g + k + 1], rstd[:, :], ALU.mult, ALU.mult)
                    if name.startswith("ffn") and k == 3:
                        ins.then_inc(sem("norm_half"), 1)
                ins.then_inc(normed, 1)
                dve.wait_ge(normed, n + 1)
                if name.startswith("ffn"):
                    dve.sem_inc(sem("norm_half"), 1)
                    for q in range(2):
                        halves_low[0] += 1
                        dve.wait_ge(sem("n_high"), halves_low[0])
                        h_ = slice(4 * q, 4 * q + 4)
                        tt(n_low[:, h_, :], nT[:, h_, :], n_high[:, h_, :].bitcast(F32), ALU.subtract).then_inc(sem("n_low"), 1)

            halves_low = [0]

            def low_part(jb, st):
                par, n = halved(jb, st)
                dve.wait_ge(high, split_no(jb, st) + 1)
                tt(w_low[:, par, 0:n], ring[:, st.slot, 0:n], w_high[:, par, 0:n].bitcast(F32), ALU.subtract).then_inc(low, 1)

            def first_low(i, s_):
                jb = by_name[f"ffn_in{i}{s_}"]
                for j in range(2):
                    low_part(jb, Step(jb.first, j, 0, False))

            def empties(name, body, before_last=None):
                jb = by_name[name]

                def one(st):
                    if before_last is not None and st.j == jb.panels - 1:
                        before_last()
                    dve.wait_ge(multiplied, st.number + 1)
                    body(st, bank[st.slot]).then_inc(emptied[st.slot], 1)
                panels_of(dve, jb, one)

            def settle(name):
                last = by_name[name].first + by_name[name].panels
                for k in range(RING):
                    dve.wait_ge(emptied[k], (last - 1 - k) // RING + 1)

            def halves(ap):
                return ap.rearrange("p (c t) -> p c t", c=2)

            def attention(key):
                base, us = unit_base[key]
                n = len(us)
                for s in range(n + LAG):
                    if s >= LAG:
                        gu, u = base + s - LAG, us[s - LAG]
                        sl = gu % LAG
                        dve.wait_ge(exped, gu + 1)
                        link(dve.reciprocal(inv[:, sl, :], sums[:, sl, :]))
                        scal = inv
                        if u["kind"] == "gated":
                            link(tt(coef[:, sl, :], inv[:, sl, :], u["extra"], ALU.mult))
                            scal = coef
                        lo = chO.take(dve) * T
                        dv = u["v"][0].shape[1]
                        for t in range(TT):
                            src = psO[:, lo + t * dv:lo + (t + 1) * dv]
                            if u["kind"] == "gated":
                                ins = stt(u["outs"][t], src, scal[:, sl, t:t + 1], u["outs"][t], ALU.mult, ALU.add)
                            else:
                                ins = ts(u["outs"][t], src, scal[:, sl, t:t + 1], ALU.mult)
                        ins.then_inc(chO.free, 1)
                    if s < n:
                        u, gu, w = us[s], base + s, us[s]["width"]
                        sl = gu % LAG
                        ps = psS[chS.take(dve)]
                        stt(soft[:, sl, 0:w], ps[:, 0:w], u["scale"], u["mask"][:, 0:w], ALU.mult, ALU.add).then_inc(chS.free, 1)
                        dve.wait_ge(chS.free, chS.got)
                        half = w - T
                        segs = ((0, half), (half, w))
                        if u["kind"] == "fox":
                            for t, (lo, hi) in enumerate(segs):
                                link(stt(soft[:, sl, lo:hi], soft[:, sl, lo:hi], u["extra"][:, t:t + 1], causal[:, lo:hi],
                                         ALU.add, ALU.add))
                        for t, (lo, hi) in enumerate(segs):
                            ins = dve.tensor_reduce(nmax[:, sl, t:t + 1], soft[:, sl, lo:hi], AX_X, ALU.max, negate=True)
                        ins.then_inc(biased, 1)
                dve.wait_ge(chO.free, chO.got)

            link(dve.memset(rstd[:, 0:1], 0.0))
            dve.sem_inc(sem("sgate_free"), 2)
            dve.sem_inc(sem("rows_used"), GATHERS)
            dve.wait_ge(sem("inputs_T"), 1)
            do_norm("mix")
            do_norm("mem")

            dve.wait_ge(multiplied, 1)
            for k, (tok_, blk) in enumerate(((tokk, blkk), (tokv, blkv))):
                dve.wait_ge(emptied[k], 1)
                if k == 0:
                    dve.wait_ge(sem("consts"), 1)
                for g in range(NSA_GROUPS):
                    src = tok_[:, g, :]
                    win = bass.AP(src.tensor, src.offset, [list(src.ap[0]), [2, LP], [CMP_STRIDE, N_CMP]])
                    pe_ = peT[:, 16 * k:16 * k + 16]
                    peb = bass.AP(pe_.tensor, pe_.offset, [list(pe_.ap[0]), [1, LP], [0, N_CMP]])
                    ins = tt(blk[:, :, g, 0:N_CMP], win, peb, ALU.add)
                ins.then_inc(sem("blocks"), 1)

            last = by_name["pool"]
            dve.wait_ge(emptied[(last.first) % RING], last.first // RING + 1)
            dve.wait_ge(emptied[(last.first + 1) % RING], (last.first + 1) // RING + 1)
            link(dve.reciprocal(icount, icount))
            for g, win in enumerate((2, 4, 8, 16)):
                src, step = uT[:, g, :], 1
                bufs = (mixT[:, 0, :], mixT[:, 1, :])
                n = 0
                while step < win:
                    dst = bufs[n % 2]
                    tt(dst[:, step:T], src[:, step:T], src[:, 0:T - step], ALU.add)
                    link(dve.tensor_copy(dst[:, 0:step], src[:, 0:step]))
                    src, step, n = dst, 2 * step, n + 1
                link(tt(mixT[:, 2, 0:win], src[:, 0:win], icount[:, 0:win], ALU.mult))
                tt(uT[:, g, 0:win], mixT[:, 2, 0:win], uT[:, g, 0:win], ALU.subtract)
                link(stt(uT[:, g, win:T], src[:, win:T], 1.0 / win, uT[:, g, win:T], ALU.mult, ALU.subtract))
            dve.sem_inc(sem("pooled"), 1)

            dve.wait_ge(sem("bias_in"), 32)
            b = bcmp.rearrange("p (t h) c -> p t h c", t=TT)
            dve.tensor_copy(b[:, 0, :, 0:7], bias[:, :, CMP_LEN - 1:P:CMP_STRIDE])
            link(dve.tensor_copy(b[:, 1, :, 0:N_CMP], bias[:, :, P + CMP_LEN - 1:3 * P:CMP_STRIDE]))
            for par in range(2):
                def mine(ap, c):
                    return ap.rearrange("p (n e r) c -> p n e r c", e=2, r=4)[:, :, par, :, 0:c]
                ps = psS[chS.take(dve)]
                tt(mine(scmp, N_CMP), mine(ps[:, :].rearrange("p (n c) -> p n c", c=16), N_CMP), mine(bcmp, N_CMP),
                   ALU.add).then_inc(chS.free, 1)
            dve.wait_ge(chS.free, chS.got)
            link(dve.tensor_reduce(cstat[:, 0], scmp, AX_X, ALU.max))

            def over_c(ap):
                return bass.AP(ap.tensor, ap.offset, [list(ap.ap[0]), [1, 32], [0, N_CMP]])

            tt(scmp, scmp, over_c(cstat[:, 0]), ALU.subtract).then_inc(sem("cmp_scores"), 1)
            dve.wait_ge(sem("cmp_exp"), 1)
            link(dve.tensor_reduce(cstat[:, 1], scmp, AX_X, ALU.add))
            link(dve.reciprocal(cstat[:, 2], cstat[:, 1]))
            c2 = cstat[:, 2].rearrange("p (t h) -> p t h", t=TT)
            c3 = cstat[:, 3].rearrange("p (t h) -> p t h", t=TT)
            g_last = by_name["gate_nsa"].first
            dve.wait_ge(emptied[g_last % RING], g_last // RING + 1)
            link(tt(c3, c2, gate_nsa[:, :, 0:NSA_HEADS], ALU.mult))
            link(ts(c3[:, 0], c3[:, 0], has[:, 0:1], ALU.mult))
            link(tt(scmp, scmp, over_c(cstat[:, 3]), ALU.mult))
            s5 = scmp.rearrange("p (t g r) c -> p t g r c", t=TT, g=4)
            for t in range(TT):
                for r in range(4):
                    ins = dve.tensor_copy(pcmp[:, t, r, :, 0:N_CMP], s5[:, t, :, r, :])
            ins.then_inc(sem("cmp_probs"), 1)
            for g in range(NSA_GROUPS):
                ps = psS[chS.take(dve)]
                dve.tensor_copy(o_nsa[:, :, 256 * g:256 * g + 256], halves(ps[:, :])).then_inc(chS.free, 1)
            for half in range(2):
                ps = psS[chS.take(dve)]
                for g in (2 * half, 2 * half + 1):
                    at_ = GAIN_AT["pool_scale"] + g
                    ins = ts(mixT[:, g, :], ps[:, (g % 2) * T:(g % 2 + 1) * T], gains[:, at_:at_ + 1], ALU.mult)
                ins.then_inc(chS.free, 1)
            dve.wait_ge(chS.free, chS.got)
            dve.sem_inc(sem("mixed"), 1)
            attention("nsa")
            attention("x")
            dve.sem_inc(sem("attended"), 1)

            def by_gate(branch):
                def body(st, bk):
                    return tt(merge[:, 8 * branch + 2 * st.j:8 * branch + 2 * st.j + 2, :], halves(bk[:, :]),
                              merge[:, 8 * branch + 2 * st.j:8 * branch + 2 * st.j + 2, :], ALU.mult)
                return body

            m_last = by_name["merge"].first + 11
            for k in range(RING):
                dve.wait_ge(emptied[k], (m_last - k) // RING + 1)
            empties("pool_out", by_gate(0))
            empties("x_out", by_gate(2))
            settle("x_out")
            tt(merge[:, 0:8, :], merge[:, 0:8, :], merge[:, 16:24, :], ALU.add)
            empties("nsa_out", by_gate(1))
            settle("nsa_out")
            tt(merge[:, 0:8, :], merge[:, 0:8, :], merge[:, 8:16, :], ALU.add).then_inc(sem("merged"), 1)

            def add_pair(scale):
                def body(st, bk):
                    x_ = xT[:, 2 * st.j:2 * st.j + 2, :]
                    return stt(x_, halves(bk[:, :]), scale, x_, ALU.mult, ALU.add)
                return body

            empties("w_o", add_pair(1.0))
            settle("w_o")
            do_norm("peer")

            it = iota16

            for t in range(TT):
                for h2 in range(PEER_HEADS // 2):
                    ps = psS[chS.take(dve)]
                    for j in range(4):
                        h, s = 2 * h2 + j // 2, j % 2
                        row = ps[:, j * P:(j + 1) * P]
                        rest = stop_[:, (j % 2) * P:(j % 2 + 1) * P]
                        link(dve.max(ktop[:, h, s, 0:8], row))
                        dve.max_index(kidx[:, h, s, 0:8].bitcast(U32), ktop[:, h, s, 0:8], row)
                        link(dve.match_replace(rest, ktop[:, h, s, 0:8], row, -3.0e38))
                        link(dve.max(ktop[:, h, s, 8:16], rest))
                        ins = dve.max_index(kidx[:, h, s, 8:16].bitcast(U32), ktop[:, h, s, 8:16], rest)
                    ins.then_inc(chS.free, 1)
                dve.wait_ge(chS.free, chS.got)
                dve.tensor_copy(kidf, kidx.bitcast(U32))
                for h in range(PEER_HEADS):
                    x0, x1 = ktop[:, h, 0, :], ktop[:, h, 1, :]
                    ap0 = bass.AP(x0.tensor, x0.offset, [list(x0.ap[0]), [1, 16], [0, 16]])
                    ap1 = bass.AP(x1.tensor, x1.offset, [list(x1.ap[0]), [0, 16], [1, 16]])
                    link(tt(cand[:, h], ap0, ap1, ALU.add))
                    row = cand[:, h].rearrange("p a b -> p (a b)")
                    link(dve.max(best[:, h, 0:8], row))
                    dve.max_index(bpos[:, h, 0:8].bitcast(U32), best[:, h, 0:8], row)
                    link(dve.match_replace(cand2[:, h], best[:, h, 0:8], row, -3.0e38))
                    link(dve.max(best[:, h, 8:16], cand2[:, h]))
                    link(dve.max_index(bpos[:, h, 8:16].bitcast(U32), best[:, h, 8:16], cand2[:, h]))
                bp = bpos.rearrange("p h k -> p (h k)").bitcast(U32)
                ts(bhalf[:, 0].bitcast(U32), bp, 4, ALU.logical_shift_right)
                link(ts(bhalf[:, 1].bitcast(U32), bp, 15, ALU.bitwise_and))
                link(dve.tensor_copy(bhalff, bhalf.bitcast(U32)))
                for s in range(2):
                    e3 = eq.rearrange("p (n c) -> p n c", c=16)
                    x_ = bhalff[:, s, :]
                    pos_b = bass.AP(x_.tensor, x_.offset, [list(x_.ap[0]), [1, SLOTS], [0, 16]])
                    io_b = bass.AP(it.tensor, it.offset, [list(it.ap[0]), [0, SLOTS], [1, 16]])
                    link(tt(e3, pos_b, io_b, ALU.is_equal))
                    k_ = kidf[:, :, s, :]
                    num_b = bass.AP(k_.tensor, k_.offset, [list(k_.ap[0]), [32, PEER_HEADS], [0, TOPK], [1, 16]])
                    e4 = eq.rearrange("p (h k c) -> p h k c", h=8, k=16)
                    link(tt(e4, e4, num_b, ALU.mult))
                    link(dve.tensor_reduce(which[:, s, :], e3, AX_X, ALU.add))
                link(stt(idf, which[:, 0, :], float(KEYS), which[:, 1, :], ALU.mult, ALU.add))
                dve.tensor_copy(ids[:, t].bitcast(U32), idf).then_inc(sem("ids_ready"), 1)
                g3 = gate[:, t].rearrange("p (h k) -> p h k", h=8)
                b0 = best[:, :, 0:1]
                top_b = bass.AP(b0.tensor, b0.offset, [list(b0.ap[0]), [16, 8], [0, 16]])
                tt(g3, best, top_b, ALU.subtract).then_inc(sem("best_ready"), 1)
                dve.wait_ge(sem("gate_exp"), t + 1)
                link(dve.tensor_reduce(gsum, g3, AX_X, ALU.add))
                link(dve.reciprocal(gsum, gsum))
                gs_b = bass.AP(gsum.tensor, gsum.offset, [list(gsum.ap[0]), [1, 8], [0, 16]])
                link(tt(g3, g3, gs_b, ALU.mult))

            for t in range(TT):
                n = (2 * t) * SLOTS
                with dve.Fori(0, SLOTS // GATHERS) as i:
                    for k in range(GATHERS):
                        dve.wait_ge(sem(f"rows_in{k}"), i * 16 + (16 + 16 * (n // GATHERS)))
                        dve.tensor_tensor_reduce(gath[:, k, :], gath[:, k, :], hrow[:, t, :], 1.0, 0.0, ALU.mult, ALU.add,
                                                 dcol[:, k:k + 1]).then_inc(sem("rows_used"), 1)
                    dve.wait_ge(sem("rows_used"), i * GATHERS + (n + 2 * GATHERS))
                    dve.tensor_copy(dots[:, t, bass.ds(i * GATHERS, GATHERS)], dcol).then_inc(sem("dots_part"), 1)
                    dve.wait_ge(sem("dots_part"), i + (t * (SLOTS // GATHERS) + 1))
                dve.wait_ge(sem("dots_part"), (t + 1) * SLOTS // GATHERS)
                dve.sem_inc(sem("dots_ready"), 1)
                dve.wait_ge(sem("gelu_done"), t + 1)
                link(tt(wgt[:, t], wgt[:, t], gate[:, t], ALU.mult))
                link(dve.memset(yacc[:, t], 0.0))
                n += SLOTS
                with dve.Fori(0, SLOTS // GATHERS) as i:
                    for k in range(GATHERS):
                        dve.wait_ge(sem(f"rows_in{k}"), i * 16 + (16 + 16 * (n // GATHERS)))
                        stt(yacc[:, t, :], gath[:, k, :], wgt[:, t, bass.ds(i * GATHERS + k, 1)], yacc[:, t, :],
                            ALU.mult, ALU.add).then_inc(sem("rows_used"), 1)
                        dve.wait_ge(sem("rows_used"), i * GATHERS + (n + GATHERS + k + 1))
                dve.sem_inc(sem("experts_done"), 1)
            for t in range(TT):
                for q in range(2):
                    ps = psS[chS.take(dve)]
                    x_ = xT[:, 4 * q:4 * q + 4, t * P:(t + 1) * P]
                    tt(x_, ps[:, :].rearrange("p (c t) -> p c t", c=4), x_, ALU.add).then_inc(chS.free, 1)
            dve.wait_ge(chS.free, chS.got)
            do_norm("first")

            pairs_done = [0]

            def ffn(i, s):
                jb, jo = by_name[f"ffn_in{i}{s}"], by_name[f"ffn_out{i}{s}"]
                k0 = pairs_done[0]
                pairs_done[0] += FC // 2
                h0 = (2 * i + s) * (FC // 2)

                def ahead(st):
                    if not st.per and st.j + 2 >= jb.panels:
                        low_part(jo, Step(jo.first, st.j + 2 - jb.panels, 0, False))
                    else:
                        low_part(jb, after(st, 2))

                def one(st):
                    if st.j % 2 == 0:
                        ahead(st)
                        return
                    gate_slot = (st.slot - 1) % RING
                    g_uses = (jb.first + st.j - 1) // RING + 1
                    more = st.turn * 2 if st.per else 0
                    dve.wait_ge(emptied[gate_slot], st.turn + g_uses)
                    dve.wait_ge(multiplied, st.number + 1)
                    sg = halves(sgate[:, (st.j // 2 + k0) % 2, :])
                    tt(sg, halves(bank[st.slot][:, :]), sg, ALU.mult).then_inc(emptied[st.slot], 1)
                    dve.wait_ge(emptied[st.slot], st.uses + 1)
                    dve.sem_inc(sem("hidden_pair"), 1)
                    ahead(st)
                    at_ = st.at(lambda j: 2 * (j // 2))
                    both = slice(at_, at_ + 2) if not st.per else bass.ds(at_, 2)
                    dve.wait_ge(sem("h_high"), h0 + st.j // 2 + 1 + more)
                    tt(h_low[:, both, :], sg, h_high[:, both, :].bitcast(F32), ALU.subtract).then_inc(sem("h_low"), 1)
                    dve.wait_ge(sem("h_low"), h0 + st.j // 2 + 1 + more)
                    dve.sem_inc(sem("sgate_free"), 1)
                panels_of(dve, jb, one, ahead=2)

                for j in range(DC):
                    if j < DC - 2:
                        low_part(jo, Step(jo.first, j + 2, 0, False))
                    st = Step(jo.first, j, 0, False)
                    dve.wait_ge(multiplied, st.number + 1)
                    stt(xT[:, j, :], bank[st.slot][:, 0:T], 0.5, xT[:, j, :], ALU.mult, ALU.add).then_inc(emptied[st.slot], 1)
                settle(f"ffn_out{i}{s}")

            def ple(i):
                name = f"ple{i}"
                k0 = pairs_done[0]
                pairs_done[0] += 4

                def one(st):
                    if st.j % 2 == 0:
                        return
                    gate_slot = (st.slot - 1) % RING
                    g_uses = (by_name[name].first + st.j - 1) // RING + 1
                    dve.wait_ge(emptied[gate_slot], st.turn + g_uses if st.per else g_uses)
                    if st.per:
                        dve.sem_inc(sem("dve_turn"), 1)
                    dve.wait_ge(multiplied, st.number + 1)
                    at_ = st.at(lambda j: 2 * (j // 2))
                    x_ = xT[:, bass.ds(at_, 2), :] if st.per else xT[:, at_:at_ + 2, :]
                    sg = halves(sgate[:, (st.j // 2 + k0) % 2, :])
                    tt(sg, halves(bank[st.slot][:, :]), sg, ALU.mult).then_inc(emptied[st.slot], 1)
                    dve.wait_ge(emptied[st.slot], st.uses + 1)
                    if st.per:
                        dve.sem_inc(sem("dve_turn"), 1)
                    tt(x_, x_, sg, ALU.add).then_inc(sem("sgate_free"), 1)
                panels_of(dve, by_name[name], one)
                dve.wait_ge(sem("sgate_free"), pairs_done[0] + 2)

            first_low(0, 0)
            do_norm("ffn00")
            ffn(0, 0)
            do_norm("mix0")
            dve.wait_ge(sem("pos_in"), 48)
            R = slice(0, ROPE)
            link(dve.tensor_copy(posf[R, :], posi[R, :].bitcast(I32)))
            link(ts(ang[R, 0], posf[R, :], freq[R, 0:1], ALU.mult))
            link(ts(ang[R, 1], ang[R, 0], INV_TWO_PI, ALU.mult))
            link(ts(ang[R, 1], ang[R, 1], MAGIC, ALU.add))
            link(ts(ang[R, 1], ang[R, 1], -MAGIC, ALU.add))
            for part_ in TWO_PI_PARTS:
                link(stt(ang[R, 0], ang[R, 1], -part_, ang[R, 0], ALU.mult, ALU.add))
            link(ts(ang[R, 0], ang[R, 0], 3.1415925, ALU.min, -3.1415925, ALU.max))
            dve.sem_inc(sem("angles"), 1)
            dve.wait_ge(sem("sines"), 2)
            link(tt(cosT[R, :], cosT[R, :], cosT[R, :], ALU.mult))
            ts(cosT[R, :], cosT[R, :], -2.0, ALU.mult, 1.0, ALU.add)
            link(ts(sinT[0:32, :], sinT[0:32, :], -1.0, ALU.mult))
            for name, dst in (("cq", cqT), ("ckv", None)):
                st = Step(by_name[name].first, 0, 0, False)
                dve.wait_ge(multiplied, st.number + 1)
                bk = bank[st.slot]
                if dst is not None:
                    link2 = dve.tensor_copy(dst, halves(bk[:, :]))
                else:
                    dve.tensor_copy(ckvT, bk[:, 0:T].rearrange("p (c t) -> p c t", c=1))
                    link2 = dve.tensor_copy(krT[R, :], bk[R, T:2 * T])
                link2.then_inc(emptied[st.slot], 1)
                dve.wait_ge(emptied[st.slot], st.uses + 1)
            do_norm("cq")
            do_norm("ckv")

            def rotate(dst, src):
                link(tt(rope_sw[R, :], rope_sw[R, :], sinT[R, :], ALU.mult))
                link(tt(src, src, cosT[R, :], ALU.mult))
                link(tt(dst, src, rope_sw[R, :], ALU.add))
                dve.sem_inc(sem("rope_go"), 1)

            dve.sem_inc(sem("rope_go"), 1)
            dve.wait_ge(sem("swapped"), 1)
            rotate(krT[R, :], krT[R, :])
            for h in range(MLA_HEADS):
                st = Step(by_name["uq"].first, h, 0, False)
                dve.wait_ge(emptied[st.slot], st.uses + 1)
                rotate(qrT[R, h, :], rope_in[R, :])
            attention("mla")
            dve.sem_inc(sem("attended"), 1)
            empties("mla_o", add_pair(1.0), lambda: first_low(0, 1))
            settle("mla_o")
            do_norm("ffn01")
            ffn(0, 1)
            do_norm("ple0")
            ple(0)
            first_low(1, 0)
            do_norm("ffn10")
            ffn(1, 0)
            do_norm("mix1")
            st = Step(by_name["ff"].first, 0, 0, False)
            dve.wait_ge(multiplied, st.number + 1)
            f3 = [ftmp[:, k].rearrange("p (t h) -> p t h", t=TT) for k in range(6)]
            fb = bass.AP(fbias.tensor, fbias.offset, [list(fbias.ap[0]), [0, TT], [1, FOX_HEADS]])
            tt(f3[0], bank[st.slot][:, :].rearrange("p (t n) -> p t n", t=TT)[:, :, 0:FOX_HEADS], fb, ALU.add)\
                .then_inc(emptied[st.slot], 1)
            dve.wait_ge(emptied[st.slot], st.uses + 1)
            link(stt(f3[1], f3[0], -1.0, f3[0], ALU.mult, ALU.max))
            dve.sem_inc(sem("forget"), 1)
            dve.wait_ge(sem("fexp"), 1)
            link(ts(f3[2], f3[1], 1.0, ALU.add))
            dve.sem_inc(sem("forget"), 1)
            link(ts(f3[3], f3[0], 0.0, ALU.min))
            dve.wait_ge(sem("fexp"), 2)
            link(tt(logf, f3[3], f3[2], ALU.subtract))
            dve.sem_inc(sem("forget"), 1)
            for t in range(TT):
                l_ = logf[:, t, :]
                lb = bass.AP(l_.tensor, l_.offset, [list(l_.ap[0]), [1, FOX_HEADS], [0, P]])
                link(dve.tensor_copy(logf_wide[:, t].rearrange("p (h q) -> p h q", h=8), lb))
            dve.sem_inc(sem("forget"), 1)
            ps = psS[chS.take(dve)]
            dve.tensor_copy(cumq, ps[:, 0:16].rearrange("p (t h) -> p t h", t=TT)).then_inc(chS.free, 1)
            for h2 in range(FOX_HEADS // 2):
                ps = psS[chS.take(dve)]
                ts(ncum[:, 2 * h2:2 * h2 + 2, P:3 * P], halves(ps[:, :]), -1.0, ALU.mult)
                ts(ncum[:, 2 * h2:2 * h2 + 2, 0:P], halves(ps[:, :])[:, :, 0:P], -1.0, ALU.mult).then_inc(chS.free, 1)
            dve.wait_ge(chS.free, chS.got)
            attention("fox")
            dve.sem_inc(sem("attended"), 1)
            empties("fox_o", add_pair(1.0), lambda: first_low(1, 1))
            settle("fox_o")
            do_norm("ffn11")
            ffn(1, 1)
            do_norm("ple1")
            ple(1)
            do_norm("final")


NAMES = ["x", "mem", "rel_bias", "g_mix", "w_in", "w_pool_grp", "pool_scale", "w_pool_out", "w_cmp_k", "w_cmp_v", "pe_k",
         "pe_v", "w_nsa_out", "g_mem", "w_mem_kv", "w_x_out", "w_o", "g_ffn", "w_peer_q", "peer_sub_keys", "peer_u",
         "peer_v", "g_final", "p_2", "positions_2", "ffn_norm_2", "ffn_w_in_2", "ffn_w_out_2", "mix_norm_2",
         "mla_w_down_2", "mla_q_norm_2", "mla_w_uq_2", "mla_kv_norm_2", "mla_w_ukv_2", "mla_w_o_2", "fox_w_in_2",
         "fox_b_f_2", "fox_w_o_2", "ple_norm_2", "ple_w_gate_2", "ple_w_proj_2", "final_norm_2"]


def kernel(**inputs):
    import numpy as np
    import concourse.bacc as bacc
    from concourse.bass_utils import run_bass_kernel_spmd

    n = np.arange(T)[::-1]
    large = 16 + (np.log(np.maximum(n, 1).astype(np.float32) / np.float32(16)) / np.float32(math.log(8)) * np.float32(16)).astype(np.int32)
    bucket = np.where(n < 16, n, np.minimum(large, BUCKETS - 1))
    onehot = (np.arange(BUCKETS)[:, None] == bucket[None, :]).astype(np.float32)
    half = (10000.0 ** (-np.arange(0, ROPE, 2, dtype=np.float64) / ROPE)).astype(np.float32)
    freq = np.concatenate([half, half])[:, None]

    nc = bacc.Bacc("TRN2", target_bir_lowering=False, num_devices=1)
    arrays, aps = {}, {}
    for name in NAMES:
        arr = np.ascontiguousarray(inputs[name])
        arrays[name + "_in"] = arr
        aps[name] = nc.dram_tensor(name + "_in", arr.shape, mybir.dt.from_np(arr.dtype), kind="ExternalInput").ap()
    arrays["onehot_in"], arrays["freq_in"] = onehot, freq
    hot = nc.dram_tensor("onehot_in", onehot.shape, F32, kind="ExternalInput").ap()
    fr = nc.dram_tensor("freq_in", freq.shape, F32, kind="ExternalInput").ap()
    out = nc.dram_tensor("out", (1, T, D), F32, kind="ExternalOutput").ap()
    build(nc, aps, out, hot, fr)
    r = run_bass_kernel_spmd(nc, [arrays], core_ids=[0])
    return r.results[0]["out"]
```

```python
import math
from contextlib import ExitStack

import concourse.bass as bass
from concourse import mybir

ALU = mybir.AluOpType
ACT = mybir.ActivationFunctionType
F32 = mybir.dt.float32
U32 = mybir.dt.uint32
F32R = mybir.dt.float32r
I32 = mybir.dt.int32
AX_X = mybir.AxisListType.X

P = 128
T = 256
TT = T // P
D = 1024
DC = D // P
POOL_W, NSA_W, KV_W = 512, 1024, 256
NSA_HEADS, NSA_GROUPS, HEAD = 16, 4, 64
HEADS_PER_GROUP = NSA_HEADS // NSA_GROUPS
CMP_LEN, CMP_STRIDE = 32, 16
N_CMP = (T - CMP_LEN) // CMP_STRIDE + 1
CMP_SLOT = 32
LP = CMP_LEN // 2
X_HEADS = 4
BUCKETS = 32
PEER_HEADS, KEYS, TOPK = 8, 128, 16
SLOTS = PEER_HEADS * TOPK
D_FF = 2816
FC = D_FF // P
MLA_HEADS, ROPE = 8, 64
FOX_HEADS = 8
NEG = -1e30
EPS = 1e-6
MAGIC = 1.5 * 2.0 ** 23
TWO_PI_PARTS = (6.28125, 0.00193500518798828125, 2 * math.pi - 6.28125 - 0.00193500518798828125)
INV_TWO_PI = 0.15915494309189535

Z_POOL, Z_Q, Z_KV = 0, POOL_W, POOL_W + NSA_W
Z_GATE = Z_KV + 6 * KV_W
Z_QX = Z_GATE + 3 * NSA_HEADS
Z_MERGE = Z_QX + X_HEADS * P

GAINS = [("g_mix", 8), ("g_mem", 8), ("g_ffn", 8), ("g_final", 8), ("ffn_norm_2", 32), ("mix_norm_2", 16),
         ("ple_norm_2", 16), ("final_norm_2", 8), ("mla_q_norm_2", 2), ("mla_kv_norm_2", 1), ("pool_scale", 4)]
GAIN_AT = {}
for _name, _n in GAINS:
    GAIN_AT[_name] = sum(n for _, n in GAINS[:len(GAIN_AT)])
N_GAINS = sum(n for _, n in GAINS)

RING = 4
PANEL = FC * P
GATHERS = 8
LAG = 3
BY_PE = (1, 4, 7)


class Job:

    def __init__(self, name, panels, kind, weight, rows, cols, width, act):
        self.name, self.panels, self.kind = name, panels, kind
        self.weight, self.rows, self.cols, self.width, self.act = weight, rows, cols, width, act
        self.first = 0
        self.split = None
        self.split_first = 0


class Step:

    def __init__(self, first, j, turn, per):
        self.j, self.turn, self.per, self.origin = j, turn, per, first
        self.slot = (first + j) % RING
        self.uses = (first + j) // RING + turn
        self.number = first + j + (turn * RING if per else 0)

    def at(self, f):
        if not self.per:
            return f(self.j)
        return f(self.j) + self.turn * (f(self.j + RING) - f(self.j))


def panels_of(eng, job, body, ahead=0):
    turns = (job.panels - ahead) // RING
    done = 0
    if turns >= 2 and job.first >= RING:
        with eng.Fori(0, turns) as i:
            for j in range(RING):
                body(Step(job.first, j, i, True))
        done = turns * RING
    for j in range(done, job.panels):
        body(Step(job.first, j, 0, False))


def over_partitions(row, n):
    return bass.AP(row.tensor, row.offset, [[0, n], [1, row.shape[-1]]])


def build(nc, a, out, onehot, inv_freq):
    ctx = ExitStack()
    with ctx:
        def sb(name, shape, dt=F32):
            return ctx.enter_context(nc.sbuf_tensor(name, shape, dt))

        sems = {}

        def sem(name):
            if name not in sems:
                sems[name] = ctx.enter_context(nc.semaphore(name))
            return sems[name]

        xT = sb("xT", [P, DC, T])
        nT = sb("nT", [P, DC, T])
        ring = sb("ring", [P, RING, PANEL])
        work = sb("work", [P, 3, LAG, 512])
        soft, prob, probT = work[:, 0], work[:, 1], work[:, 2]
        squares = work[:, :, :, :].rearrange("p n a b -> p (n a b)")
        ident = sb("ident", [P, P])
        ones = sb("ones", [P, P])
        causal = sb("causal", [P, 3 * P])
        chunked = sb("chunked", [P, 3 * P])
        zeros = sb("zeros", [P, 512])
        tri = sb("tri", [P, TT, T])
        gains = sb("gains", [P, N_GAINS])
        root = sb("root", [P, T])
        rstd = sb("rstd", [P, T])
        nmax = sb("nmax", [P, LAG, TT])
        sums = sb("sums", [P, LAG, TT])
        inv = sb("inv", [P, LAG, TT])
        coef = sb("coef", [P, LAG, TT])
        has = sb("has", [P, 1])
        eps = sb("eps", [P, 1])
        iota16 = sb("iota16", [P, 16])[:, :]
        arena_byte = nc.sbuf_base
        arena = sb("arena", [P, 30208])
        spot = [0]

        def parts_at(name, shape, at):
            return nc.alloc_sbuf_tensor_at(name, [P] + shape, F32R, offset=arena_byte + 4 * at)

        def part(n, at=None):
            if at is None:
                at = spot[0]
                spot[0] += n
                assert spot[0] <= 30208, spot[0]
            return arena[:, at:at + n]

        merge = part(24 * T).rearrange("p (c t) -> p c t", c=24)
        tokk = part(1024, 0).rearrange("p (g t) -> p g t", g=4)
        tokv = part(1024, 1024).rearrange("p (g t) -> p g t", g=4)
        blkk = part(2048, 2048).rearrange("p (l g c) -> p l g c", l=LP, g=4)
        blkv = part(2048, 4096).rearrange("p (l g c) -> p l g c", l=LP, g=4)
        bias_at = spot[0]
        bias = part(NSA_HEADS * 384).rearrange("p (h k) -> p h k", h=NSA_HEADS)
        x_in = part(2048, bias_at).rearrange("p (t d) -> p t d", t=TT)
        mem_in = part(2048, bias_at + 2048).rearrange("p (t d) -> p t d", t=TT)
        rows_in = part(P, bias_at + 4096)
        pe_in = part(P, bias_at + 4224)
        q_at = spot[0]
        qT = part(2048).rearrange("p (c t) -> p c t", c=8)
        kselT = part(512).rearrange("p (c t) -> p c t", c=2)
        kwinT = part(512).rearrange("p (c t) -> p c t", c=2)
        vsel = part(512).rearrange("p (t d) -> p t d", t=2)
        vwin = part(512).rearrange("p (t d) -> p t d", t=2)
        o_at = spot[0]
        o_nsa = part(2048).rearrange("p (t d) -> p t d", t=2)
        memT = part(2048, o_at).rearrange("p (c t) -> p c t", c=8)
        w_cmp = part(2 * 1024).rearrange("p (k l d) -> p k l d", k=2, l=LP)
        w_grp = part(512).rearrange("p (g d) -> p g d", g=4)
        qxT = part(1024).rearrange("p (c t) -> p c t", c=4)
        kxT = part(1024).rearrange("p (c t) -> p c t", c=4)
        vx = part(1024).rearrange("p (t d) -> p t d", t=2)
        uT = part(1024).rearrange("p (c t) -> p c t", c=4)
        mixT = part(1024).rearrange("p (c t) -> p c t", c=4)
        o_x = part(1024, spot[0]).rearrange("p (t d) -> p t d", t=2)
        pcmp = part(1024).rearrange("p (t r g c) -> p t r g c", t=2, r=4, g=4)
        pcmpT = part(1024).rearrange("p (t r q) -> p t r q", t=2, r=4)
        scmp = part(480).rearrange("p (n c) -> p n c", c=N_CMP)
        bcmp = part(512).rearrange("p (n c) -> p n c", c=16)
        kcT = part(2 * N_CMP).rearrange("p (s c) -> p s c", s=2)
        vc = part(HEAD)
        cstat = part(4 * 32).rearrange("p (k n) -> p k n", k=4)
        gate_nsa = part(TT * 48).rearrange("p (t n) -> p t n", t=TT)
        peT = part(32)
        table = part(384, q_at)
        rel = part(16, q_at + 384)
        hot = part(256, q_at + 400)
        icount = part(16)
        oxT = uT[:, :, :]
        spot[0] = 0
        gath = part(GATHERS * D).rearrange("p (k d) -> p k d", k=GATHERS)
        qpT = part(16 * T).rearrange("p (c t) -> p c t", c=16)
        sub_in = part(2048).rearrange("p (c k) -> p c k", c=16)
        eq = sub_in.rearrange("p c k -> p (c k)")
        hrow = part(2048).rearrange("p (t d) -> p t d", t=TT)
        subT = part(2048).rearrange("p (c k) -> p c k", c=16)
        cand = part(2048).rearrange("p (h a b) -> p h a b", h=8, a=16)
        cand2 = part(2048).rearrange("p (h n) -> p h n", h=8)
        yacc = part(2048).rearrange("p (t d) -> p t d", t=TT)
        stop_ = part(2 * P)
        ktop = part(256).rearrange("p (h s k) -> p h s k", h=8, s=2)
        kidx = part(256).rearrange("p (h s k) -> p h s k", h=8, s=2)
        kidf = part(256).rearrange("p (h s k) -> p h s k", h=8, s=2)
        best = part(P).rearrange("p (h k) -> p h k", h=8)
        bpos = part(P).rearrange("p (h k) -> p h k", h=8)
        bhalf = part(2 * P).rearrange("p (s n) -> p s n", s=2)
        bhalff = part(2 * P).rearrange("p (s n) -> p s n", s=2)
        which = part(2 * P).rearrange("p (s n) -> p s n", s=2)
        idf = part(P)
        ids = part(TT * P).rearrange("p (t n) -> p t n", t=TT)
        idcol = part(GATHERS)
        gate = part(TT * P).rearrange("p (t n) -> p t n", t=TT)
        dots = part(TT * P).rearrange("p (t n) -> p t n", t=TT)
        wgt = part(TT * P).rearrange("p (t n) -> p t n", t=TT)
        dcol = part(GATHERS)
        gsum = part(8)
        wcol = part(len(BY_PE))
        diag = part(len(BY_PE) * P).rearrange("p (k n) -> p k n", k=len(BY_PE))
        w_high = parts_at("w_high", [2, PANEL], 0)
        w_low = parts_at("w_low", [2, PANEL], 2 * PANEL)
        h_high = parts_at("h_high", [FC, T], 4 * PANEL)
        h_low = parts_at("h_low", [FC, T], 4 * PANEL + FC * T)
        spot[0] = 4 * PANEL + 2 * FC * T
        n_high = parts_at("n_high", [DC, T], spot[0])
        n_low = parts_at("n_low", [DC, T], spot[0] + DC * T)
        spot[0] += 2 * DC * T
        sgate = part(1024).rearrange("p (k n) -> p k n", k=2)
        p_in = part(4 * 256).rearrange("p (i t d) -> p i t d", i=2, t=2)
        pT = part(4 * 256).rearrange("p (i c t) -> p i c t", i=2, c=2)
        fbias = part(8)
        freq = part(1)
        posi = part(256)
        spot[0] = 0
        q2T = part(2048).rearrange("p (c t) -> p c t", c=8)
        qrT = part(2048).rearrange("p (c t) -> p c t", c=8)
        k2T = part(2048).rearrange("p (c t) -> p c t", c=8)
        v2 = part(2048).rearrange("p (t d) -> p t d", t=2)
        o2 = part(2048).rearrange("p (t d) -> p t d", t=2)
        cqT = part(512).rearrange("p (c t) -> p c t", c=2)
        ckvT = part(256).rearrange("p (c t) -> p c t", c=1)
        krT = part(256)
        rope_in = part(256)
        rope_sw = part(256)
        cosT = part(256)
        sinT = part(256)
        ncum = part(8 * 384).rearrange("p (h k) -> p h k", h=8)
        ftmp = part(6 * 16).rearrange("p (k n) -> p k n", k=6)
        logf = part(16).rearrange("p (t h) -> p t h", t=2)
        logf_wide = part(2048).rearrange("p (t n) -> p t n", t=2)
        cumq = part(16).rearrange("p (t h) -> p t h", t=2)
        posf = part(256)
        ang = part(3 * 256).rearrange("p (k t) -> p k t", k=3)
        assert spot[0] <= 4 * PANEL + 2 * FC * T
        xrow = part(2048, 0).rearrange("p (t d) -> p t d", t=TT)

        bank = [ctx.enter_context(nc.psum_tensor(f"bank{i}", [P, 512], F32)) for i in range(RING)]
        psS = [ctx.enter_context(nc.psum_tensor(f"psS{i}", [P, 512], F32)) for i in range(2)]
        psP = ctx.enter_context(nc.psum_tensor("psP", [P, 512], F32))
        psO = ctx.enter_context(nc.psum_tensor("psO", [P, 512], F32))
        toeplitz = nc.dram_tensor("toeplitz", (NSA_HEADS, P, 384), F32, kind="Internal")

        w_in = a["w_in"][0]
        L = range(2)

        def wv(ap):
            return ap.rearrange("(c p) n -> p c n", p=P)

        def job(name, panels, kind, weight, cols, width, act, chunks=DC):
            return Job(name, panels, kind, lambda j: wv(weight), lambda j: chunks, cols, width, lambda j: act)

        jobs = [job("kv", 6, None, w_in, lambda j: Z_KV + 256 * j, 256, nT)]
        jobs[0].kind = lambda j: "T" if j in (3, 5) else "F"
        jobs += [
            job("q", 4, "F", w_in, lambda j: Z_Q + 256 * j, 256, nT),
            job("gate_nsa", 1, "T", w_in, lambda j: Z_GATE, 48, nT),
            job("qx", 2, "F", w_in, lambda j: Z_QX + 256 * j, 256, nT),
            job("pool", 2, "F", w_in, lambda j: Z_POOL + 256 * j, 256, nT),
            job("kx", 2, "F", a["w_mem_kv"][0], lambda j: 256 * j, 256, memT),
            job("vx", 2, "T", a["w_mem_kv"][0], lambda j: 512 + 256 * j, 256, memT),
            job("merge", 12, "F", w_in, lambda j: Z_MERGE + 256 * j, 256, nT),
            job("pool_out", 4, "F", a["w_pool_out"][0], lambda j: 256 * j, 256, mixT, 4),
            job("x_out", 4, "F", a["w_x_out"][0], lambda j: 256 * j, 256, oxT, 4),
            job("nsa_out", 4, "F", a["w_nsa_out"][0], lambda j: 256 * j, 256, nT),
            job("w_o", 4, "F", a["w_o"][0], lambda j: 256 * j, 256, merge),
            job("peer_q", 8, "F", a["w_peer_q"][0], lambda j: 256 * j, 256, nT),
        ]

        def ffn_jobs(i, s):
            w = a["ffn_w_in_2"][i, s]
            j1 = job(f"ffn_in{i}{s}", FC, "F", w, lambda j: (j % 2) * D_FF + 256 * (j // 2), 256, None)
            j2 = job(f"ffn_out{i}{s}", DC, "F", a["ffn_w_out_2"][i, s], lambda j: 128 * j, 128, None, FC)
            j1.split, j2.split = (n_high, n_low), (h_high, h_low)
            return [j1, j2]

        def ple_job(i):
            g, w = a["ple_w_gate_2"][i], a["ple_w_proj_2"][i]
            return [Job(f"ple{i}", 8, "F", lambda j: wv(w if j % 2 else g), lambda j: 2 if j % 2 else DC,
                        lambda j: 256 * (j // 2), 256, lambda j: pT[:, i] if j % 2 else nT)]

        jobs += ffn_jobs(0, 0) + [
            job("cq", 1, "F", a["mla_w_down_2"][0], lambda j: 0, 256, nT),
            job("ckv", 1, "F", a["mla_w_down_2"][0], lambda j: 256, 192, nT),
            job("uq", 8, "F", a["mla_w_uq_2"][0], lambda j: 192 * j, 192, cqT, 2),
            job("ukv", 8, "FT", a["mla_w_ukv_2"][0], lambda j: 256 * j, 256, ckvT, 1),
            job("mla_o", 4, "F", a["mla_w_o_2"][0], lambda j: 256 * j, 256, nT),
        ] + ffn_jobs(0, 1) + ple_job(0) + ffn_jobs(1, 0) + [
            job("fq", 4, "F", a["fox_w_in_2"][0], lambda j: 256 * j, 256, nT),
            job("fk", 4, "F", a["fox_w_in_2"][0], lambda j: D + 256 * j, 256, nT),
            job("fv", 4, "T", a["fox_w_in_2"][0], lambda j: 2 * D + 256 * j, 256, nT),
            job("ff", 1, "T", a["fox_w_in_2"][0], lambda j: 3 * D, FOX_HEADS, nT),
            job("fox_o", 4, "F", a["fox_w_o_2"][0], lambda j: 256 * j, 256, nT),
        ] + ffn_jobs(1, 1) + ple_job(1)
        at = 0
        by_name = {}
        n_split = 0
        for j_ in jobs:
            j_.first, j_.split_first = at, n_split
            if j_.split:
                n_split += j_.panels
            at += j_.panels
            by_name[j_.name] = j_
        landed = [sem(f"landed{k}") for k in range(RING)]
        multiplied = sem("multiplied")
        emptied = [sem(f"emptied{k}") for k in range(RING)]
        high = sem("high")
        low = sem("low")

        def after(st, n):
            return Step(st.origin, st.j + n, st.turn, st.per)

        def split_no(job_, st):
            return st.number - job_.first + job_.split_first

        def halved(job_, st):
            return (job_.split_first + st.j) % 2, job_.rows(st.j) * job_.width

        def unit(lhs, rhs, scale, mask, width, v, outs, kind, extra=None):
            return dict(lhs=lhs, rhs=rhs, scale=scale, mask=mask, width=width, v=v, outs=outs, kind=kind, extra=extra)

        SEGS = {384: [(0, [(0, 0)]), (1, [(1, 0), (2, 1)])],
                512: [(0, [(0, 0), (1, 1)]), (1, [(2, 0), (3, 1)])]}

        def tok(ap, t):
            return ap[:, t * P:(t + 1) * P]

        nsa_units = []
        for b, (kT_, v_) in enumerate(((kselT, vsel), (kwinT, vwin))):
            for h in range(NSA_HEADS):
                g = h // HEADS_PER_GROUP
                lo = HEAD * (g % 2)
                nsa_units.append(unit(
                    [qT[lo:lo + HEAD, (g // 2) * 4 + h % 4, :]], [kT_[lo:lo + HEAD, g // 2, :]], 1.0, bias[:, h, :], 384,
                    [v_[:, k, g * HEAD:(g + 1) * HEAD] for k in range(TT)],
                    [o_nsa[:, t, h * HEAD:(h + 1) * HEAD] for t in range(TT)],
                    "gated", gate_nsa[:, :, (b + 1) * NSA_HEADS + h]))
        x_units = [unit([qxT[:, h, :]], [kxT[:, h, :]], float(P) ** -0.5, zeros[:, :], 512,
                        [vx[:, k, h * P:(h + 1) * P] for k in range(TT)],
                        [o_x[:, t, h * P:(h + 1) * P] for t in range(TT)], "plain") for h in range(X_HEADS)]
        mla_units = [unit([q2T[:, h, :], qrT[0:ROPE, h, :]], [k2T[:, h, :], krT[0:ROPE, :]], float(P + ROPE) ** -0.5,
                          chunked[:, :], 384, [v2[:, k, h * P:(h + 1) * P] for k in range(TT)],
                          [o2[:, t, h * P:(h + 1) * P] for t in range(TT)], "plain") for h in range(MLA_HEADS)]
        fox_units = [unit([q2T[:, h, :]], [k2T[:, h, :]], float(P) ** -0.5, ncum[:, h, :], 384,
                          [v2[:, k, h * P:(h + 1) * P] for k in range(TT)],
                          [o2[:, t, h * P:(h + 1) * P] for t in range(TT)], "fox", cumq[:, :, h]) for h in range(FOX_HEADS)]
        unit_base = {}
        n_ = 0
        for key, us in (("nsa", nsa_units), ("x", x_units), ("mla", mla_units), ("fox", fox_units)):
            unit_base[key] = (n_, us)
            n_ += len(us)
        biased = sem("biased")
        exped = sem("exped")
        probs_up = sem("probs_up")

        class Channel:

            def __init__(self, name, depth):
                self.full, self.free, self.depth = sem(name + "_full"), sem(name + "_free"), depth
                self.put = self.got = 0

            def claim(self, pe):
                if self.put >= self.depth:
                    pe.wait_ge(self.free, self.put - self.depth + 1)
                self.put += 1
                return (self.put - 1) % self.depth

            def take(self, eng):
                self.got += 1
                eng.wait_ge(self.full, self.got)
                return (self.got - 1) % self.depth

        chS, chP, chO = Channel("S", 2), Channel("P", 1), Channel("O", 1)

        norms = {}

        def norm(name, src, dst, gain, chunks, after_job=None):
            norms[name] = (len(norms), src, dst, GAIN_AT[gain[0]] + gain[1], chunks)
            if after_job:
                early[name] = (len(early), after_job, 1 if after_job.startswith("ffn_out") or after_job == "first" else 2)
            if chunks == DC:
                whole[name] = len(whole)

        early, whole = {}, {}
        norm("mix", xT, nT, ("g_mix", 0), DC)
        norm("mem", memT, memT, ("g_mem", 0), DC)
        norm("peer", xT, nT, ("g_ffn", 0), DC, "w_o")
        norm("first", xT, xT, ("g_final", 0), DC)
        norm("ffn00", xT, nT, ("ffn_norm_2", 0), DC, "first")
        norm("mix0", xT, nT, ("mix_norm_2", 0), DC, "ffn_out00")
        norm("cq", cqT, cqT, ("mla_q_norm_2", 0), 2)
        norm("ckv", ckvT, ckvT, ("mla_kv_norm_2", 0), 1)
        norm("ffn01", xT, nT, ("ffn_norm_2", 8), DC, "mla_o")
        norm("ple0", xT, nT, ("ple_norm_2", 0), DC, "ffn_out01")
        norm("ffn10", xT, nT, ("ffn_norm_2", 16), DC, "ple0")
        norm("mix1", xT, nT, ("mix_norm_2", 8), DC, "ffn_out10")
        norm("ffn11", xT, nT, ("ffn_norm_2", 24), DC, "fox_o")
        norm("ple1", xT, nT, ("ple_norm_2", 8), DC, "ffn_out11")
        norm("final", xT, xT, ("final_norm_2", 0), DC, "ple1")
        late = [name for name in norms if name not in early]
        PAIRS = DC // 2
        norm_pair = sem("norm_pair")
        early_sum = sem("early_sum")
        squared_v, squared_s = sem("squared_v"), sem("squared_s")
        rooted, normed = sem("rooted"), sem("normed")
        src_ready = sem("src_ready")

        ple_pairs = {"ple0": 2 * (FC // 2), "ple1": 4 * (FC // 2) + 4}

        block = ctx.enter_context(nc.Block())

        @block.sync
        def _(sp):
            for jb in jobs:
                def load(st):
                    if not (isinstance(st.number, int) and st.number < RING):
                        sp.wait_ge(emptied[st.slot], st.uses)
                    c = jb.rows(st.j)
                    src = jb.weight(st.j)
                    cols = st.at(jb.cols)
                    src = src[:, :, bass.ds(cols, jb.width)] if st.per else src[:, :, cols:cols + jb.width]
                    dst = ring[:, st.slot, 0:c * jb.width].rearrange("p (c n) -> p c n", c=c)
                    sp.dma_start(dst, src).then_inc(landed[st.slot], 16)
                panels_of(sp, jb, load)
            sp.wait_ge(sem("out_rows"), 4)
            sp.dma_start(out.rearrange("b (t p) d -> p (b t) d", p=P), xrow[:, :, :]).then_inc(sem("stored"), 16)
            sp.wait_ge(sem("stored"), 16)

        @block.gpsimd
        def _(pool):
            chain = [0]

            def link(ins):
                ins.then_inc(sem("pool_chain"), 1)
                chain[0] += 1
                pool.wait_ge(sem("pool_chain"), chain[0])

            def fill(ap, value, keep, base, pattern, mult):
                return pool.affine_select(out=ap, in_=ap, compare_op=keep, fill=value, base=base, pattern=pattern,
                                          channel_multiplier=mult)

            link(pool.memset(ident[:, :], 0.0))
            link(fill(ident[:, :], 1.0, ALU.not_equal, 0, [[-1, P]], 1))
            link(pool.memset(ones[:, :], 1.0))
            link(pool.memset(eps[:, :], EPS))
            pool.sem_inc(sem("consts"), 1)
            link(pool.memset(has[:, :], 1.0))
            link(fill(has[:, :], 0.0, ALU.is_ge, -(CMP_LEN - 1), [[0, 1]], 1))
            link(pool.memset(zeros[:, :], 0.0))
            link(pool.memset(causal[:, :], 0.0))
            link(pool.memset(chunked[:, :], 0.0))
            for lo in (0, 2 * P):
                link(fill(causal[:, lo:lo + P], NEG, ALU.is_ge, 0, [[-1, P]], 1))
            for lo in (HEAD, 2 * P + HEAD):
                link(pool.memset(chunked[0:64, lo:lo + 64], NEG))
            link(pool.memset(tri[:, :, :], 1.0))
            link(fill(tri[:, :, :], 0.0, ALU.is_ge, 0, [[-P, TT], [1, T]], -1))
            link(pool.memset(pcmp, 0.0))
            link(pool.memset(blkv, 0.0))
            link(pool.memset(bcmp, NEG))
            link(pool.memset(table, NEG))
            link(pool.iota(icount, pattern=[[1, 16]], base=1, channel_multiplier=0, allow_small_or_imprecise_dtypes=True))
            link(pool.iota(iota16, pattern=[[1, 16]], base=0, channel_multiplier=0, allow_small_or_imprecise_dtypes=True))
            pool.sem_inc(sem("consts"), 1)

            def early_squares(name):
                n = norms[name][0]
                e, after_job, width = early[name]
                total, one = squares[:, 0:width * T], squares[:, 512:512 + width * T]
                pool.wait_ge(normed, n)
                for g in range(DC // width - 1):
                    if after_job == "first":
                        pool.wait_ge(sem("first_chunk"), g + 1)
                    elif after_job.startswith("ple"):
                        pool.wait_ge(sem("sgate_free"), 2 + ple_pairs[after_job] + g + 1)
                    else:
                        no = by_name[after_job].first + g
                        pool.wait_ge(emptied[no % RING], no // RING + 1)
                    x_ = xT[:, g * width:(g + 1) * width, :].rearrange("p c t -> p (c t)")
                    if g == 0:
                        link(pool.tensor_tensor(total, x_, x_, ALU.mult))
                    else:
                        link(pool.tensor_tensor(one, x_, x_, ALU.mult))
                        link(pool.tensor_tensor(total, total, one, ALU.add))
                pool.sem_inc(early_sum, 1)

            early_squares("peer")
            for t in range(TT):
                for ph, rows in enumerate(("peer_u", "peer_v")):
                    src = a[rows][0]
                    numbers = ids.bitcast(U32)
                    n = (t * 2 + ph) * SLOTS
                    if (t, ph) == (1, 0):
                        pool.wait_ge(sem("pe_rows"), (SLOTS // GATHERS + 1) * len(BY_PE))

                    with pool.Fori(0, PEER_HEADS) as h:
                        pool.wait_ge(sem("ids_ready"), h + (t * PEER_HEADS + 1))
                        for row in range(TOPK):
                            k = row % GATHERS
                            if (t, ph) == (0, 1) and k in BY_PE:
                                n_pe = (row // GATHERS) * len(BY_PE) + BY_PE.index(k)
                                pool.wait_ge(sem("pe_rows"), h * (2 * len(BY_PE)) + (n_pe + 1))
                            pool.wait_ge(sem("rows_used"), h * TOPK + (n + row + 1))
                            pool.sem_inc(sem("gather_turn"), 1)
                            pool.tensor_copy(idcol[:, k:k + 1].bitcast(U32),
                                             numbers[:, t, bass.ds(h * TOPK + row, 1)]).then_inc(sem("idcol_ready"), 1)
                            pool.wait_ge(sem("idcol_ready"), h * TOPK + (n + row + 1))
                            pool.sem_inc(sem("gather_turn"), 1)
                            pool.indirect_dma_start(
                                gath[:, k, :], None, src,
                                bass.IndirectOffsetOnAxis(ap=idcol[:, k:k + 1].bitcast(U32), axis=0)
                            ).then_inc(sem(f"rows_in{k}"), 16)
            for name in early:
                if name != "peer":
                    early_squares(name)

        @block.scalar
        def _(act):
            chain = [0]

            def link(ins):
                ins.then_inc(sem("act_chain"), 1)
                chain[0] += 1
                act.wait_ge(sem("act_chain"), chain[0])

            act.dma_start(x_in, a["x"][0].rearrange("(t p) d -> p t d", p=P)).then_inc(sem("x_in"), 16)
            for name, n in GAINS:
                src = a[name]
                if len(src.shape) > 1:
                    src = src.rearrange("a b c -> (a b c)" if len(src.shape) > 2 else "a b -> (a b)")
                act.dma_start(rows_in[GAIN_AT[name]:GAIN_AT[name] + n, :], src.rearrange("(r p) -> r p", p=P)).then_inc(sem("gains_in"), 16)
            for k, name in enumerate(("pe_k", "pe_v")):
                act.dma_start(pe_in[16 * k:16 * k + 16, :], a[name][0].rearrange("(l e) d -> l (e d)", e=2)).then_inc(sem("pe_in"), 16)
            act.dma_start(mem_in, a["mem"][0].rearrange("(t p) d -> p t d", p=P)).then_inc(sem("mem_in"), 16)
            act.dma_start(rel[0:BUCKETS, :], a["rel_bias"]).then_inc(sem("rel_in"), 16)
            act.dma_start(hot[0:BUCKETS, :], onehot).then_inc(sem("rel_in"), 16)
            for k, name in enumerate(("w_cmp_k", "w_cmp_v")):
                act.dma_start(w_cmp[:, k], a[name][0].rearrange("(l p) d -> p l d", p=P)).then_inc(sem("cmp_in"), 16)
            act.dma_start(w_grp, a["w_pool_grp"][0].rearrange("g c d -> c g d")).then_inc(sem("grp_in"), 16)

            def copy_out(dst, src):
                return act.activation(dst, src, ACT.Copy)

            def from_P(dst, cols=slice(0, 512), rows=slice(0, P), name="turned"):
                chP.take(act)
                copy_out(dst, psP[rows, cols]).then_inc(chP.free, 1)

            def quads(ap):
                return ap.rearrange("p (c t) -> p c t", c=4)

            def norm_root(name):
                n, src, dst, g, c = norms[name]
                if name in late:
                    act.wait_ge(src_ready, late.index(name) + 1)
                    act.activation(squares[:, 0:c * T].rearrange("p (c t) -> p c t", c=c)[:, :, P:T], src[:, 0:c, P:T],
                                   ACT.Square).then_inc(squared_s, 1)
                chP.take(act)
                if n > 0:
                    act.wait_ge(normed, n)
                act.activation(root[:, :], psP[:, 0:T], ACT.Sqrt, scale=1.0 / (P * c), bias=eps[:, 0:1]).then_inc(rooted, 1)
                act.wait_ge(rooted, n + 1)
                act.sem_inc(chP.free, 1)

            def empties(name, body):
                jb = by_name[name]

                def one(st):
                    act.wait_ge(multiplied, st.number + 1)
                    if st.per:
                        act.sem_inc(sem("act_turn"), 1)
                    body(st, bank[st.slot]).then_inc(emptied[st.slot], 1)
                panels_of(act, jb, one)

            def high_part(jb, st, free=True):
                par, n = halved(jb, st)
                act.wait_ge(landed[st.slot], st.uses * 16 + 16)
                if free:
                    act.wait_ge(multiplied, st.number - 1)
                copy_out(w_high[:, par, 0:n], ring[:, st.slot, 0:n]).then_inc(high, 1)

            def attention(key):
                base, us = unit_base[key]
                n = len(us)
                for s in range(n + 2):
                    if s >= 2:
                        gu, w = base + s - 2, us[s - 2]["width"]
                        if gu >= LAG:
                            act.wait_ge(chO.full, gu - LAG + 1)
                        chP.take(act)
                        copy_out(probT[:, gu % LAG, 0:w], psP[:, 0:w]).then_inc(chP.free, 1)
                        act.wait_ge(chP.free, chP.got)
                        act.sem_inc(probs_up, 1)
                    if s < n:
                        u, gu, w = us[s], base + s, us[s]["width"]
                        act.wait_ge(biased, gu + 1)
                        half = w - 2 * P
                        for t, (lo, hi) in enumerate(((0, half), (half, w))):
                            ins = act.activation(prob[:, gu % LAG, lo:hi], soft[:, gu % LAG, lo:hi], ACT.Exp,
                                                 bias=nmax[:, gu % LAG, t:t + 1], accum_out=sums[:, gu % LAG, t:t + 1])
                        ins.then_inc(exped, 1)

            act.wait_ge(sem("consts"), 1)

            def input_T(dst):
                for t in range(TT):
                    for h in range(2):
                        chP.take(act)
                        copy_out(dst[:, 4 * h:4 * h + 4, t * P:(t + 1) * P], quads(psP[:, :])).then_inc(chP.free, 1)
                act.wait_ge(chP.free, chP.got)
                act.sem_inc(sem("inputs_T"), 1)

            input_T(xT)
            norm_root("mix")
            from_P(gains[:, :], slice(0, N_GAINS))
            from_P(peT, slice(0, 32))
            act.wait_ge(chP.free, chP.got)
            act.sem_inc(sem("gains_T"), 1)
            input_T(memT)
            act.wait_ge(sem("consts"), 2)
            chP.take(act)
            copy_out(table[0:NSA_HEADS, 0:T], psP[0:NSA_HEADS, 0:T]).then_inc(chP.free, 1)
            act.wait_ge(chP.free, chP.got)
            row = table[0:NSA_HEADS, :]
            act.dma_start(toeplitz[:, :, :], bass.AP(row.tensor, row.offset, [list(row.ap[0]), [0, P], [1, 384]]))\
                .then_inc(sem("table_out"), 16)

            def kv_out(st, bk):
                j = st.j
                if j < 2:
                    dst = (tokk, tokv)[j]
                    for par in range(2):
                        src = bk[64 * par:64 * par + 64, :].rearrange("p (c t) -> p c t", c=2)
                        copy_out(dst[0:64, par::2, :], src)
                        ins = copy_out(dst[64:128, par::2, 0:T - 1], src[:, :, 1:T])
                    return ins
                dst = (kselT, vsel, kwinT, vwin)[j - 2]
                return copy_out(dst, bk[:, :].rearrange("p (c t) -> p c t", c=2))

            empties("kv", kv_out)
            act.wait_ge(sem("table_out"), 16)
            line = toeplitz[:, :, :]
            wide = bass.AP(line.tensor, P - 1, [[383, P], [P * 384, NSA_HEADS], [1, T]])
            corner = bass.AP(line.tensor, 2 * P - 1, [[383, P], [P * 384, NSA_HEADS], [1, P]])
            act.dma_start(bias[:, :, P:3 * P], wide).then_inc(sem("bias_in"), 16)
            act.dma_start(bias[:, :, 0:P], corner).then_inc(sem("bias_in"), 16)

            norm_root("mem")

            def q_out(st, bk):
                g = st.j
                for par in range(2):
                    ins = act.activation(
                        qT[64 * (g % 2):64 * (g % 2) + 64, (g // 2) * 4 + par:(g // 2) * 4 + 4:2, :],
                        bk[64 * par:64 * par + 64, :].rearrange("p (c t) -> p c t", c=2), ACT.Copy, scale=HEAD ** -0.5)
                return ins

            empties("q", q_out)
            empties("gate_nsa", lambda st, bk: act.activation(
                gate_nsa, bk[:, :].rearrange("p (t n) -> p t n", t=TT)[:, :, 0:48], ACT.Sigmoid))

            def pairs(dst):
                return lambda st, bk: copy_out(dst[:, 2 * st.j:2 * st.j + 2, :], bk[:, :].rearrange("p (c t) -> p c t", c=2))

            def tokens(dst):
                return lambda st, bk: copy_out(dst[:, :, 256 * st.j:256 * st.j + 256], bk[:, :].rearrange("p (t n) -> p t n", t=2))

            empties("qx", pairs(qxT))
            empties("pool", pairs(uT))
            empties("kx", pairs(kxT))
            empties("vx", tokens(vx))
            chP.take(act)
            for par in range(2):
                ins = copy_out(kcT[64 * par:64 * par + 64, :, :],
                               psP[0:64, 0:4 * N_CMP].rearrange("p (g c) -> p g c", g=4)[:, par::2, :])
            ins.then_inc(chP.free, 1)
            chP.take(act)
            copy_out(vc, psP[:, 0:HEAD]).then_inc(chP.free, 1)
            act.wait_ge(chP.free, chP.got)
            act.sem_inc(sem("kc_ready"), 1)
            act.wait_ge(sem("cmp_scores"), 1)
            act.activation(scmp, scmp, ACT.Exp).then_inc(sem("cmp_exp"), 1)
            for t in range(TT):
                chP.take(act)
                copy_out(pcmpT[:, t], quads(psP[:, :])).then_inc(chP.free, 1)
            act.wait_ge(chP.free, chP.got)
            act.sem_inc(sem("pcmp_T"), 1)
            attention("nsa")
            attention("x")

            def turn_back(dst, quarters):
                for t in range(TT):
                    for h in range(quarters):
                        chP.take(act)
                        copy_out(dst[:, 4 * h:4 * h + 4, t * P:(t + 1) * P], quads(psP[:, :])).then_inc(chP.free, 1)
                act.wait_ge(chP.free, chP.got)
                act.sem_inc(sem("turned"), 1)

            turn_back(oxT, 1)
            act.dma_start(sub_in, a["peer_sub_keys"][0].rearrange("h s k c -> k (h s) c")).then_inc(sem("sub_in"), 16)
            empties("merge", lambda st, bk: act.activation(
                merge[:, bass.ds(st.at(lambda j: 2 * j), 2), :], bk[:, :].rearrange("p (c t) -> p c t", c=2), ACT.Sigmoid))
            turn_back(nT, 2)
            norm_root("peer")
            for j in range(PEER_HEADS):
                st = Step(by_name["peer_q"].first, j, 0, False)
                act.wait_ge(multiplied, st.number + 1)
                copy_out(qpT[:, 2 * j:2 * j + 2, :], bank[st.slot][:, :].rearrange("p (c t) -> p c t", c=2))\
                    .then_inc(emptied[st.slot], 1)
                if j == 1:
                    for q in range(4):
                        chP.take(act)
                        copy_out(subT[:, 4 * q:4 * q + 4, :], quads(psP[:, :])).then_inc(chP.free, 1)
                    act.wait_ge(chP.free, chP.got)
                    act.sem_inc(sem("sub_T"), 1)
                if j == 2:
                    for t in range(TT):
                        for h in range(2):
                            chP.take(act)
                            copy_out(hrow[:, t, 512 * h:512 * h + 512], psP[:, :]).then_inc(chP.free, 1)
                    act.wait_ge(chP.free, chP.got)
                    act.sem_inc(sem("hrow_T"), 1)
            for t in range(TT):
                act.wait_ge(sem("best_ready"), t + 1)
                act.activation(gate[:, t], gate[:, t], ACT.Exp).then_inc(sem("gate_exp"), 1)
                act.wait_ge(sem("dots_ready"), t + 1)
                act.activation(wgt[:, t], dots[:, t], ACT.Gelu).then_inc(sem("gelu_done"), 1)
                if t == 0:
                    act.wait_ge(sem("weights"), 1)
                    with act.Fori(0, SLOTS // GATHERS) as i:
                        for n, k in enumerate(BY_PE):
                            act.wait_ge(sem("pe_rows"), i * len(BY_PE) + (n + 1))
                            act.sem_inc(sem("act_turn"), 1)
                            copy_out(wcol[:, n:n + 1], wgt[:, 0, bass.ds(i * GATHERS + k, 1)]).then_inc(sem("wcol_ready"), 1)
                            act.wait_ge(sem("wcol_ready"), i * len(BY_PE) + (n + 1))
                            act.activation(diag[:, n, :], ident[:, :], ACT.Copy, scale=wcol[:, n:n + 1])\
                                .then_inc(sem("diagonal"), 1)
            norm_root("first")
            act.wait_ge(normed, norms["first"][0] + 1)
            for i in L:
                act.dma_start(p_in[:, i], a["p_2"][i, 0].rearrange("(t p) d -> p t d", p=P)).then_inc(sem("p_in"), 16)
            act.dma_start(posi[0:ROPE, :].bitcast(I32), over_partitions(a["positions_2"], ROPE)).then_inc(sem("pos_in"), 16)
            act.dma_start(freq[0:ROPE, :], inv_freq).then_inc(sem("pos_in"), 16)
            act.dma_start(fbias, over_partitions(a["fox_b_f_2"], P)).then_inc(sem("pos_in"), 16)

            ffn_pairs = [0]

            def first_high(i, s_):
                jb = by_name[f"ffn_in{i}{s_}"]
                for j in range(2):
                    high_part(jb, Step(jb.first, j, 0, False), free=False)

            def norm_high(name):
                for q in range(PAIRS):
                    act.wait_ge(norm_pair, PAIRS * whole[name] + q + 1)
                    copy_out(n_high[:, 2 * q:2 * q + 2, :], nT[:, 2 * q:2 * q + 2, :]).then_inc(sem("n_high"), 1)

            def ffn_gates(i, s_):
                jb, jo = by_name[f"ffn_in{i}{s_}"], by_name[f"ffn_out{i}{s_}"]
                k0 = ffn_pairs[0]
                ffn_pairs[0] += FC // 2
                h0 = (2 * i + s_) * (FC // 2)

                def ahead(st):
                    if not st.per and st.j + 2 >= jb.panels:
                        high_part(jo, Step(jo.first, st.j + 2 - jb.panels, 0, False))
                    else:
                        high_part(jb, after(st, 2))

                def one(st):
                    pair = k0 + (st.j // 2) + (st.turn * 2 if st.per else 0)
                    if st.j % 2 == 0:
                        act.wait_ge(sem("sgate_free"), pair + 1)
                        if st.per:
                            act.sem_inc(sem("act_turn"), 1)
                        act.wait_ge(multiplied, st.number + 1)
                        act.activation(sgate[:, (st.j // 2 + k0) % 2, :], bank[st.slot][:, :], ACT.Silu)\
                            .then_inc(emptied[st.slot], 1)
                        ahead(st)
                    else:
                        ahead(st)
                        act.wait_ge(sem("hidden_pair"), h0 + st.j // 2 + 1 + (st.turn * 2 if st.per else 0))
                        if st.per:
                            act.sem_inc(sem("act_turn"), 1)
                        at_ = st.at(lambda j: 2 * (j // 2))
                        dst = h_high[:, bass.ds(at_, 2), :] if st.per else h_high[:, at_:at_ + 2, :]
                        copy_out(dst, sgate[:, (st.j // 2 + k0) % 2, :].rearrange("p (c t) -> p c t", c=2))\
                            .then_inc(sem("h_high"), 1)
                panels_of(act, jb, one, ahead=2)
                for j in range(DC - 2):
                    high_part(jo, Step(jo.first, j + 2, 0, False))

            first_high(0, 0)
            norm_root("ffn00")
            norm_high("ffn00")
            ffn_gates(0, 0)
            norm_root("mix0")
            act.wait_ge(sem("angles"), 1)
            act.activation(cosT[0:ROPE, :], ang[0:ROPE, 0, :], ACT.Sin, scale=0.5).then_inc(sem("sines"), 1)
            act.activation(sinT[0:ROPE, :], ang[0:ROPE, 0, :], ACT.Sin).then_inc(sem("sines"), 1)
            norm_root("cq")
            norm_root("ckv")

            def swap(src):
                copy_out(rope_sw[0:32, :], src[32:64, :])
                return copy_out(rope_sw[32:64, :], src[0:32, :])

            act.wait_ge(sem("rope_go"), 1)
            swap(krT).then_inc(sem("swapped"), 1)

            def uq_out(st, bk):
                h = st.j
                act.wait_ge(sem("rope_go"), h + 2)
                copy_out(q2T[:, h, :], bk[:, 0:T])
                copy_out(rope_in[0:ROPE, :], bk[0:ROPE, T:2 * T])
                return swap(bk[:, T:2 * T])

            for h in range(MLA_HEADS):
                st = Step(by_name["uq"].first, h, 0, False)
                act.wait_ge(multiplied, st.number + 1)
                uq_out(st, bank[st.slot]).then_inc(emptied[st.slot], 1)
            for h in range(MLA_HEADS):
                st = Step(by_name["ukv"].first, h, 0, False)
                act.wait_ge(multiplied, st.number + 1)
                copy_out(k2T[:, h, :], bank[st.slot][:, 0:T])
                copy_out(v2[:, :, h * P:(h + 1) * P], bank[st.slot][:, T:2 * T].rearrange("p (t n) -> p t n", t=2))\
                    .then_inc(emptied[st.slot], 1)
            attention("mla")
            turn_back(nT, 2)
            first_high(0, 1)
            norm_root("ffn01")
            norm_high("ffn01")
            ffn_gates(0, 1)
            for i in L:
                chP.take(act)
                copy_out(pT[:, i].rearrange("p c t -> p (c t)"), psP[:, :]).then_inc(chP.free, 1)
            act.wait_ge(chP.free, chP.got)
            act.sem_inc(sem("p_T"), 1)

            def ple_gates(name):
                jb = by_name[name]
                k0 = ffn_pairs[0]
                ffn_pairs[0] += 4

                def one(st):
                    if st.j % 2:
                        return
                    pair = k0 + (st.j // 2) + (st.turn * 2 if st.per else 0)
                    act.wait_ge(sem("sgate_free"), pair + 1)
                    if st.per:
                        act.sem_inc(sem("act_turn"), 1)
                    act.wait_ge(multiplied, st.number + 1)
                    act.activation(sgate[:, (st.j // 2 + k0) % 2, :], bank[st.slot][:, :], ACT.Sigmoid)\
                        .then_inc(emptied[st.slot], 1)
                panels_of(act, jb, one)

            norm_root("ple0")
            ple_gates("ple0")
            first_high(1, 0)
            norm_root("ffn10")
            norm_high("ffn10")
            ffn_gates(1, 0)
            norm_root("mix1")
            empties("fq", pairs(q2T))
            empties("fk", pairs(k2T))
            empties("fv", tokens(v2))
            act.wait_ge(sem("forget"), 1)
            act.activation(ftmp[:, 1], ftmp[:, 1], ACT.Exp, scale=-1.0).then_inc(sem("fexp"), 1)
            act.wait_ge(sem("forget"), 2)
            act.activation(ftmp[:, 2], ftmp[:, 2], ACT.Ln).then_inc(sem("fexp"), 1)
            attention("fox")
            turn_back(nT, 2)
            first_high(1, 1)
            norm_root("ffn11")
            norm_high("ffn11")
            ffn_gates(1, 1)
            norm_root("ple1")
            ple_gates("ple1")
            norm_root("final")
            for t in range(TT):
                for h in range(2):
                    chP.take(act)
                    copy_out(xrow[:, t, 512 * h:512 * h + 512], psP[:, :]).then_inc(sem("out_rows"), 1)
                    act.wait_ge(sem("out_rows"), 2 * t + h + 1)
                    act.sem_inc(chP.free, 1)

        @block.tensor
        def _(pe):
            def products(name, ready=None, only=None, pairs_ready=None):
                jb = by_name[name]
                if ready is not None:
                    pe.wait_ge(*ready)

                def one(st):
                    if jb.split:
                        pe.wait_ge(low, split_no(jb, st) + 1)
                    else:
                        pe.wait_ge(landed[st.slot], st.uses * 16 + 16)
                    if not (isinstance(st.uses, int) and st.uses == 0):
                        pe.wait_ge(emptied[st.slot], st.uses)
                    c, w, act_ = jb.rows(st.j), jb.width, jb.act(st.j)
                    if jb.split:
                        par, n = halved(jb, st)
                        wh, wl = (x[:, par, 0:n].rearrange("p (c n) -> p c n", c=c) for x in (w_high, w_low))
                        ah, al = jb.split
                        for m in range(0, w, P):
                            dst = bank[st.slot][:, (m // P) * T:(m // P) * T + T]
                            for k in range(c):
                                if pairs_ready and st.j == 0 and m == 0 and k % 2 == 0:
                                    pe.wait_ge(pairs_ready[0], pairs_ready[1] + k // 2 + 1)
                                for n_, (x, y) in enumerate(((wh, al), (wl, ah), (wh, ah))):
                                    mm = pe.matmul(dst, x[:, k, m:m + P], y[:, k, :], start=(k == 0 and n_ == 0),
                                                   stop=(k == c - 1 and n_ == 2))
                        mm.then_inc(multiplied, 1)
                        return
                    wt = ring[:, st.slot, 0:c * w].rearrange("p (c n) -> p c n", c=c)
                    kind = jb.kind(st.j) if callable(jb.kind) else jb.kind
                    bk = bank[st.slot]
                    groups = []
                    if kind == "F":
                        for m in range(0, w, P):
                            mw = min(P, w - m)
                            o = (m // P) * T
                            groups.append((bk[0:mw, o:o + T], lambda k, m=m, mw=mw: (wt[:, k, m:m + mw], act_[:, k, :])))
                    else:
                        lo = 0
                        if kind == "FT":
                            groups.append((bk[:, 0:T], lambda k: (wt[:, k, 0:P], act_[:, k, :])))
                            lo = P
                        for t in range(TT):
                            o = T + t * P if kind == "FT" else t * T
                            groups.append((bk[:, o:o + w - lo],
                                           lambda k, t=t, lo=lo: (act_[:, k, t * P:(t + 1) * P], wt[:, k, lo:w])))
                    for n_, (dst, ops) in enumerate(groups):
                        for k in range(c):
                            if pairs_ready and st.j == 0 and n_ == 0 and k % 2 == 0:
                                pe.wait_ge(pairs_ready[0], pairs_ready[1] + k // 2 + 1)
                            lhs, rhs = ops(k)
                            mm = pe.matmul(dst, lhs, rhs, start=(k == 0), stop=(k == c - 1))
                    mm.then_inc(multiplied, 1)
                if only is None:
                    panels_of(pe, jb, one)
                else:
                    for j in only:
                        one(Step(jb.first, j, 0, False))

            def all_left(name):
                last = by_name[name].first + by_name[name].panels
                for k in range(RING):
                    pe.wait_ge(emptied[k], (last - 1 - k) // RING + 1)

            def turn(pieces):
                chP.claim(pe)
                for o, src in pieces:
                    n, m = src.shape[0], src.shape[1]
                    mm = pe.transpose(psP[0:m, o:o + n], src, ident[0:n, 0:n])
                mm.then_inc(chP.full, 1)

            def norm_sum(name):
                n, src, dst, g, c = norms[name]
                if name in late:
                    pe.wait_ge(squared_v, n + 1)
                    pe.wait_ge(squared_s, late.index(name) + 1)
                    chP.claim(pe)
                    for k in range(c):
                        mm = pe.matmul(psP[:, 0:T], ones[:, :], squares[:, k * T:(k + 1) * T], start=(k == 0), stop=(k == c - 1))
                else:
                    e, after_job, width = early[name]
                    pe.wait_ge(early_sum, e + 1)
                    chP.claim(pe)
                    for k in range(width):
                        pe.matmul(psP[:, 0:T], ones[:, :], squares[:, k * T:(k + 1) * T], start=(k == 0), stop=False)
                    pe.wait_ge(squared_v, n + 1)
                    for k in range(width):
                        mm = pe.matmul(psP[:, 0:T], ones[:, :], squares[:, 1024 + k * T:1024 + (k + 1) * T], start=False,
                                       stop=(k == width - 1))
                mm.then_inc(chP.full, 1)

            def attention(key):
                base, us = unit_base[key]
                n = len(us)
                for s in range(n + LAG):
                    if s < n:
                        u = us[s]
                        ps = psS[chS.claim(pe)]
                        half = u["width"] - T
                        for t, (lo, hi) in enumerate(((0, half), (half, u["width"]))):
                            for k, (ql, kr) in enumerate(zip(u["lhs"], u["rhs"])):
                                mm = pe.matmul(ps[:, lo:hi], ql[:, t * P:(t + 1) * P], kr[:, 0:hi - lo],
                                               start=(k == 0), stop=(k == len(u["lhs"]) - 1))
                        mm.then_inc(chS.full, 1)
                    if 2 <= s < n + 2:
                        gu, w = base + s - 2, us[s - 2]["width"]
                        pe.wait_ge(exped, gu + 1)
                        turn([(o, prob[:, gu % LAG, o:o + P]) for o in range(0, w, P)])
                    if s >= LAG:
                        gu, u = base + s - LAG, us[s - LAG]
                        pe.wait_ge(probs_up, gu + 1)
                        lo = chO.claim(pe) * T
                        dv = u["v"][0].shape[1]
                        for t, pieces in SEGS[u["width"]]:
                            for k, (c, kt) in enumerate(pieces):
                                mm = pe.matmul(psO[:, lo + t * dv:lo + (t + 1) * dv], probT[:, gu % LAG, c * P:(c + 1) * P],
                                               u["v"][kt], start=(k == 0), stop=(k == len(pieces) - 1))
                        mm.then_inc(chO.full, 1)

            def rows_to_T(src, blocks):
                for t in range(TT):
                    for q in range(blocks // 4):
                        turn([(j * P, src[:, t, (4 * q + j) * P:(4 * q + j + 1) * P]) for j in range(4)])

            pe.wait_ge(sem("consts"), 1)
            pe.wait_ge(sem("x_in"), 16)
            rows_to_T(x_in, 8)
            norm_sum("mix")
            pe.wait_ge(sem("gains_in"), 16 * len(GAINS))
            turn([(0, rows_in[0:N_GAINS, :])])
            pe.wait_ge(sem("pe_in"), 32)
            turn([(0, pe_in[0:32, :])])
            pe.wait_ge(sem("mem_in"), 16)
            rows_to_T(mem_in, 8)
            pe.wait_ge(sem("rel_in"), 32)
            chP.claim(pe)
            pe.matmul(psP[0:NSA_HEADS, 0:T], rel[0:BUCKETS, :], hot[0:BUCKETS, :], start=True, stop=True).then_inc(chP.full, 1)
            products("kv", pairs_ready=(norm_pair, PAIRS * whole["mix"]))
            norm_sum("mem")
            products("q")
            products("gate_nsa")
            products("qx")
            products("pool")
            products("kx", (normed, norms["mem"][0] + 1))
            products("vx")
            pe.wait_ge(sem("consts"), 2)
            pe.wait_ge(sem("blocks"), 2)
            pe.wait_ge(sem("cmp_in"), 32)
            chP.claim(pe)
            for l in range(LP):
                mm = pe.matmul(psP[0:HEAD, 0:4 * N_CMP], w_cmp[:, 0, l, :], blkk[:, l, :, 0:N_CMP], start=(l == 0), stop=(l == LP - 1))
            mm.then_inc(chP.full, 1)
            chP.claim(pe)
            for l in range(LP):
                mm = pe.matmul(psP[:, 0:HEAD], blkv[:, l].rearrange("p g c -> p (g c)"), w_cmp[:, 1, l, :],
                               start=(l == 0), stop=(l == LP - 1))
            mm.then_inc(chP.full, 1)
            pe.wait_ge(sem("kc_ready"), 1)
            all_left("vx")
            for par in range(2):
                ps = psS[chS.claim(pe)]
                lo = HEAD * par
                for t in range(TT):
                    for g in (par, par + 2):
                        for r in range(HEADS_PER_GROUP):
                            o = (t * NSA_HEADS + g * HEADS_PER_GROUP + r) * 16
                            mm = pe.matmul(ps[:, o:o + N_CMP], qT[lo:lo + HEAD, (g // 2) * 4 + r, t * P:(t + 1) * P],
                                           kcT[lo:lo + HEAD, g // 2, :], start=True, stop=True)
                mm.then_inc(chS.full, 1)
            pe.wait_ge(sem("cmp_probs"), 1)
            for t in range(TT):
                turn([(r * P, pcmp[:, t, r].rearrange("p g c -> p (g c)")) for r in range(4)])
            pe.wait_ge(sem("pcmp_T"), 1)
            for g in range(NSA_GROUPS):
                ps = psS[chS.claim(pe)]
                lo = CMP_SLOT * g
                for t in range(TT):
                    for r in range(HEADS_PER_GROUP):
                        o = t * T + r * HEAD
                        mm = pe.matmul(ps[:, o:o + HEAD], pcmpT[lo:lo + N_CMP, t, r, :], vc[lo:lo + N_CMP, :],
                                       start=True, stop=True)
                mm.then_inc(chS.full, 1)
            pe.wait_ge(sem("pooled"), 1)
            pe.wait_ge(sem("grp_in"), 16)
            for half in range(2):
                ps = psS[chS.claim(pe)]
                for g in (2 * half, 2 * half + 1):
                    mm = pe.matmul(ps[:, (g % 2) * T:(g % 2 + 1) * T], w_grp[:, g, :], uT[:, g, :], start=True, stop=True)
                mm.then_inc(chS.full, 1)
            pe.wait_ge(sem("bias_in"), 32)
            attention("nsa")
            attention("x")
            pe.wait_ge(sem("attended"), 1)
            rows_to_T(o_x, 4)
            products("merge")
            rows_to_T(o_nsa, 8)
            products("pool_out", (sem("mixed"), 1))
            products("x_out", (sem("turned"), 1))
            products("nsa_out", (sem("turned"), 2))
            products("w_o", (sem("merged"), 1))
            norm_sum("peer")
            q_first = by_name["peer_q"].first

            def key_scores(t, pair):
                ps = psS[chS.claim(pe)]
                for j in range(4):
                    c = 4 * pair + j
                    mm = pe.matmul(ps[:, j * P:(j + 1) * P], qpT[:, c, t * P:(t + 1) * P], subT[:, c, :], start=True, stop=True)
                mm.then_inc(chS.full, 1)

            def queries_left(pair):
                for n in (q_first + 2 * pair, q_first + 2 * pair + 1):
                    pe.wait_ge(emptied[n % RING], n // RING + 1)

            products("peer_q", None, range(2), (norm_pair, PAIRS * whole["peer"]))
            pe.wait_ge(sem("sub_in"), 16)
            for q in range(4):
                turn([(j * P, sub_in[:, 4 * q + j, :]) for j in range(4)])
            products("peer_q", None, range(2, 3))
            pe.wait_ge(sem("sub_T"), 1)
            queries_left(0)
            key_scores(0, 0)
            for t in range(TT):
                for q in range(2):
                    turn([(j * P, nT[:, 4 * q + j, t * P:(t + 1) * P]) for j in range(4)])
            products("peer_q", None, range(3, 6))
            queries_left(1)
            key_scores(0, 1)
            products("peer_q", None, range(6, 8))
            for t, pair in ((0, 2), (0, 3), (1, 0), (1, 1)):
                if t == 0:
                    queries_left(pair)
                key_scores(t, pair)
            pe.sem_inc(sem("pe_rows"), len(BY_PE))

            def row_sum(lhs, rhs, start, stop):
                for q in range(2):
                    mm = pe.matmul(bank[q][:, :], lhs, rhs[:, 512 * q:512 * q + 512] if rhs.shape[-1] > 512 else rhs,
                                   start=start, stop=stop)
                return mm

            row_sum(zeros[:, 0:P], zeros[:, :], True, False)
            ROUNDS = SLOTS // GATHERS
            for pair in range(PEER_HEADS // 2):
                done = pair * ROUNDS // 4
                with pe.Fori(0, ROUNDS // 4) as i:
                    for n, k in enumerate(BY_PE):
                        pe.wait_ge(sem(f"rows_in{k}"), i * 16 + 16 * (ROUNDS + done + 1))
                        pe.wait_ge(sem("diagonal"), i * len(BY_PE) + (done * len(BY_PE) + n + 1))
                        row_sum(diag[:, n, :], gath[:, k, :], False, False).then_inc(sem("pe_rows"), 1)
                if pair < 2:
                    key_scores(1, pair + 2)
            row_sum(zeros[:, 0:P], zeros[:, :], False, True).then_inc(sem("pe_sum"), 1)
            for t in range(TT):
                pe.wait_ge(sem("experts_done"), t + 1)
                for q in range(2):
                    ps = psS[chS.claim(pe)]
                    for j in range(4):
                        mm = pe.transpose(ps[:, j * P:(j + 1) * P], yacc[:, t, (4 * q + j) * P:(4 * q + j + 1) * P], ident[:, :])
                    mm.then_inc(chS.full, 1)
            norm_sum("first")

            def ffn(i, s):
                n = f"ffn{i}{s}"
                norm_sum(n)
                products(f"ffn_in{i}{s}", pairs_ready=(sem("n_low"), PAIRS * (2 * i + s)))
                products(f"ffn_out{i}{s}", pairs_ready=(sem("h_low"), (2 * i + s) * (FC // 2)))

            ffn(0, 0)
            norm_sum("mix0")
            products("cq", pairs_ready=(norm_pair, PAIRS * whole["mix0"]))
            products("ckv")
            norm_sum("cq")
            norm_sum("ckv")
            products("uq", (normed, norms["cq"][0] + 1))
            products("ukv", (normed, norms["ckv"][0] + 1))

            all_left("ukv")
            pe.wait_ge(sem("rope_go"), 2 + MLA_HEADS)
            attention("mla")
            pe.wait_ge(sem("attended"), 2)
            rows_to_T(o2, 8)
            products("mla_o", (sem("turned"), 3))
            ffn(0, 1)
            pe.wait_ge(sem("p_in"), 32)
            for i in L:
                turn([(c * T + t * P, p_in[:, i, t, c * P:(c + 1) * P]) for c in range(2) for t in range(TT)])
            norm_sum("ple0")
            pe.wait_ge(sem("p_T"), 1)
            products("ple0", pairs_ready=(norm_pair, PAIRS * whole["ple0"]))
            ffn(1, 0)
            norm_sum("mix1")
            products("fq", pairs_ready=(norm_pair, PAIRS * whole["mix1"]))
            products("fk")
            products("fv")
            products("ff")
            pe.wait_ge(sem("forget"), 3)
            ps = psS[chS.claim(pe)]
            for t in range(TT):
                for j in range(t + 1):
                    mm = pe.matmul(ps[:, t * FOX_HEADS:(t + 1) * FOX_HEADS], tri[:, j, t * P:(t + 1) * P], logf[:, j, :],
                                   start=(j == 0), stop=(j == t))
            mm.then_inc(chS.full, 1)
            pe.wait_ge(sem("forget"), 4)
            for h2 in range(FOX_HEADS // 2):
                ps = psS[chS.claim(pe)]
                for j in range(2):
                    h = 2 * h2 + j
                    for t in range(TT):
                        mm = pe.matmul(ps[:, j * T:(j + 1) * T], logf_wide[:, t, h * P:(h + 1) * P], tri[:, t, :],
                                       start=(t == 0), stop=(t == TT - 1))
                mm.then_inc(chS.full, 1)
            all_left("ff")
            attention("fox")
            pe.wait_ge(sem("attended"), 3)
            rows_to_T(o2, 8)
            products("fox_o", (sem("turned"), 4))
            ffn(1, 1)
            norm_sum("ple1")
            products("ple1", pairs_ready=(norm_pair, PAIRS * whole["ple1"]))
            norm_sum("final")
            pe.wait_ge(normed, norms["final"][0] + 1)
            for t in range(TT):
                for q in range(2):
                    turn([(j * P, xT[:, 4 * q + j, t * P:(t + 1) * P]) for j in range(4)])

        @block.vector
        def _(dve):
            chain = [0]

            def link(ins):
                ins.then_inc(sem("dve_chain"), 1)
                chain[0] += 1
                dve.wait_ge(sem("dve_chain"), chain[0])

            def tt(o, x, y, op):
                return dve.tensor_tensor(o, x, y, op)

            def ts(o, x, s1, op0, s2=None, op1=None):
                return dve.tensor_scalar(o, x, s1, s2, op0, op1) if op1 is not None else dve.tensor_scalar(o, x, s1, None, op0)

            def stt(o, x, s, y, op0, op1):
                return dve.scalar_tensor_tensor(out=o, in0=x, scalar=s, in1=y, op0=op0, op1=op1)

            def ready(name):
                dve.sem_inc(src_ready, 1)

            def do_norm(name):
                n, src, dst, g, c = norms[name]
                sq = squares[:, 0:c * T].rearrange("p (c t) -> p c t", c=c)
                if name in late:
                    dve.sem_inc(src_ready, 1)
                    tt(sq[:, :, 0:P], src[:, 0:c, 0:P], src[:, 0:c, 0:P], ALU.mult).then_inc(squared_v, 1)
                else:
                    width = early[name][2]
                    x_ = src[:, c - width:c, :]
                    tt(squares[:, 1024:1024 + width * T].rearrange("p (c t) -> p c t", c=width), x_, x_, ALU.mult)\
                        .then_inc(squared_v, 1)
                dve.wait_ge(rooted, n + 1)
                link(dve.reciprocal(rstd[:, :], root[:, :]))
                if name == "mix":
                    dve.wait_ge(sem("gains_T"), 1)

                def low_half(q):
                    lows[0] += 1
                    dve.wait_ge(sem("n_high"), lows[0])
                    h_ = slice(2 * q, 2 * q + 2)
                    tt(n_low[:, h_, :], nT[:, h_, :], n_high[:, h_, :].bitcast(F32), ALU.subtract).then_inc(sem("n_low"), 1)

                for k in range(c):
                    ins = stt(dst[:, k, :], src[:, k, :], gains[:, g + k:g + k + 1], rstd[:, :], ALU.mult, ALU.mult)
                    if name == "first" and k < c - 1:
                        ins.then_inc(sem("first_chunk"), 1)
                    elif c == DC and k % 2 and k < c - 1:
                        ins.then_inc(norm_pair, 1)
                    if name.startswith("ffn") and k % 2 and k > 1:
                        low_half(k // 2 - 1)
                ins.then_inc(normed, 1)
                dve.wait_ge(normed, n + 1)
                if c == DC:
                    dve.sem_inc(norm_pair, PAIRS if name == "first" else 1)
                if name.startswith("ffn"):
                    low_half(PAIRS - 1)

            lows = [0]

            def low_part(jb, st):
                par, n = halved(jb, st)
                dve.wait_ge(high, split_no(jb, st) + 1)
                tt(w_low[:, par, 0:n], ring[:, st.slot, 0:n], w_high[:, par, 0:n].bitcast(F32), ALU.subtract).then_inc(low, 1)

            def first_low(i, s_):
                jb = by_name[f"ffn_in{i}{s_}"]
                for j in range(2):
                    low_part(jb, Step(jb.first, j, 0, False))

            def empties(name, body, before_last=None):
                jb = by_name[name]

                def one(st):
                    if before_last is not None and st.j == jb.panels - 1:
                        before_last()
                    dve.wait_ge(multiplied, st.number + 1)
                    body(st, bank[st.slot]).then_inc(emptied[st.slot], 1)
                panels_of(dve, jb, one)

            def settle(name):
                last = by_name[name].first + by_name[name].panels
                for k in range(RING):
                    dve.wait_ge(emptied[k], (last - 1 - k) // RING + 1)

            def halves(ap):
                return ap.rearrange("p (c t) -> p c t", c=2)

            def attention(key):
                base, us = unit_base[key]
                n = len(us)
                for s in range(n + LAG):
                    if s >= LAG:
                        gu, u = base + s - LAG, us[s - LAG]
                        sl = gu % LAG
                        dve.wait_ge(exped, gu + 1)
                        link(dve.reciprocal(inv[:, sl, :], sums[:, sl, :]))
                        scal = inv
                        if u["kind"] == "gated":
                            link(tt(coef[:, sl, :], inv[:, sl, :], u["extra"], ALU.mult))
                            scal = coef
                    if s < n:
                        v, gv, w = us[s], base + s, us[s]["width"]
                        sl = gv % LAG
                        ps = psS[chS.take(dve)]
                        stt(soft[:, sl, 0:w], ps[:, 0:w], v["scale"], v["mask"][:, 0:w], ALU.mult, ALU.add).then_inc(chS.free, 1)
                        dve.wait_ge(chS.free, chS.got)
                        half = w - T
                        segs = ((0, half), (half, w))
                        if v["kind"] == "fox":
                            for t, (lo, hi) in enumerate(segs):
                                ins = stt(soft[:, sl, lo:hi], soft[:, sl, lo:hi], v["extra"][:, t:t + 1], causal[:, lo:hi],
                                          ALU.add, ALU.add)
                            link(ins)
                        for t, (lo, hi) in enumerate(segs):
                            ins = dve.tensor_reduce(nmax[:, sl, t:t + 1], soft[:, sl, lo:hi], AX_X, ALU.max, negate=True)
                        ins.then_inc(biased, 1)
                    if s >= LAG:
                        sl = gu % LAG
                        lo = chO.take(dve) * T
                        dv = u["v"][0].shape[1]
                        for t in range(TT):
                            src = psO[:, lo + t * dv:lo + (t + 1) * dv]
                            if u["kind"] == "gated":
                                ins = stt(u["outs"][t], src, scal[:, sl, t:t + 1], u["outs"][t], ALU.mult, ALU.add)
                            else:
                                ins = ts(u["outs"][t], src, scal[:, sl, t:t + 1], ALU.mult)
                        ins.then_inc(chO.free, 1)
                dve.wait_ge(chO.free, chO.got)

            link(dve.memset(rstd[:, 0:1], 0.0))
            dve.sem_inc(sem("sgate_free"), 2)
            dve.sem_inc(sem("rows_used"), GATHERS)
            dve.wait_ge(sem("inputs_T"), 1)
            do_norm("mix")

            dve.wait_ge(multiplied, 1)
            for k, (tok_, blk) in enumerate(((tokk, blkk), (tokv, blkv))):
                dve.wait_ge(emptied[k], 1)
                if k == 0:
                    dve.wait_ge(sem("consts"), 2)
                for g in range(NSA_GROUPS):
                    src = tok_[:, g, :]
                    win = bass.AP(src.tensor, src.offset, [list(src.ap[0]), [2, LP], [CMP_STRIDE, N_CMP]])
                    pe_ = peT[:, 16 * k:16 * k + 16]
                    peb = bass.AP(pe_.tensor, pe_.offset, [list(pe_.ap[0]), [1, LP], [0, N_CMP]])
                    ins = tt(blk[:, :, g, 0:N_CMP], win, peb, ALU.add)
                ins.then_inc(sem("blocks"), 1)

            dve.wait_ge(sem("inputs_T"), 2)
            do_norm("mem")

            last = by_name["pool"]
            dve.wait_ge(emptied[(last.first) % RING], last.first // RING + 1)
            dve.wait_ge(emptied[(last.first + 1) % RING], (last.first + 1) // RING + 1)
            link(dve.reciprocal(icount, icount))
            for g, win in enumerate((2, 4, 8, 16)):
                src, step = uT[:, g, :], 1
                bufs = (mixT[:, 0, :], mixT[:, 1, :])
                n = 0
                while step < win:
                    dst = bufs[n % 2]
                    tt(dst[:, step:T], src[:, step:T], src[:, 0:T - step], ALU.add)
                    link(dve.tensor_copy(dst[:, 0:step], src[:, 0:step]))
                    src, step, n = dst, 2 * step, n + 1
                link(tt(mixT[:, 2, 0:win], src[:, 0:win], icount[:, 0:win], ALU.mult))
                tt(uT[:, g, 0:win], mixT[:, 2, 0:win], uT[:, g, 0:win], ALU.subtract)
                link(stt(uT[:, g, win:T], src[:, win:T], 1.0 / win, uT[:, g, win:T], ALU.mult, ALU.subtract))
            dve.sem_inc(sem("pooled"), 1)

            dve.wait_ge(sem("bias_in"), 32)
            b = bcmp.rearrange("p (t h) c -> p t h c", t=TT)
            dve.tensor_copy(b[:, 0, :, 0:7], bias[:, :, CMP_LEN - 1:P:CMP_STRIDE])
            link(dve.tensor_copy(b[:, 1, :, 0:N_CMP], bias[:, :, P + CMP_LEN - 1:3 * P:CMP_STRIDE]))
            for par in range(2):
                def mine(ap, c):
                    return ap.rearrange("p (n e r) c -> p n e r c", e=2, r=4)[:, :, par, :, 0:c]
                ps = psS[chS.take(dve)]
                tt(mine(scmp, N_CMP), mine(ps[:, :].rearrange("p (n c) -> p n c", c=16), N_CMP), mine(bcmp, N_CMP),
                   ALU.add).then_inc(chS.free, 1)
            dve.wait_ge(chS.free, chS.got)
            link(dve.tensor_reduce(cstat[:, 0], scmp, AX_X, ALU.max))

            def over_c(ap):
                return bass.AP(ap.tensor, ap.offset, [list(ap.ap[0]), [1, 32], [0, N_CMP]])

            tt(scmp, scmp, over_c(cstat[:, 0]), ALU.subtract).then_inc(sem("cmp_scores"), 1)
            dve.wait_ge(sem("cmp_exp"), 1)
            link(dve.tensor_reduce(cstat[:, 1], scmp, AX_X, ALU.add))
            link(dve.reciprocal(cstat[:, 2], cstat[:, 1]))
            c2 = cstat[:, 2].rearrange("p (t h) -> p t h", t=TT)
            c3 = cstat[:, 3].rearrange("p (t h) -> p t h", t=TT)
            g_last = by_name["gate_nsa"].first
            dve.wait_ge(emptied[g_last % RING], g_last // RING + 1)
            link(tt(c3, c2, gate_nsa[:, :, 0:NSA_HEADS], ALU.mult))
            link(ts(c3[:, 0], c3[:, 0], has[:, 0:1], ALU.mult))
            link(tt(scmp, scmp, over_c(cstat[:, 3]), ALU.mult))
            s5 = scmp.rearrange("p (t g r) c -> p t g r c", t=TT, g=4)
            for t in range(TT):
                for r in range(4):
                    ins = dve.tensor_copy(pcmp[:, t, r, :, 0:N_CMP], s5[:, t, :, r, :])
            ins.then_inc(sem("cmp_probs"), 1)
            for g in range(NSA_GROUPS):
                ps = psS[chS.take(dve)]
                dve.tensor_copy(o_nsa[:, :, 256 * g:256 * g + 256], halves(ps[:, :])).then_inc(chS.free, 1)
            for half in range(2):
                ps = psS[chS.take(dve)]
                for g in (2 * half, 2 * half + 1):
                    at_ = GAIN_AT["pool_scale"] + g
                    ins = ts(mixT[:, g, :], ps[:, (g % 2) * T:(g % 2 + 1) * T], gains[:, at_:at_ + 1], ALU.mult)
                ins.then_inc(chS.free, 1)
            dve.wait_ge(chS.free, chS.got)
            dve.sem_inc(sem("mixed"), 1)
            attention("nsa")
            attention("x")
            dve.sem_inc(sem("attended"), 1)

            def by_gate(branch):
                def body(st, bk):
                    return tt(merge[:, 8 * branch + 2 * st.j:8 * branch + 2 * st.j + 2, :], halves(bk[:, :]),
                              merge[:, 8 * branch + 2 * st.j:8 * branch + 2 * st.j + 2, :], ALU.mult)
                return body

            m_last = by_name["merge"].first + 11
            for k in range(RING):
                dve.wait_ge(emptied[k], (m_last - k) // RING + 1)
            empties("pool_out", by_gate(0))
            empties("x_out", by_gate(2))
            settle("x_out")
            tt(merge[:, 0:8, :], merge[:, 0:8, :], merge[:, 16:24, :], ALU.add)
            empties("nsa_out", by_gate(1))
            settle("nsa_out")
            tt(merge[:, 0:8, :], merge[:, 0:8, :], merge[:, 8:16, :], ALU.add).then_inc(sem("merged"), 1)

            def add_pair(scale):
                def body(st, bk):
                    x_ = xT[:, 2 * st.j:2 * st.j + 2, :]
                    return stt(x_, halves(bk[:, :]), scale, x_, ALU.mult, ALU.add)
                return body

            empties("w_o", add_pair(1.0))
            settle("w_o")
            do_norm("peer")

            it = iota16

            key_bank = [None]

            def choose(t, h):
                if h % 2 == 0:
                    key_bank[0] = psS[chS.take(dve)]
                sides = range(2)
                row = [key_bank[0][:, (2 * (h % 2) + s) * P:(2 * (h % 2) + s + 1) * P] for s in sides]
                rest = [stop_[:, s * P:(s + 1) * P] for s in sides]
                first, second = slice(0, 8), slice(8, 16)
                dve.max(ktop[:, h, 0, first], row[0])
                link(dve.max(ktop[:, h, 1, first], row[1]))
                for s in sides:
                    dve.max_index(kidx[:, h, s, first].bitcast(U32), ktop[:, h, s, first], row[s])
                dve.match_replace(rest[0], ktop[:, h, 0, first], row[0], -3.0e38)
                ins = dve.match_replace(rest[1], ktop[:, h, 1, first], row[1], -3.0e38)
                link(ins)
                if h % 2:
                    dve.sem_inc(chS.free, 1)
                dve.max(ktop[:, h, 0, second], rest[0])
                link(dve.max(ktop[:, h, 1, second], rest[1]))
                x0, x1 = ktop[:, h, 0, :], ktop[:, h, 1, :]
                ap0 = bass.AP(x0.tensor, x0.offset, [list(x0.ap[0]), [1, 16], [0, 16]])
                ap1 = bass.AP(x1.tensor, x1.offset, [list(x1.ap[0]), [0, 16], [1, 16]])
                tt(cand[:, h], ap0, ap1, ALU.add)
                dve.max_index(kidx[:, h, 0, second].bitcast(U32), ktop[:, h, 0, second], rest[0])
                link(dve.max_index(kidx[:, h, 1, second].bitcast(U32), ktop[:, h, 1, second], rest[1]))
                sums_ = cand[:, h].rearrange("p a b -> p (a b)")
                dve.tensor_copy(kidf[:, h], kidx[:, h].bitcast(U32))
                link(dve.max(best[:, h, first], sums_))
                dve.max_index(bpos[:, h, first].bitcast(U32), best[:, h, first], sums_)
                link(dve.match_replace(cand2[:, h], best[:, h, first], sums_, -3.0e38))
                link(dve.max(best[:, h, second], cand2[:, h]))
                link(dve.max_index(bpos[:, h, second].bitcast(U32), best[:, h, second], cand2[:, h]))
                bp = bpos[:, h, :].bitcast(U32)
                mine_ = slice(h * TOPK, (h + 1) * TOPK)
                ts(bhalf[:, 0, mine_].bitcast(U32), bp, 4, ALU.logical_shift_right)
                link(ts(bhalf[:, 1, mine_].bitcast(U32), bp, 15, ALU.bitwise_and))
                link(dve.tensor_copy(bhalff[:, :, mine_], bhalf[:, :, mine_].bitcast(U32)))
                e4 = eq[:, 0:2 * TOPK * TOPK].rearrange("p (s k c) -> p s k c", s=2, k=TOPK)
                x_, k_ = bhalff[:, :, mine_], kidf[:, h]
                pos_b = bass.AP(x_.tensor, x_.offset, [list(x_.ap[0]), [P, 2], [1, TOPK], [0, TOPK]])
                io_b = bass.AP(it.tensor, it.offset, [list(it.ap[0]), [0, 2], [0, TOPK], [1, TOPK]])
                num_b = bass.AP(k_.tensor, k_.offset, [list(k_.ap[0]), [TOPK, 2], [0, TOPK], [1, TOPK]])
                link(tt(e4, pos_b, io_b, ALU.is_equal))
                link(tt(e4, e4, num_b, ALU.mult))
                link(dve.tensor_reduce(which[:, :, mine_], e4, AX_X, ALU.add))
                link(stt(idf[:, mine_], which[:, 0, mine_], float(KEYS), which[:, 1, mine_], ALU.mult, ALU.add))
                dve.tensor_copy(ids[:, t, mine_].bitcast(U32), idf[:, mine_]).then_inc(sem("ids_ready"), 1)

            def gates_of(t):
                g3 = gate[:, t].rearrange("p (h k) -> p h k", h=8)
                b0 = best[:, :, 0:1]
                top_b = bass.AP(b0.tensor, b0.offset, [list(b0.ap[0]), [16, 8], [0, 16]])
                tt(g3, best, top_b, ALU.subtract).then_inc(sem("best_ready"), 1)
                dve.wait_ge(sem("gate_exp"), t + 1)
                link(dve.tensor_reduce(gsum, g3, AX_X, ALU.add))
                link(dve.reciprocal(gsum, gsum))
                gs_b = bass.AP(gsum.tensor, gsum.offset, [list(gsum.ap[0]), [1, 8], [0, 16]])
                link(tt(g3, g3, gs_b, ALU.mult))

            ROUNDS = SLOTS // GATHERS
            PER_HEAD = TOPK // GATHERS

            def dot_rows(t, lo, rounds):
                before = 2 * t * ROUNDS + lo
                with dve.Fori(0, rounds) as i:
                    for k in range(GATHERS):
                        dve.wait_ge(sem(f"rows_in{k}"), i * 16 + 16 * (before + 1))
                        dve.tensor_tensor_reduce(gath[:, k, :], gath[:, k, :], hrow[:, t, :], 1.0, 0.0, ALU.mult, ALU.add,
                                                 dcol[:, k:k + 1]).then_inc(sem("rows_used"), 1)
                    dve.wait_ge(sem("rows_used"), i * GATHERS + (before + 2) * GATHERS)
                    dve.tensor_copy(dots[:, t, bass.ds(i * GATHERS + lo * GATHERS, GATHERS)], dcol).then_inc(sem("dots_part"), 1)
                    dve.wait_ge(sem("dots_part"), i + (lo + 1))

            def dot_head(t, h):
                for row in range(TOPK):
                    n = h * TOPK + row
                    k = n % GATHERS
                    dve.wait_ge(sem(f"rows_in{k}"), 16 * (2 * t * ROUNDS + n // GATHERS + 1))
                    dve.tensor_tensor_reduce(gath[:, k, :], gath[:, k, :], hrow[:, t, :], 1.0, 0.0, ALU.mult, ALU.add,
                                             dots[:, t, n:n + 1]).then_inc(sem("rows_used"), 1)

            def sum_rows(t, lo, rounds, others=()):
                before = (2 * t + 1) * ROUNDS + lo
                with dve.Fori(0, rounds) as i:
                    for k in range(GATHERS):
                        if k in others:
                            dve.sem_inc(sem("rows_used"), 1)
                            continue
                        dve.wait_ge(sem(f"rows_in{k}"), i * 16 + 16 * (before + 1))
                        stt(yacc[:, t, :], gath[:, k, :], wgt[:, t, bass.ds(i * GATHERS + (lo * GATHERS + k), 1)], yacc[:, t, :],
                            ALU.mult, ALU.add).then_inc(sem("rows_used"), 1)
                        dve.wait_ge(sem("rows_used"), i * GATHERS + ((before + 1) * GATHERS + k + 1))

            AHEAD = 2
            for h in range(AHEAD):
                choose(0, h)
            dve.wait_ge(sem("hrow_T"), 1)
            for t in range(TT):
                if t == 0:
                    for h in range(PEER_HEADS):
                        dot_head(t, h)
                        if h + AHEAD < PEER_HEADS:
                            choose(t, h + AHEAD)
                    dve.wait_ge(sem("rows_used"), SLOTS + GATHERS)
                else:
                    dot_rows(t, 0, ROUNDS)
                dve.sem_inc(sem("dots_ready"), 1)
                if t == 0:
                    gates_of(0)
                dve.wait_ge(sem("gelu_done"), t + 1)
                link(tt(wgt[:, t], wgt[:, t], gate[:, t], ALU.mult))
                dve.sem_inc(sem("weights"), 1)
                link(dve.memset(yacc[:, t], 0.0))
                if t == 0:
                    for h in range(PEER_HEADS):
                        choose(1, h)
                        sum_rows(t, h * PER_HEAD, PER_HEAD, BY_PE)
                    gates_of(1)
                    dve.wait_ge(sem("pe_sum"), 1)
                    for q in range(2):
                        y_ = yacc[:, t, 512 * q:512 * q + 512]
                        link(tt(y_, bank[q][:, :], y_, ALU.add))
                else:
                    sum_rows(t, 0, ROUNDS)
                dve.sem_inc(sem("experts_done"), 1)
            for t in range(TT):
                for q in range(2):
                    ps = psS[chS.take(dve)]
                    x_ = xT[:, 4 * q:4 * q + 4, t * P:(t + 1) * P]
                    tt(x_, ps[:, :].rearrange("p (c t) -> p c t", c=4), x_, ALU.add).then_inc(chS.free, 1)
            dve.wait_ge(chS.free, chS.got)
            do_norm("first")

            pairs_done = [0]

            def ffn(i, s):
                jb, jo = by_name[f"ffn_in{i}{s}"], by_name[f"ffn_out{i}{s}"]
                k0 = pairs_done[0]
                pairs_done[0] += FC // 2
                h0 = (2 * i + s) * (FC // 2)

                def ahead(st):
                    if not st.per and st.j + 2 >= jb.panels:
                        low_part(jo, Step(jo.first, st.j + 2 - jb.panels, 0, False))
                    else:
                        low_part(jb, after(st, 2))

                def one(st):
                    if st.j % 2 == 0:
                        ahead(st)
                        return
                    gate_slot = (st.slot - 1) % RING
                    g_uses = (jb.first + st.j - 1) // RING + 1
                    more = st.turn * 2 if st.per else 0
                    dve.wait_ge(emptied[gate_slot], st.turn + g_uses)
                    dve.wait_ge(multiplied, st.number + 1)
                    sg = halves(sgate[:, (st.j // 2 + k0) % 2, :])
                    tt(sg, halves(bank[st.slot][:, :]), sg, ALU.mult).then_inc(emptied[st.slot], 1)
                    dve.wait_ge(emptied[st.slot], st.uses + 1)
                    dve.sem_inc(sem("hidden_pair"), 1)
                    ahead(st)
                    at_ = st.at(lambda j: 2 * (j // 2))
                    both = slice(at_, at_ + 2) if not st.per else bass.ds(at_, 2)
                    dve.wait_ge(sem("h_high"), h0 + st.j // 2 + 1 + more)
                    tt(h_low[:, both, :], sg, h_high[:, both, :].bitcast(F32), ALU.subtract).then_inc(sem("h_low"), 1)
                    dve.wait_ge(sem("h_low"), h0 + st.j // 2 + 1 + more)
                    dve.sem_inc(sem("sgate_free"), 1)
                panels_of(dve, jb, one, ahead=2)

                for j in range(DC):
                    if j < DC - 2:
                        low_part(jo, Step(jo.first, j + 2, 0, False))
                    st = Step(jo.first, j, 0, False)
                    dve.wait_ge(multiplied, st.number + 1)
                    stt(xT[:, j, :], bank[st.slot][:, 0:T], 0.5, xT[:, j, :], ALU.mult, ALU.add).then_inc(emptied[st.slot], 1)
                settle(f"ffn_out{i}{s}")

            def ple(i):
                name = f"ple{i}"
                k0 = pairs_done[0]
                pairs_done[0] += 4

                def one(st):
                    if st.j % 2 == 0:
                        return
                    gate_slot = (st.slot - 1) % RING
                    g_uses = (by_name[name].first + st.j - 1) // RING + 1
                    dve.wait_ge(emptied[gate_slot], st.turn + g_uses if st.per else g_uses)
                    if st.per:
                        dve.sem_inc(sem("dve_turn"), 1)
                    dve.wait_ge(multiplied, st.number + 1)
                    at_ = st.at(lambda j: 2 * (j // 2))
                    x_ = xT[:, bass.ds(at_, 2), :] if st.per else xT[:, at_:at_ + 2, :]
                    sg = halves(sgate[:, (st.j // 2 + k0) % 2, :])
                    tt(sg, halves(bank[st.slot][:, :]), sg, ALU.mult).then_inc(emptied[st.slot], 1)
                    dve.wait_ge(emptied[st.slot], st.uses + 1)
                    if st.per:
                        dve.sem_inc(sem("dve_turn"), 1)
                    tt(x_, x_, sg, ALU.add).then_inc(sem("sgate_free"), 1)
                panels_of(dve, by_name[name], one)
                dve.wait_ge(sem("sgate_free"), pairs_done[0] + 2)

            first_low(0, 0)
            do_norm("ffn00")
            ffn(0, 0)
            do_norm("mix0")
            dve.wait_ge(sem("pos_in"), 48)
            R = slice(0, ROPE)
            link(dve.tensor_copy(posf[R, :], posi[R, :].bitcast(I32)))
            link(ts(ang[R, 0], posf[R, :], freq[R, 0:1], ALU.mult))
            link(ts(ang[R, 1], ang[R, 0], INV_TWO_PI, ALU.mult))
            link(ts(ang[R, 1], ang[R, 1], MAGIC, ALU.add))
            link(ts(ang[R, 1], ang[R, 1], -MAGIC, ALU.add))
            for part_ in TWO_PI_PARTS:
                link(stt(ang[R, 0], ang[R, 1], -part_, ang[R, 0], ALU.mult, ALU.add))
            link(ts(ang[R, 0], ang[R, 0], 3.1415925, ALU.min, -3.1415925, ALU.max))
            dve.sem_inc(sem("angles"), 1)
            dve.wait_ge(sem("sines"), 2)
            link(tt(cosT[R, :], cosT[R, :], cosT[R, :], ALU.mult))
            ts(cosT[R, :], cosT[R, :], -2.0, ALU.mult, 1.0, ALU.add)
            link(ts(sinT[0:32, :], sinT[0:32, :], -1.0, ALU.mult))
            for name, dst in (("cq", cqT), ("ckv", None)):
                st = Step(by_name[name].first, 0, 0, False)
                dve.wait_ge(multiplied, st.number + 1)
                bk = bank[st.slot]
                if dst is not None:
                    link2 = dve.tensor_copy(dst, halves(bk[:, :]))
                else:
                    dve.tensor_copy(ckvT, bk[:, 0:T].rearrange("p (c t) -> p c t", c=1))
                    link2 = dve.tensor_copy(krT[R, :], bk[R, T:2 * T])
                link2.then_inc(emptied[st.slot], 1)
                dve.wait_ge(emptied[st.slot], st.uses + 1)
            do_norm("cq")
            do_norm("ckv")

            def rotate(dst, src):
                link(tt(rope_sw[R, :], rope_sw[R, :], sinT[R, :], ALU.mult))
                link(tt(src, src, cosT[R, :], ALU.mult))
                link(tt(dst, src, rope_sw[R, :], ALU.add))
                dve.sem_inc(sem("rope_go"), 1)

            dve.sem_inc(sem("rope_go"), 1)
            dve.wait_ge(sem("swapped"), 1)
            rotate(krT[R, :], krT[R, :])
            for h in range(MLA_HEADS):
                st = Step(by_name["uq"].first, h, 0, False)
                dve.wait_ge(emptied[st.slot], st.uses + 1)
                rotate(qrT[R, h, :], rope_in[R, :])
            attention("mla")
            dve.sem_inc(sem("attended"), 1)
            empties("mla_o", add_pair(1.0), lambda: first_low(0, 1))
            settle("mla_o")
            do_norm("ffn01")
            ffn(0, 1)
            do_norm("ple0")
            ple(0)
            first_low(1, 0)
            do_norm("ffn10")
            ffn(1, 0)
            do_norm("mix1")
            st = Step(by_name["ff"].first, 0, 0, False)
            dve.wait_ge(multiplied, st.number + 1)
            f3 = [ftmp[:, k].rearrange("p (t h) -> p t h", t=TT) for k in range(6)]
            fb = bass.AP(fbias.tensor, fbias.offset, [list(fbias.ap[0]), [0, TT], [1, FOX_HEADS]])
            tt(f3[0], bank[st.slot][:, :].rearrange("p (t n) -> p t n", t=TT)[:, :, 0:FOX_HEADS], fb, ALU.add)\
                .then_inc(emptied[st.slot], 1)
            dve.wait_ge(emptied[st.slot], st.uses + 1)
            link(stt(f3[1], f3[0], -1.0, f3[0], ALU.mult, ALU.max))
            dve.sem_inc(sem("forget"), 1)
            dve.wait_ge(sem("fexp"), 1)
            link(ts(f3[2], f3[1], 1.0, ALU.add))
            dve.sem_inc(sem("forget"), 1)
            link(ts(f3[3], f3[0], 0.0, ALU.min))
            dve.wait_ge(sem("fexp"), 2)
            link(tt(logf, f3[3], f3[2], ALU.subtract))
            dve.sem_inc(sem("forget"), 1)
            for t in range(TT):
                l_ = logf[:, t, :]
                lb = bass.AP(l_.tensor, l_.offset, [list(l_.ap[0]), [1, FOX_HEADS], [0, P]])
                link(dve.tensor_copy(logf_wide[:, t].rearrange("p (h q) -> p h q", h=8), lb))
            dve.sem_inc(sem("forget"), 1)
            ps = psS[chS.take(dve)]
            dve.tensor_copy(cumq, ps[:, 0:16].rearrange("p (t h) -> p t h", t=TT)).then_inc(chS.free, 1)
            for h2 in range(FOX_HEADS // 2):
                ps = psS[chS.take(dve)]
                ts(ncum[:, 2 * h2:2 * h2 + 2, P:3 * P], halves(ps[:, :]), -1.0, ALU.mult)
                ts(ncum[:, 2 * h2:2 * h2 + 2, 0:P], halves(ps[:, :])[:, :, 0:P], -1.0, ALU.mult).then_inc(chS.free, 1)
            dve.wait_ge(chS.free, chS.got)
            attention("fox")
            dve.sem_inc(sem("attended"), 1)
            empties("fox_o", add_pair(1.0), lambda: first_low(1, 1))
            settle("fox_o")
            do_norm("ffn11")
            ffn(1, 1)
            do_norm("ple1")
            ple(1)
            do_norm("final")


NAMES = ["x", "mem", "rel_bias", "g_mix", "w_in", "w_pool_grp", "pool_scale", "w_pool_out", "w_cmp_k", "w_cmp_v", "pe_k",
         "pe_v", "w_nsa_out", "g_mem", "w_mem_kv", "w_x_out", "w_o", "g_ffn", "w_peer_q", "peer_sub_keys", "peer_u",
         "peer_v", "g_final", "p_2", "positions_2", "ffn_norm_2", "ffn_w_in_2", "ffn_w_out_2", "mix_norm_2",
         "mla_w_down_2", "mla_q_norm_2", "mla_w_uq_2", "mla_kv_norm_2", "mla_w_ukv_2", "mla_w_o_2", "fox_w_in_2",
         "fox_b_f_2", "fox_w_o_2", "ple_norm_2", "ple_w_gate_2", "ple_w_proj_2", "final_norm_2"]


def kernel(**inputs):
    import numpy as np
    import concourse.bacc as bacc
    from concourse.bass_utils import run_bass_kernel_spmd

    n = np.arange(T)[::-1]
    large = 16 + (np.log(np.maximum(n, 1).astype(np.float32) / np.float32(16)) / np.float32(math.log(8)) * np.float32(16)).astype(np.int32)
    bucket = np.where(n < 16, n, np.minimum(large, BUCKETS - 1))
    onehot = (np.arange(BUCKETS)[:, None] == bucket[None, :]).astype(np.float32)
    half = (10000.0 ** (-np.arange(0, ROPE, 2, dtype=np.float64) / ROPE)).astype(np.float32)
    freq = np.concatenate([half, half])[:, None]

    nc = bacc.Bacc("TRN2", target_bir_lowering=False, num_devices=1)
    arrays, aps = {}, {}
    for name in NAMES:
        arr = np.ascontiguousarray(inputs[name])
        arrays[name + "_in"] = arr
        aps[name] = nc.dram_tensor(name + "_in", arr.shape, mybir.dt.from_np(arr.dtype), kind="ExternalInput").ap()
    arrays["onehot_in"], arrays["freq_in"] = onehot, freq
    hot = nc.dram_tensor("onehot_in", onehot.shape, F32, kind="ExternalInput").ap()
    fr = nc.dram_tensor("freq_in", freq.shape, F32, kind="ExternalInput").ap()
    out = nc.dram_tensor("out", (1, T, D), F32, kind="ExternalOutput").ap()
    build(nc, aps, out, hot, fr)
    r = run_bass_kernel_spmd(nc, [arrays], core_ids=[0])
    return r.results[0]["out"]
```

```python
import math
from contextlib import ExitStack

import concourse.bass as bass
from concourse import mybir

ALU = mybir.AluOpType
ACT = mybir.ActivationFunctionType
F32 = mybir.dt.float32
U32 = mybir.dt.uint32
F32R = mybir.dt.float32r
I32 = mybir.dt.int32
AX_X = mybir.AxisListType.X

P = 128
T = 256
TT = T // P
D = 1024
DC = D // P
POOL_W, NSA_W, KV_W = 512, 1024, 256
NSA_HEADS, NSA_GROUPS, HEAD = 16, 4, 64
HEADS_PER_GROUP = NSA_HEADS // NSA_GROUPS
CMP_LEN, CMP_STRIDE = 32, 16
N_CMP = (T - CMP_LEN) // CMP_STRIDE + 1
CMP_SLOT = 32
LP = CMP_LEN // 2
X_HEADS = 4
BUCKETS = 32
PEER_HEADS, KEYS, TOPK = 8, 128, 16
SLOTS = PEER_HEADS * TOPK
D_FF = 2816
FC = D_FF // P
MLA_HEADS, ROPE = 8, 64
FOX_HEADS = 8
NEG = -1e30
EPS = 1e-6
MAGIC = 1.5 * 2.0 ** 23
TWO_PI_PARTS = (6.28125, 0.00193500518798828125, 2 * math.pi - 6.28125 - 0.00193500518798828125)
INV_TWO_PI = 0.15915494309189535

Z_POOL, Z_Q, Z_KV = 0, POOL_W, POOL_W + NSA_W
Z_GATE = Z_KV + 6 * KV_W
Z_QX = Z_GATE + 3 * NSA_HEADS
Z_MERGE = Z_QX + X_HEADS * P

GAINS = [("g_mix", 8), ("g_mem", 8), ("g_ffn", 8), ("g_final", 8), ("ffn_norm_2", 32), ("mix_norm_2", 16),
         ("ple_norm_2", 16), ("final_norm_2", 8), ("mla_q_norm_2", 2), ("mla_kv_norm_2", 1), ("pool_scale", 4)]
GAIN_AT = {}
for _name, _n in GAINS:
    GAIN_AT[_name] = sum(n for _, n in GAINS[:len(GAIN_AT)])
N_GAINS = sum(n for _, n in GAINS)

RING = 4
PANEL = FC * P
GATHERS = 8
LAG = 3
BY_PE = (1, 4, 7)


class Job:

    def __init__(self, name, panels, kind, weight, rows, cols, width, act):
        self.name, self.panels, self.kind = name, panels, kind
        self.weight, self.rows, self.cols, self.width, self.act = weight, rows, cols, width, act
        self.first = 0
        self.split = None
        self.split_first = 0


class Step:

    def __init__(self, first, j, turn, per):
        self.j, self.turn, self.per, self.origin = j, turn, per, first
        self.slot = (first + j) % RING
        self.uses = (first + j) // RING + turn
        self.number = first + j + (turn * RING if per else 0)

    def at(self, f):
        if not self.per:
            return f(self.j)
        return f(self.j) + self.turn * (f(self.j + RING) - f(self.j))


def panels_of(eng, job, body, ahead=0, peeled=0):
    for j in range(peeled):
        body(Step(job.first, j, 0, False))
    turns = (job.panels - peeled - ahead) // RING
    done = peeled
    if turns >= 2 and job.first >= RING:
        with eng.Fori(0, turns) as i:
            for j in range(peeled, peeled + RING):
                body(Step(job.first, j, i, True))
        done += turns * RING
    for j in range(done, job.panels):
        body(Step(job.first, j, 0, False))


def over_partitions(row, n):
    return bass.AP(row.tensor, row.offset, [[0, n], [1, row.shape[-1]]])


def build(nc, a, out, onehot, inv_freq):
    ctx = ExitStack()
    with ctx:
        def sb(name, shape, dt=F32):
            return ctx.enter_context(nc.sbuf_tensor(name, shape, dt))

        sems = {}

        def sem(name):
            if name not in sems:
                sems[name] = ctx.enter_context(nc.semaphore(name))
            return sems[name]

        xT = sb("xT", [P, DC, T])
        nT_byte = nc.sbuf_base
        nT = sb("nT", [P, DC, T])
        ring_byte = nc.sbuf_base
        ring = sb("ring", [P, RING, PANEL])
        work = sb("work", [P, 3, LAG, 512])
        soft, prob, probT = work[:, 0], work[:, 1], work[:, 2]
        squares = work[:, :, :, :].rearrange("p n a b -> p (n a b)")
        ident = sb("ident", [P, P])
        ones = sb("ones", [P, P])
        causal = sb("causal", [P, 3 * P])
        chunked = sb("chunked", [P, 3 * P])
        zeros = sb("zeros", [P, 512])
        tri = sb("tri", [P, TT, T])
        gains = sb("gains", [P, N_GAINS])
        root = sb("root", [P, T])
        rstd = sb("rstd", [P, T])
        nmax = sb("nmax", [P, LAG, TT])
        sums = sb("sums", [P, LAG, TT])
        inv = sb("inv", [P, LAG, TT])
        coef = sb("coef", [P, LAG, TT])
        has = sb("has", [P, 1])
        eps = sb("eps", [P, 1])
        unused = sb("unused", [P, 1])
        iota16 = sb("iota16", [P, 16])[:, :]
        arena_byte = nc.sbuf_base
        arena = sb("arena", [P, 30208])
        spot = [0]

        def parts_at(name, shape, at, base=arena_byte):
            return nc.alloc_sbuf_tensor_at(name, [P] + shape, F32R, offset=base + 4 * at)

        def part(n, at=None):
            if at is None:
                at = spot[0]
                spot[0] += n
                assert spot[0] <= 30208, spot[0]
            return arena[:, at:at + n]

        merge = part(24 * T).rearrange("p (c t) -> p c t", c=24)
        tokk = part(1024, 0).rearrange("p (g t) -> p g t", g=4)
        tokv = part(1024, 1024).rearrange("p (g t) -> p g t", g=4)
        blkk = part(2048, 2048).rearrange("p (l g c) -> p l g c", l=LP, g=4)
        blkv = part(2048, 4096).rearrange("p (l g c) -> p l g c", l=LP, g=4)
        bias_at = spot[0]
        bias = part(NSA_HEADS * 384).rearrange("p (h k) -> p h k", h=NSA_HEADS)
        w_high1 = parts_at("w_high1", [2, 2048], bias_at)
        n_high1 = parts_at("n_high1", [DC, T], bias_at + 4096)
        m_low = parts_at("m_low", [DC, T], 0)
        n_high2 = parts_at("n_high2", [DC, T], 16 * T)
        x_in = part(2048, bias_at).rearrange("p (t d) -> p t d", t=TT)
        mem_in = part(2048, bias_at + 2048).rearrange("p (t d) -> p t d", t=TT)
        rows_in = part(P, bias_at + 4096)
        pe_in = part(P, bias_at + 4224)
        q_at = spot[0]
        qT = part(2048).rearrange("p (c t) -> p c t", c=8)
        kselT = part(512).rearrange("p (c t) -> p c t", c=2)
        kwinT = part(512).rearrange("p (c t) -> p c t", c=2)
        vsel = part(512).rearrange("p (t d) -> p t d", t=2)
        vwin = part(512).rearrange("p (t d) -> p t d", t=2)
        o_at = spot[0]
        o_nsa = part(2048).rearrange("p (t d) -> p t d", t=2)
        memT = part(2048, o_at).rearrange("p (c t) -> p c t", c=8)
        w_cmp = part(2 * 1024).rearrange("p (k l d) -> p k l d", k=2, l=LP)
        w_grp = part(512).rearrange("p (g d) -> p g d", g=4)
        qxT = part(1024).rearrange("p (c t) -> p c t", c=4)
        kxT = part(1024).rearrange("p (c t) -> p c t", c=4)
        vx = part(1024).rearrange("p (t d) -> p t d", t=2)
        ox_low, mix_low = parts_at("ox_low", [4, T], spot[0]), parts_at("mix_low", [4, T], spot[0] + 1024)
        ox_high, mix_high = parts_at("ox_high", [4, T], q_at), parts_at("mix_high", [4, T], q_at + 1024)
        uT = part(1024).rearrange("p (c t) -> p c t", c=4)
        mixT = part(1024).rearrange("p (c t) -> p c t", c=4)
        o_x = part(1024, spot[0]).rearrange("p (t d) -> p t d", t=2)
        pcmp = part(1024).rearrange("p (t r g c) -> p t r g c", t=2, r=4, g=4)
        pcmpT = part(1024).rearrange("p (t r q) -> p t r q", t=2, r=4)
        scmp = part(480).rearrange("p (n c) -> p n c", c=N_CMP)
        bcmp = part(512).rearrange("p (n c) -> p n c", c=16)
        kcT = part(2 * N_CMP).rearrange("p (s c) -> p s c", s=2)
        vc = part(HEAD)
        cstat = part(4 * 32).rearrange("p (k n) -> p k n", k=4)
        gate_nsa = part(TT * 48).rearrange("p (t n) -> p t n", t=TT)
        peT = part(32)
        table = part(384, q_at)
        rel = part(16, q_at + 384)
        hot = part(256, q_at + 400)
        icount = part(16)
        oxT = uT[:, :, :]
        spot[0] = 0
        gath = part(GATHERS * D).rearrange("p (k d) -> p k d", k=GATHERS)
        qpT = part(16 * T).rearrange("p (c t) -> p c t", c=16)
        hrow = part(2048).rearrange("p (t d) -> p t d", t=TT)
        sub_in = part(2048).rearrange("p (c k) -> p c k", c=16)
        eq = sub_in.rearrange("p c k -> p (c k)")
        subT = part(2048).rearrange("p (c k) -> p c k", c=16)
        cand = part(2048).rearrange("p (h a b) -> p h a b", h=8, a=16)
        cand2 = part(2048).rearrange("p (h n) -> p h n", h=8)
        yacc = part(2048).rearrange("p (t d) -> p t d", t=TT)
        stop_ = part(2 * P)
        ktop = part(256).rearrange("p (h s k) -> p h s k", h=8, s=2)
        kidx = part(256).rearrange("p (h s k) -> p h s k", h=8, s=2)
        kidf = part(256).rearrange("p (h s k) -> p h s k", h=8, s=2)
        best = part(P).rearrange("p (h k) -> p h k", h=8)
        bpos = part(P).rearrange("p (h k) -> p h k", h=8)
        bhalf = part(2 * P).rearrange("p (s n) -> p s n", s=2)
        bhalff = part(2 * P).rearrange("p (s n) -> p s n", s=2)
        which = part(2 * P).rearrange("p (s n) -> p s n", s=2)
        idf = part(P)
        ids = part(TT * P).rearrange("p (t n) -> p t n", t=TT)
        idcol = part(GATHERS)
        gate = part(TT * P).rearrange("p (t n) -> p t n", t=TT)
        dots = part(TT * P).rearrange("p (t n) -> p t n", t=TT)
        wgt = part(TT * P).rearrange("p (t n) -> p t n", t=TT)
        dcol = part(GATHERS)
        gsum = part(8)
        wcol = part(len(BY_PE))
        diag = part(len(BY_PE) * P).rearrange("p (k n) -> p k n", k=len(BY_PE))
        w_high = parts_at("w_high", [2, PANEL], 0)
        h_high = parts_at("h_high", [FC, T], 2 * PANEL)
        h_low = parts_at("h_low", [FC, T], 2 * PANEL + FC * T)
        w_low = parts_at("w_low", [RING, PANEL], 0, ring_byte)
        n_low = parts_at("n_low", [DC, T], 0, nT_byte)
        spot[0] = 30208 - 2048 - 3 * 1024 - 8 - 1 - 256
        fence = spot[0] = spot[0] // 8 * 8
        n_high = parts_at("n_high", [DC, T], spot[0])
        spot[0] += DC * T
        sgate = part(1024).rearrange("p (k n) -> p k n", k=2)
        p_at = spot[0]
        p_in = part(4 * 256).rearrange("p (i t d) -> p i t d", i=2, t=2)
        pT = part(4 * 256).rearrange("p (i c t) -> p i c t", i=2, c=2)
        p_high = parts_at("p_high", [2, 2, T], p_at)
        p_low = parts_at("p_low", [2, 2, T], p_at + 1024)
        fbias = part(8)
        freq = part(1)
        posi = part(256)
        spot[0] = 2 * PANEL
        q2T = part(2048).rearrange("p (c t) -> p c t", c=8)
        qrT = part(2048).rearrange("p (c t) -> p c t", c=8)
        k2T = part(2048).rearrange("p (c t) -> p c t", c=8)
        v2 = part(2048).rearrange("p (t d) -> p t d", t=2)
        o2 = part(2048).rearrange("p (t d) -> p t d", t=2)
        cqT = part(512).rearrange("p (c t) -> p c t", c=2)
        ckvT = part(256).rearrange("p (c t) -> p c t", c=1)
        krT = part(256)
        rope_in = part(256)
        rope_sw = part(256)
        cosT = part(256)
        sinT = part(256)
        ncum = part(8 * 384).rearrange("p (h k) -> p h k", h=8)
        ftmp = part(6 * 16).rearrange("p (k n) -> p k n", k=6)
        logf = part(16).rearrange("p (t h) -> p t h", t=2)
        logf_wide = part(2048).rearrange("p (t n) -> p t n", t=2)
        cumq = part(16).rearrange("p (t h) -> p t h", t=2)
        posf = part(256)
        ang = part(3 * 256).rearrange("p (k t) -> p k t", k=3)
        assert spot[0] <= fence and 2 * PANEL + 2 * FC * T <= fence
        xrow = part(2048, 0).rearrange("p (t d) -> p t d", t=TT)

        bank = [ctx.enter_context(nc.psum_tensor(f"bank{i}", [P, 512], F32)) for i in range(RING)]
        psS = [ctx.enter_context(nc.psum_tensor(f"psS{i}", [P, 512], F32)) for i in range(2)]
        psP = ctx.enter_context(nc.psum_tensor("psP", [P, 512], F32))
        psO = ctx.enter_context(nc.psum_tensor("psO", [P, 512], F32))
        toeplitz = nc.dram_tensor("toeplitz", (NSA_HEADS, P, 384), F32, kind="Internal")

        w_in = a["w_in"][0]
        L = range(2)

        def wv(ap):
            return ap.rearrange("(c p) n -> p c n", p=P)

        def job(name, panels, kind, weight, cols, width, act, chunks=DC):
            return Job(name, panels, kind, lambda j: wv(weight), lambda j: chunks, cols, width, lambda j: act)

        jobs = [job("kv", 6, None, w_in, lambda j: Z_KV + 256 * j, 256, nT)]
        jobs[0].kind = lambda j: "T" if j in (3, 5) else "F"
        jobs += [
            job("q", 4, "F", w_in, lambda j: Z_Q + 256 * j, 256, nT),
            job("gate_nsa", 1, "T", w_in, lambda j: Z_GATE, 48, nT),
            job("qx", 2, "F", w_in, lambda j: Z_QX + 256 * j, 256, nT),
            job("pool", 2, "F", w_in, lambda j: Z_POOL + 256 * j, 256, nT),
            job("kx", 2, "F", a["w_mem_kv"][0], lambda j: 256 * j, 256, memT),
            job("vx", 2, "T", a["w_mem_kv"][0], lambda j: 512 + 256 * j, 256, memT),
            job("merge", 12, "F", w_in, lambda j: Z_MERGE + 256 * j, 256, nT),
            job("pool_out", 4, "F", a["w_pool_out"][0], lambda j: 256 * j, 256, mixT, 4),
            job("x_out", 4, "F", a["w_x_out"][0], lambda j: 256 * j, 256, oxT, 4),
            job("nsa_out", 4, "F", a["w_nsa_out"][0], lambda j: 256 * j, 256, nT),
            job("w_o", 4, "F", a["w_o"][0], lambda j: 256 * j, 256, merge),
            job("peer_q", 8, "F", a["w_peer_q"][0], lambda j: 256 * j, 256, nT),
        ]

        def ffn_jobs(i, s):
            w = a["ffn_w_in_2"][i, s]
            j1 = job(f"ffn_in{i}{s}", FC, "F", w, lambda j: (j % 2) * D_FF + 256 * (j // 2), 256, None)
            j2 = job(f"ffn_out{i}{s}", DC, "F", a["ffn_w_out_2"][i, s], lambda j: 128 * j, 128, None, FC)
            j1.split, j2.split = lambda j: (n_high, n_low), lambda j: (h_high, h_low)
            return [j1, j2]

        def ple_job(i):
            jp = job(f"proj{i}", 1, "F", a["ple_w_proj_2"][i], lambda j: 0, D, None, 2)
            jg = job(f"ple{i}", 4, "F", a["ple_w_gate_2"][i], lambda j: 256 * j, 256, None)
            jp.split, jg.split = lambda j: (p_high[:, i], p_low[:, i]), lambda j: (n_high, n_low)
            return [jp, jg]

        jobs += ffn_jobs(0, 0) + [
            job("cq", 1, "F", a["mla_w_down_2"][0], lambda j: 0, 256, nT),
            job("ckv", 1, "F", a["mla_w_down_2"][0], lambda j: 256, 192, nT),
            job("uq", 8, "F", a["mla_w_uq_2"][0], lambda j: 192 * j, 192, cqT, 2),
            job("ukv", 8, "FT", a["mla_w_ukv_2"][0], lambda j: 256 * j, 256, ckvT, 1),
            job("mla_o", 4, "F", a["mla_w_o_2"][0], lambda j: 256 * j, 256, nT),
        ] + ffn_jobs(0, 1) + ple_job(0) + ffn_jobs(1, 0) + [
            job("fq", 4, "F", a["fox_w_in_2"][0], lambda j: 256 * j, 256, nT),
            job("fk", 4, "F", a["fox_w_in_2"][0], lambda j: D + 256 * j, 256, nT),
            job("fv", 4, "T", a["fox_w_in_2"][0], lambda j: 2 * D + 256 * j, 256, nT),
            job("ff", 1, "T", a["fox_w_in_2"][0], lambda j: 3 * D, FOX_HEADS, nT),
            job("fox_o", 4, "F", a["fox_w_o_2"][0], lambda j: 256 * j, 256, nT),
        ] + ffn_jobs(1, 1) + ple_job(1)
        FIRST_BLOCK = {"merge": (n_high1, n_low), "nsa_out": (n_high1, n_low), "w_o": (n_high2, m_low),
                       "pool_out": (mix_high, mix_low), "x_out": (ox_high, ox_low)}
        for j_ in jobs:
            if j_.name in FIRST_BLOCK:
                j_.split = lambda j, parts=FIRST_BLOCK[j_.name]: parts
            if j_.name in ("mla_o", "fq", "fk", "fv", "ff", "fox_o"):
                j_.split = lambda j: (n_high, n_low)
        at = 0
        by_name = {}
        n_split = 0
        for j_ in jobs:
            j_.first, j_.split_first = at, n_split
            if j_.split:
                n_split += j_.panels
            at += j_.panels
            by_name[j_.name] = j_
        landed = [sem(f"landed{k}") for k in range(RING)]
        multiplied = sem("multiplied")
        emptied = [sem(f"emptied{k}") for k in range(RING)]
        high = sem("high")
        low = sem("low")

        def after(st, n):
            return Step(st.origin, st.j + n, st.turn, st.per)

        def split_no(job_, st):
            return st.number - job_.first + job_.split_first

        BY_POOL = {"merge": 2, "ffn_in00": 2, "mla_o": 2, "ple0": 1, "fox_o": 2, "ple1": 1}

        def low_written(job_, st):
            order = [j_.name for j_ in jobs]
            sooner = sum(BY_POOL[key] for key in BY_POOL if order.index(key) < order.index(job_.name))
            if job_.name in BY_POOL:
                if st.j < BY_POOL[job_.name]:
                    return sem("pool_low"), sooner + st.j + 1
                sooner += BY_POOL[job_.name]
            return low, split_no(job_, st) + 1 - sooner

        def high_of(job_, st):
            n = job_.rows(st.j) * job_.width
            w = w_high1 if job_.name in FIRST_BLOCK else w_high
            return w[:, (job_.split_first + st.j) % 2, 0:n], n

        in_parts = [(j_, k) for j_ in jobs if j_.split for k in range(j_.panels)]

        def first_part(key, s, make):
            if key in ("mla", "fox") and s in (4, 6) or key == "x" and s < 2:
                jb = by_name["merge" if key == "x" else key + "_o"]
                make(jb, Step(jb.first, s if key == "x" else (s - 4) // 2, 0, False))

        def two_on(job_, st):
            if st.per or st.j + 2 < job_.panels:
                return job_, after(st, 2)
            n = job_.split_first + st.j + 2
            if n >= len(in_parts) or (in_parts[n][0].name in ("ffn_in00", "mla_o", "fox_o") and job_ is not in_parts[n][0]):
                return None
            jb, k = in_parts[n]
            return jb, Step(jb.first, k, 0, False)

        def unit(lhs, rhs, scale, mask, width, v, outs, kind, extra=None):
            return dict(lhs=lhs, rhs=rhs, scale=scale, mask=mask, width=width, v=v, outs=outs, kind=kind, extra=extra)

        SEGS = {384: [(0, [(0, 0)]), (1, [(1, 0), (2, 1)])],
                512: [(0, [(0, 0), (1, 1)]), (1, [(2, 0), (3, 1)])]}

        nsa_units = []
        for b, (kT_, v_) in enumerate(((kselT, vsel), (kwinT, vwin))):
            for h in range(NSA_HEADS):
                g = h // HEADS_PER_GROUP
                lo = HEAD * (g % 2)
                nsa_units.append(unit(
                    [qT[lo:lo + HEAD, (g // 2) * 4 + h % 4, :]], [kT_[lo:lo + HEAD, g // 2, :]], 1.0, bias[:, h, :], 384,
                    [v_[:, k, g * HEAD:(g + 1) * HEAD] for k in range(TT)],
                    [o_nsa[:, t, h * HEAD:(h + 1) * HEAD] for t in range(TT)],
                    "gated", gate_nsa[:, :, (b + 1) * NSA_HEADS + h]))
        x_units = [unit([qxT[:, h, :]], [kxT[:, h, :]], float(P) ** -0.5, zeros[:, :], 512,
                        [vx[:, k, h * P:(h + 1) * P] for k in range(TT)],
                        [o_x[:, t, h * P:(h + 1) * P] for t in range(TT)], "plain") for h in range(X_HEADS)]
        mla_units = [unit([q2T[:, h, :], qrT[0:ROPE, h, :]], [k2T[:, h, :], krT[0:ROPE, :]], float(P + ROPE) ** -0.5,
                          chunked[:, :], 384, [v2[:, k, h * P:(h + 1) * P] for k in range(TT)],
                          [o2[:, t, h * P:(h + 1) * P] for t in range(TT)], "plain") for h in range(MLA_HEADS)]
        fox_units = [unit([q2T[:, h, :]], [k2T[:, h, :]], float(P) ** -0.5, ncum[:, h, :], 384,
                          [v2[:, k, h * P:(h + 1) * P] for k in range(TT)],
                          [o2[:, t, h * P:(h + 1) * P] for t in range(TT)], "fox", cumq[:, :, h]) for h in range(FOX_HEADS)]
        unit_base = {}
        n_ = 0
        for key, us in (("nsa", nsa_units), ("x", x_units), ("mla", mla_units), ("fox", fox_units)):
            unit_base[key] = (n_, us)
            n_ += len(us)
        biased = sem("biased")
        exped = sem("exped")
        probs_up = sem("probs_up")

        class Channel:

            def __init__(self, name, depth):
                self.full, self.free, self.depth = sem(name + "_full"), sem(name + "_free"), depth
                self.put = self.got = 0

            def claim(self, pe):
                if self.put >= self.depth:
                    pe.wait_ge(self.free, self.put - self.depth + 1)
                self.put += 1
                return (self.put - 1) % self.depth

            def take(self, eng):
                self.got += 1
                eng.wait_ge(self.full, self.got)
                return (self.got - 1) % self.depth

        turned_back = []
        chS, chP, chO = Channel("S", 2), Channel("P", 1), Channel("O", 1)
        chJ = Channel("J", 4)

        def proj_banks(i):
            return [psS[0], psS[1], psO, bank[by_name[f"proj{i}"].first % RING]]

        projected = squares[:, 2560:2560 + 2048]

        norms = {}

        def norm(name, src, dst, gain, chunks, after_job=None):
            norms[name] = (len(norms), src, dst, GAIN_AT[gain[0]] + gain[1], chunks)
            if after_job:
                early[name] = (len(early), after_job, 1 if after_job.startswith("ffn_out") else 2)
            if chunks == DC:
                whole[name] = len(whole)

        early, whole = {}, {}
        norm("mix", xT, nT, ("g_mix", 0), DC)
        norm("mem", memT, memT, ("g_mem", 0), DC)
        norm("peer", xT, nT, ("g_ffn", 0), DC, "w_o")
        norm("first", xT, xT, ("g_final", 0), DC)
        norm("ffn00", xT, nT, ("ffn_norm_2", 0), DC)
        norm("mix0", xT, nT, ("mix_norm_2", 0), DC, "ffn_out00")
        norm("cq", cqT, cqT, ("mla_q_norm_2", 0), 2)
        norm("ckv", ckvT, ckvT, ("mla_kv_norm_2", 0), 1)
        norm("ffn01", xT, nT, ("ffn_norm_2", 8), DC, "mla_o")
        norm("ple0", xT, nT, ("ple_norm_2", 0), DC, "ffn_out01")
        norm("ffn10", xT, nT, ("ffn_norm_2", 16), DC, "ple0")
        norm("mix1", xT, nT, ("mix_norm_2", 8), DC, "ffn_out10")
        norm("ffn11", xT, nT, ("ffn_norm_2", 24), DC, "fox_o")
        norm("ple1", xT, nT, ("ple_norm_2", 8), DC, "ffn_out11")
        norm("final", xT, xT, ("final_norm_2", 0), DC, "ple1")
        late = [name for name in norms if name not in early]

        def squares_by_act(name):
            n = late.index(name)
            return n + 1 + (n >= late.index("first"))

        PAIRS = DC // 2
        split_norms = ["ffn00", "ffn01", "ple0", "ffn10", "mix1", "ffn11", "ple1"]
        norm_pair = sem("norm_pair")
        early_sum = sem("early_sum")
        squared_v, squared_s = sem("squared_v"), sem("squared_s")
        rooted, normed = sem("rooted"), sem("normed")
        src_ready = sem("src_ready")

        ple_pairs = {"ple0": 2 * (FC // 2), "ple1": 4 * (FC // 2) + 4}

        block = ctx.enter_context(nc.Block())

        @block.sync
        def _(sp):
            for jb in jobs:
                def load(st):
                    if not (isinstance(st.number, int) and st.number < RING):
                        sp.wait_ge(emptied[st.slot], st.uses)
                    c = jb.rows(st.j)
                    src = jb.weight(st.j)
                    cols = st.at(jb.cols)
                    src = src[:, :, bass.ds(cols, jb.width)] if st.per else src[:, :, cols:cols + jb.width]
                    dst = ring[:, st.slot, 0:c * jb.width].rearrange("p (c n) -> p c n", c=c)
                    sp.dma_start(dst, src).then_inc(landed[st.slot], 16)
                panels_of(sp, jb, load)
            sp.wait_ge(sem("out_rows"), 4)
            sp.dma_start(out.rearrange("b (t p) d -> p (b t) d", p=P), xrow[:, :, :]).then_inc(sem("stored"), 16)
            sp.wait_ge(sem("stored"), 16)

        @block.gpsimd
        def _(pool):
            chain = [0]

            def link(ins):
                ins.then_inc(sem("pool_chain"), 1)
                chain[0] += 1
                pool.wait_ge(sem("pool_chain"), chain[0])

            def fill(ap, value, keep, base, pattern, mult):
                return pool.affine_select(out=ap, in_=ap, compare_op=keep, fill=value, base=base, pattern=pattern,
                                          channel_multiplier=mult)

            link(pool.memset(ident[:, :], 0.0))
            link(fill(ident[:, :], 1.0, ALU.not_equal, 0, [[-1, P]], 1))
            link(pool.memset(ones[:, :], 1.0))
            link(pool.memset(eps[:, :], EPS))
            pool.sem_inc(sem("consts"), 1)
            link(pool.memset(has[:, :], 1.0))
            link(fill(has[:, :], 0.0, ALU.is_ge, -(CMP_LEN - 1), [[0, 1]], 1))
            link(pool.memset(zeros[:, :], 0.0))
            link(pool.memset(causal[:, :], 0.0))
            link(pool.memset(chunked[:, :], 0.0))
            for lo in (0, 2 * P):
                link(fill(causal[:, lo:lo + P], NEG, ALU.is_ge, 0, [[-1, P]], 1))
            for lo in (HEAD, 2 * P + HEAD):
                link(pool.memset(chunked[0:64, lo:lo + 64], NEG))
            link(pool.memset(tri[:, :, :], 1.0))
            link(fill(tri[:, :, :], 0.0, ALU.is_ge, 0, [[-P, TT], [1, T]], -1))
            link(pool.memset(pcmp, 0.0))
            link(pool.memset(blkv, 0.0))
            link(pool.memset(bcmp, NEG))
            link(pool.memset(table, NEG))
            link(pool.iota(icount, pattern=[[1, 16]], base=1, channel_multiplier=0, allow_small_or_imprecise_dtypes=True))
            link(pool.iota(iota16, pattern=[[1, 16]], base=0, channel_multiplier=0, allow_small_or_imprecise_dtypes=True))
            pool.sem_inc(sem("consts"), 1)

            def early_squares(name):
                n = norms[name][0]
                e, after_job, width = early[name]
                total, one = squares[:, 0:width * T], squares[:, 512:512 + width * T]
                pool.wait_ge(normed, n)
                for g in range(DC // width - 1):
                    if after_job.startswith("ple"):
                        pool.wait_ge(sem("sgate_free"), 2 + ple_pairs[after_job] + g + 1)
                    else:
                        no = by_name[after_job].first + g
                        pool.wait_ge(emptied[no % RING], no // RING + 1)
                    x_ = xT[:, g * width:(g + 1) * width, :].rearrange("p c t -> p (c t)")
                    if g == 0:
                        link(pool.tensor_tensor(total, x_, x_, ALU.mult))
                    else:
                        link(pool.tensor_tensor(one, x_, x_, ALU.mult))
                        link(pool.tensor_tensor(total, total, one, ALU.add))
                pool.sem_inc(early_sum, 1)

            def first_lows(name):
                jb = by_name[name]
                for j in range(BY_POOL[name]):
                    st = Step(jb.first, j, 0, False)
                    wh, n = high_of(jb, st)
                    pool.wait_ge(high, split_no(jb, st) + 1)
                    pool.tensor_tensor(w_low[:, st.slot, 0:n], ring[:, st.slot, 0:n], wh.bitcast(F32), ALU.subtract)\
                        .then_inc(sem("pool_low"), 1)

            first_lows("merge")
            for q in range(PAIRS):
                pool.wait_ge(sem("merge_high"), q + 1)
                h_ = slice(2 * q, 2 * q + 2)
                pool.tensor_tensor(n_low[:, h_, :], nT[:, h_, :], n_high1[:, h_, :].bitcast(F32), ALU.subtract)\
                    .then_inc(sem("merge_low"), 1)
            pool.tensor_tensor(mix_low[:, :, :], mixT, mix_high[:, :, :].bitcast(F32), ALU.subtract).then_inc(sem("mix_low"), 1)
            early_squares("peer")
            for t in range(TT):
                for ph, rows in enumerate(("peer_u", "peer_v")):
                    src = a[rows][0]
                    numbers = ids.bitcast(U32)
                    n = (t * 2 + ph) * SLOTS
                    if (t, ph) == (1, 0):
                        pool.wait_ge(sem("pe_rows"), (SLOTS // GATHERS + 1) * len(BY_PE))

                    with pool.Fori(0, PEER_HEADS) as h:
                        pool.wait_ge(sem("ids_ready"), h + (t * PEER_HEADS + 1))
                        for row in range(TOPK):
                            k = row % GATHERS
                            if (t, ph) == (0, 1) and k in BY_PE:
                                n_pe = (row // GATHERS) * len(BY_PE) + BY_PE.index(k)
                                pool.wait_ge(sem("pe_rows"), h * (2 * len(BY_PE)) + (n_pe + 1))
                            pool.wait_ge(sem("rows_used"), h * TOPK + (n + row + 1))
                            pool.sem_inc(sem("gather_turn"), 1)
                            pool.tensor_copy(idcol[:, k:k + 1].bitcast(U32),
                                             numbers[:, t, bass.ds(h * TOPK + row, 1)]).then_inc(sem("idcol_ready"), 1)
                            pool.wait_ge(sem("idcol_ready"), h * TOPK + (n + row + 1))
                            pool.sem_inc(sem("gather_turn"), 1)
                            pool.indirect_dma_start(
                                gath[:, k, :], None, src,
                                bass.IndirectOffsetOnAxis(ap=idcol[:, k:k + 1].bitcast(U32), axis=0)
                            ).then_inc(sem(f"rows_in{k}"), 16)
            first_lows("ffn_in00")
            for name in early:
                if name in ("ffn01", "ffn11"):
                    first_lows(early[name][1])
                if name != "peer":
                    early_squares(name)
                if name in BY_POOL:
                    first_lows(name)

        @block.scalar
        def _(act):
            chain = [0]

            def link(ins):
                ins.then_inc(sem("act_chain"), 1)
                chain[0] += 1
                act.wait_ge(sem("act_chain"), chain[0])

            act.dma_start(x_in, a["x"][0].rearrange("(t p) d -> p t d", p=P)).then_inc(sem("x_in"), 16)
            for name, n in GAINS:
                src = a[name]
                if len(src.shape) > 1:
                    src = src.rearrange("a b c -> (a b c)" if len(src.shape) > 2 else "a b -> (a b)")
                act.dma_start(rows_in[GAIN_AT[name]:GAIN_AT[name] + n, :], src.rearrange("(r p) -> r p", p=P)).then_inc(sem("gains_in"), 16)
            for k, name in enumerate(("pe_k", "pe_v")):
                act.dma_start(pe_in[16 * k:16 * k + 16, :], a[name][0].rearrange("(l e) d -> l (e d)", e=2)).then_inc(sem("pe_in"), 16)
            act.dma_start(mem_in, a["mem"][0].rearrange("(t p) d -> p t d", p=P)).then_inc(sem("mem_in"), 16)
            act.dma_start(rel[0:BUCKETS, :], a["rel_bias"]).then_inc(sem("rel_in"), 16)
            act.dma_start(hot[0:BUCKETS, :], onehot).then_inc(sem("rel_in"), 16)
            for k, name in enumerate(("w_cmp_k", "w_cmp_v")):
                act.dma_start(w_cmp[:, k], a[name][0].rearrange("(l p) d -> p l d", p=P)).then_inc(sem("cmp_in"), 16)
            act.dma_start(w_grp, a["w_pool_grp"][0].rearrange("g c d -> c g d")).then_inc(sem("grp_in"), 16)

            def copy_out(dst, src):
                return act.activation(dst, src, ACT.Copy)

            def from_P(dst, cols=slice(0, 512), rows=slice(0, P)):
                chP.take(act)
                copy_out(dst, psP[rows, cols]).then_inc(chP.free, 1)

            def quads(ap):
                return ap.rearrange("p (c t) -> p c t", c=4)

            def by_chunk(ap):
                return ap[:, 0:DC * T].rearrange("p (c t) -> p c t", c=DC)

            def prepare_root():
                act.activation(unused[:, 0:1], eps[:, 0:1], ACT.Sqrt)

            def norm_root(name):
                n, src, dst, g, c = norms[name]
                if name in late and name != "first":
                    act.wait_ge(src_ready, late.index(name) + 1)
                    act.activation(squares[:, 0:c * T].rearrange("p (c t) -> p c t", c=c)[:, :, P:T], src[:, 0:c, P:T],
                                   ACT.Square).then_inc(squared_s, 1)
                chP.take(act)
                if n > 0:
                    act.wait_ge(normed, n)
                act.activation(root[:, :], psP[:, 0:T], ACT.Sqrt, scale=1.0 / (P * c), bias=eps[:, 0:1]).then_inc(rooted, 1)
                act.wait_ge(rooted, n + 1)
                act.sem_inc(chP.free, 1)

            def empties(name, body):
                jb = by_name[name]

                def one(st):
                    if jb.split:
                        high_ahead(jb, st)
                    act.wait_ge(multiplied, st.number + 1)
                    if st.per:
                        act.sem_inc(sem("act_turn"), 1)
                    body(st, bank[st.slot]).then_inc(emptied[st.slot], 1)
                panels_of(act, jb, one, ahead=2 if jb.split else 0)

            def high_part(jb, st):
                dst, n = high_of(jb, st)
                act.wait_ge(landed[st.slot], st.uses * 16 + 16)
                act.wait_ge(multiplied, st.number - 1)
                if st.per:
                    act.sem_inc(sem("act_turn"), 1)
                copy_out(dst, ring[:, st.slot, 0:n]).then_inc(high, 1)

            def high_ahead(jb, st):
                target = two_on(jb, st)
                if target:
                    high_part(*target)

            def high_of_each(name):
                panels_of(act, by_name[name], lambda st: high_ahead(by_name[name], st), ahead=2)

            def attention(key):
                base, us = unit_base[key]
                n = len(us)
                for s in range(n + 2):
                    first_part(key, s, high_part)
                    if s >= 2:
                        gu, w = base + s - 2, us[s - 2]["width"]
                        if gu >= LAG:
                            act.wait_ge(chO.full, gu - LAG + 1)
                        chP.take(act)
                        copy_out(probT[:, gu % LAG, 0:w], psP[:, 0:w]).then_inc(chP.free, 1)
                        act.wait_ge(chP.free, chP.got)
                        act.sem_inc(probs_up, 1)
                    if s < n:
                        u, gu, w = us[s], base + s, us[s]["width"]
                        act.wait_ge(biased, gu + 1)
                        half = w - 2 * P
                        for t, (lo, hi) in enumerate(((0, half), (half, w))):
                            ins = act.activation(prob[:, gu % LAG, lo:hi], soft[:, gu % LAG, lo:hi], ACT.Exp,
                                                 bias=nmax[:, gu % LAG, t:t + 1], accum_out=sums[:, gu % LAG, t:t + 1])
                        ins.then_inc(exped, 1)

            act.wait_ge(sem("consts"), 1)

            def input_T(dst):
                for t in range(TT):
                    for h in range(2):
                        chP.take(act)
                        copy_out(dst[:, 4 * h:4 * h + 4, t * P:(t + 1) * P], quads(psP[:, :])).then_inc(chP.free, 1)
                act.wait_ge(chP.free, chP.got)
                act.sem_inc(sem("inputs_T"), 1)

            input_T(xT)
            norm_root("mix")
            from_P(gains[:, :], slice(0, N_GAINS))
            from_P(peT, slice(0, 32))
            act.wait_ge(chP.free, chP.got)
            act.sem_inc(sem("gains_T"), 1)
            input_T(memT)
            act.wait_ge(sem("consts"), 2)
            chP.take(act)
            copy_out(table[0:NSA_HEADS, 0:T], psP[0:NSA_HEADS, 0:T]).then_inc(chP.free, 1)
            act.wait_ge(chP.free, chP.got)
            row = table[0:NSA_HEADS, :]
            act.dma_start(toeplitz[:, :, :], bass.AP(row.tensor, row.offset, [list(row.ap[0]), [0, P], [1, 384]]))\
                .then_inc(sem("table_out"), 16)

            def kv_out(st, bk):
                j = st.j
                if j < 2:
                    dst = (tokk, tokv)[j]
                    for par in range(2):
                        src = bk[64 * par:64 * par + 64, :].rearrange("p (c t) -> p c t", c=2)
                        copy_out(dst[0:64, par::2, :], src)
                        ins = copy_out(dst[64:128, par::2, 0:T - 1], src[:, :, 1:T])
                    return ins
                dst = (kselT, vsel, kwinT, vwin)[j - 2]
                return copy_out(dst, bk[:, :].rearrange("p (c t) -> p c t", c=2))

            empties("kv", kv_out)
            act.wait_ge(sem("table_out"), 16)
            line = toeplitz[:, :, :]
            wide = bass.AP(line.tensor, P - 1, [[383, P], [P * 384, NSA_HEADS], [1, T]])
            corner = bass.AP(line.tensor, 2 * P - 1, [[383, P], [P * 384, NSA_HEADS], [1, P]])
            act.dma_start(bias[:, :, P:3 * P], wide).then_inc(sem("bias_in"), 16)
            act.dma_start(bias[:, :, 0:P], corner).then_inc(sem("bias_in"), 16)

            norm_root("mem")

            def q_out(st, bk):
                g = st.j
                for par in range(2):
                    ins = act.activation(
                        qT[64 * (g % 2):64 * (g % 2) + 64, (g // 2) * 4 + par:(g // 2) * 4 + 4:2, :],
                        bk[64 * par:64 * par + 64, :].rearrange("p (c t) -> p c t", c=2), ACT.Copy, scale=HEAD ** -0.5)
                return ins

            empties("q", q_out)
            empties("gate_nsa", lambda st, bk: act.activation(
                gate_nsa, bk[:, :].rearrange("p (t n) -> p t n", t=TT)[:, :, 0:48], ACT.Sigmoid))

            def pairs(dst):
                return lambda st, bk: copy_out(dst[:, 2 * st.j:2 * st.j + 2, :], bk[:, :].rearrange("p (c t) -> p c t", c=2))

            def tokens(dst):
                return lambda st, bk: copy_out(dst[:, :, 256 * st.j:256 * st.j + 256], bk[:, :].rearrange("p (t n) -> p t n", t=2))

            empties("qx", pairs(qxT))
            empties("pool", pairs(uT))
            empties("kx", pairs(kxT))
            empties("vx", tokens(vx))
            chP.take(act)
            for par in range(2):
                ins = copy_out(kcT[64 * par:64 * par + 64, :, :],
                               psP[0:64, 0:4 * N_CMP].rearrange("p (g c) -> p g c", g=4)[:, par::2, :])
            ins.then_inc(chP.free, 1)
            chP.take(act)
            copy_out(vc, psP[:, 0:HEAD]).then_inc(chP.free, 1)
            act.wait_ge(chP.free, chP.got)
            act.sem_inc(sem("kc_ready"), 1)
            act.wait_ge(sem("cmp_scores"), 1)
            act.activation(scmp, scmp, ACT.Exp).then_inc(sem("cmp_exp"), 1)
            for t in range(TT):
                chP.take(act)
                copy_out(pcmpT[:, t], quads(psP[:, :])).then_inc(chP.free, 1)
            act.wait_ge(chP.free, chP.got)
            act.sem_inc(sem("pcmp_T"), 1)
            attention("nsa")
            attention("x")
            copy_out(mix_high[:, :, :], mixT)
            for q in range(PAIRS):
                copy_out(n_high1[:, 2 * q:2 * q + 2, :], nT[:, 2 * q:2 * q + 2, :]).then_inc(sem("merge_high"), 1)

            def turn_back(dst, quarters, high_too=None):
                for t in range(TT):
                    for h in range(quarters):
                        chP.take(act)
                        if high_too is not None:
                            copy_out(high_too[:, 4 * h:4 * h + 4, t * P:(t + 1) * P], quads(psP[:, :]))
                            turned_back.append(chP.got)
                        copy_out(dst[:, 4 * h:4 * h + 4, t * P:(t + 1) * P], quads(psP[:, :])).then_inc(chP.free, 1)

            turn_back(oxT, 1, ox_high)
            act.dma_start(sub_in, a["peer_sub_keys"][0].rearrange("h s k c -> k (h s) c")).then_inc(sem("sub_in"), 16)
            empties("merge", lambda st, bk: act.activation(
                merge[:, bass.ds(st.at(lambda j: 2 * j), 2), :], bk[:, :].rearrange("p (c t) -> p c t", c=2), ACT.Sigmoid))
            turn_back(nT, 2, n_high1)
            high_of_each("pool_out")
            high_of_each("x_out")
            for j in range(4):
                high_ahead(by_name["nsa_out"], Step(by_name["nsa_out"].first, j, 0, False))
                act.wait_ge(sem("merged"), j + 1)
                copy_out(n_high2[:, 2 * j:2 * j + 2, :], merge[:, 2 * j:2 * j + 2, :]).then_inc(sem("m_high"), 1)
            high_of_each("w_o")
            norm_root("peer")
            for q in range(4):
                chP.take(act)
                copy_out(subT[:, 4 * q:4 * q + 4, :], quads(psP[:, :])).then_inc(chP.free, 1)
            act.wait_ge(chP.free, chP.got)
            act.sem_inc(sem("sub_T"), 1)
            for j in range(PEER_HEADS):
                st = Step(by_name["peer_q"].first, j, 0, False)
                act.wait_ge(multiplied, st.number + 1)
                copy_out(qpT[:, 2 * j:2 * j + 2, :], bank[st.slot][:, :].rearrange("p (c t) -> p c t", c=2))\
                    .then_inc(emptied[st.slot], 1)
                if j == 1:
                    for t in range(TT):
                        for h in range(2):
                            chP.take(act)
                            copy_out(hrow[:, t, 512 * h:512 * h + 512], psP[:, :]).then_inc(chP.free, 1)
                    act.wait_ge(chP.free, chP.got)
                    act.sem_inc(sem("hrow_T"), 1)
            for t in range(TT):
                act.wait_ge(sem("best_ready"), t + 1)
                act.activation(gate[:, t], gate[:, t], ACT.Exp).then_inc(sem("gate_exp"), 1)
                act.wait_ge(sem("dots_ready"), t + 1)
                act.activation(wgt[:, t], dots[:, t], ACT.Gelu).then_inc(sem("gelu_done"), 1)
                if t == 0:
                    act.wait_ge(sem("weights"), 1)
                    with act.Fori(0, SLOTS // GATHERS) as i:
                        for n, k in enumerate(BY_PE):
                            act.wait_ge(sem("pe_rows"), i * len(BY_PE) + (n + 1))
                            act.sem_inc(sem("act_turn"), 1)
                            copy_out(wcol[:, n:n + 1], wgt[:, 0, bass.ds(i * GATHERS + k, 1)]).then_inc(sem("wcol_ready"), 1)
                            act.wait_ge(sem("wcol_ready"), i * len(BY_PE) + (n + 1))
                            act.activation(diag[:, n, :], ident[:, :], ACT.Copy, scale=wcol[:, n:n + 1])\
                                .then_inc(sem("diagonal"), 1)
                    act.wait_ge(sem("added"), 2)
                    act.activation(by_chunk(squares)[:, :, 0:P], xT[:, :, 0:P], ACT.Square).then_inc(squared_s, 1)
            act.wait_ge(sem("experts_done"), TT)
            jb = by_name["ffn_in00"]
            high_part(jb, Step(jb.first, 0, 0, False))
            act.wait_ge(sem("added"), 3)
            act.activation(by_chunk(squares)[:, 0:4, P:T], xT[:, 0:4, P:T], ACT.Square).then_inc(squared_s, 1)
            prepare_root()
            high_part(jb, Step(jb.first, 1, 0, False))
            norm_root("first")
            ffn_pairs = [0]

            def norm_high(name):
                for q in range(PAIRS):
                    act.wait_ge(norm_pair, PAIRS * whole[name] + q + 1)
                    copy_out(n_high[:, 2 * q:2 * q + 2, :], nT[:, 2 * q:2 * q + 2, :]).then_inc(sem("n_high"), 1)

            def ffn_gates(i, s_):
                jb, jo = by_name[f"ffn_in{i}{s_}"], by_name[f"ffn_out{i}{s_}"]
                k0 = ffn_pairs[0]
                ffn_pairs[0] += FC // 2
                h0 = (2 * i + s_) * (FC // 2)

                def ahead(st):
                    high_ahead(jb, st)

                def one(st):
                    pair = k0 + (st.j // 2) + (st.turn * 2 if st.per else 0)
                    if st.j % 2 == 0:
                        act.wait_ge(sem("sgate_free"), pair + 1)
                        if st.per:
                            act.sem_inc(sem("act_turn"), 1)
                        act.wait_ge(multiplied, st.number + 1)
                        act.activation(sgate[:, (st.j // 2 + k0) % 2, :], bank[st.slot][:, :], ACT.Silu)\
                            .then_inc(emptied[st.slot], 1)
                        ahead(st)
                    else:
                        ahead(st)
                        act.wait_ge(sem("hidden_pair"), h0 + st.j // 2 + 1 + (st.turn * 2 if st.per else 0))
                        if st.per:
                            act.sem_inc(sem("act_turn"), 1)
                        at_ = st.at(lambda j: 2 * (j // 2))
                        dst = h_high[:, bass.ds(at_, 2), :] if st.per else h_high[:, at_:at_ + 2, :]
                        copy_out(dst, sgate[:, (st.j // 2 + k0) % 2, :].rearrange("p (c t) -> p c t", c=2))\
                            .then_inc(sem("h_high"), 1)
                panels_of(act, jb, one, ahead=2)
                prepare_root()
                high_of_each(jo.name)

            norm_root("ffn00")
            norm_high("ffn00")
            act.wait_ge(normed, norms["first"][0] + 1)
            for i in L:
                act.dma_start(p_in[:, i], a["p_2"][i, 0].rearrange("(t p) d -> p t d", p=P)).then_inc(sem("p_in"), 16)
            act.dma_start(posi[0:ROPE, :].bitcast(I32), over_partitions(a["positions_2"], ROPE)).then_inc(sem("pos_in"), 16)
            act.dma_start(freq[0:ROPE, :], inv_freq).then_inc(sem("pos_in"), 16)
            act.dma_start(fbias, over_partitions(a["fox_b_f_2"], P)).then_inc(sem("pos_in"), 16)

            ffn_gates(0, 0)
            norm_root("mix0")
            act.wait_ge(sem("angles"), 1)
            act.activation(cosT[0:ROPE, :], ang[0:ROPE, 0, :], ACT.Sin, scale=0.5).then_inc(sem("sines"), 1)
            act.activation(sinT[0:ROPE, :], ang[0:ROPE, 0, :], ACT.Sin).then_inc(sem("sines"), 1)
            norm_root("cq")
            norm_root("ckv")

            def swap(src):
                copy_out(rope_sw[0:32, :], src[32:64, :])
                return copy_out(rope_sw[32:64, :], src[0:32, :])

            act.wait_ge(sem("rope_go"), 1)
            swap(krT).then_inc(sem("swapped"), 1)

            def uq_out(st, bk):
                h = st.j
                act.wait_ge(sem("rope_go"), h + 2)
                copy_out(q2T[:, h, :], bk[:, 0:T])
                copy_out(rope_in[0:ROPE, :], bk[0:ROPE, T:2 * T])
                return swap(bk[:, T:2 * T])

            for h in range(MLA_HEADS):
                st = Step(by_name["uq"].first, h, 0, False)
                act.wait_ge(multiplied, st.number + 1)
                uq_out(st, bank[st.slot]).then_inc(emptied[st.slot], 1)
            for h in range(MLA_HEADS):
                st = Step(by_name["ukv"].first, h, 0, False)
                act.wait_ge(multiplied, st.number + 1)
                copy_out(k2T[:, h, :], bank[st.slot][:, 0:T])
                copy_out(v2[:, :, h * P:(h + 1) * P], bank[st.slot][:, T:2 * T].rearrange("p (t n) -> p t n", t=2))\
                    .then_inc(emptied[st.slot], 1)
            for i in L:
                chP.take(act)
                copy_out(pT[:, i].rearrange("p c t -> p (c t)"), psP[:, :]).then_inc(chP.free, 1)
            act.wait_ge(chP.free, chP.got)
            for i in L:
                copy_out(p_high[:, i], pT[:, i]).then_inc(sem("p_high"), 1)
            attention("mla")
            prepare_root()
            turn_back(nT, 2, n_high)
            high_of_each("mla_o")
            norm_root("ffn01")
            norm_high("ffn01")
            ffn_gates(0, 1)
            def ple_norm(i):
                jb = by_name[f"proj{i}"]

                def leave(q):
                    bk = proj_banks(i)[chJ.take(act)]
                    copy_out(projected[:, 512 * q:512 * q + 512], bk[:, :]).then_inc(chJ.free, 1)

                norm_root(f"ple{i}")
                for q in range(3):
                    leave(q)
                norm_high(f"ple{i}")
                leave(3)
                act.wait_ge(chJ.free, chJ.got)
                act.sem_inc(emptied[jb.first % RING], 1)
                high_ahead(jb, Step(jb.first, 0, 0, False))

            def ple_gates(i):
                jb = by_name[f"ple{i}"]
                k0 = ffn_pairs[0]
                ffn_pairs[0] += 4
                for j in range(4):
                    st = Step(jb.first, j, 0, False)
                    if j < 3:
                        high_ahead(jb, st)
                    act.wait_ge(sem("sgate_free"), k0 + j + 1)
                    act.wait_ge(multiplied, st.number + 1)
                    act.activation(sgate[:, (j + k0) % 2, :], bank[st.slot][:, :], ACT.Sigmoid).then_inc(emptied[st.slot], 1)
                prepare_root()
                high_ahead(jb, st)

            ple_norm(0)
            ple_gates(0)
            norm_root("ffn10")
            norm_high("ffn10")
            ffn_gates(1, 0)
            norm_root("mix1")
            norm_high("mix1")
            empties("fq", pairs(q2T))
            empties("fk", pairs(k2T))
            empties("fv", tokens(v2))
            act.wait_ge(sem("forget"), 1)
            act.activation(ftmp[:, 1], ftmp[:, 1], ACT.Exp, scale=-1.0).then_inc(sem("fexp"), 1)
            act.wait_ge(sem("forget"), 2)
            act.activation(ftmp[:, 2], ftmp[:, 2], ACT.Ln).then_inc(sem("fexp"), 1)
            attention("fox")
            prepare_root()
            turn_back(nT, 2, n_high)
            high_of_each("fox_o")
            norm_root("ffn11")
            norm_high("ffn11")
            ffn_gates(1, 1)
            ple_norm(1)
            ple_gates(1)
            norm_root("final")
            for t in range(TT):
                for h in range(2):
                    chP.take(act)
                    copy_out(xrow[:, t, 512 * h:512 * h + 512], psP[:, :]).then_inc(sem("out_rows"), 1)
                    act.wait_ge(sem("out_rows"), 2 * t + h + 1)
                    act.sem_inc(chP.free, 1)

        @block.tensor
        def _(pe):
            def products(name, ready=None, only=None, pairs_ready=None):
                jb = by_name[name]
                if ready is not None:
                    pe.wait_ge(*ready)

                def one(st):
                    if jb.split:
                        pe.wait_ge(*low_written(jb, st))
                    else:
                        pe.wait_ge(landed[st.slot], st.uses * 16 + 16)
                    if not (isinstance(st.uses, int) and st.uses == 0):
                        pe.wait_ge(emptied[st.slot], st.uses)
                    c, w = jb.rows(st.j), jb.width
                    if jb.split:
                        wh, n = high_of(jb, st)
                        wh, wl = (x.rearrange("p (c n) -> p c n", c=c) for x in (wh, w_low[:, st.slot, 0:n]))
                        ah, al = jb.split(st.j)
                        passes = ((wh, al), (wl, ah), (wh, ah))
                    else:
                        passes = ((ring[:, st.slot, 0:c * w].rearrange("p (c n) -> p c n", c=c), jb.act(st.j)),)
                    kind = jb.kind(st.j) if callable(jb.kind) else jb.kind
                    bk = bank[st.slot]
                    groups = []
                    if kind == "F":
                        for m in range(0, w, P):
                            mw = min(P, w - m)
                            o = (m // P) * T
                            groups.append((bk[0:mw, o:o + T], lambda wt, act_, k, m=m, mw=mw: (wt[:, k, m:m + mw], act_[:, k, :])))
                    else:
                        lo = 0
                        if kind == "FT":
                            groups.append((bk[:, 0:T], lambda wt, act_, k: (wt[:, k, 0:P], act_[:, k, :])))
                            lo = P
                        for t in range(TT):
                            o = T + t * P if kind == "FT" else t * T
                            groups.append((bk[:, o:o + w - lo],
                                           lambda wt, act_, k, t=t, lo=lo: (act_[:, k, t * P:(t + 1) * P], wt[:, k, lo:w])))
                    for n_, (dst, ops) in enumerate(groups):
                        for k in range(c):
                            if pairs_ready and st.j == 0 and n_ == 0 and k % 2 == 0:
                                pe.wait_ge(pairs_ready[0], pairs_ready[1] + k // 2 + 1)
                            for i_, (wt, act_) in enumerate(passes):
                                lhs, rhs = ops(wt, act_, k)
                                mm = pe.matmul(dst, lhs, rhs, start=(k == 0 and i_ == 0), stop=(k == c - 1 and i_ == len(passes) - 1))
                    mm.then_inc(multiplied, 1)
                if only is None:
                    panels_of(pe, jb, one, peeled=RING if name in ("merge", "ffn_in00") else 0)
                else:
                    for j in only:
                        one(Step(jb.first, j, 0, False))

            def projections(i):
                jb = by_name[f"proj{i}"]
                st = Step(jb.first, 0, 0, False)
                pe.wait_ge(*low_written(jb, st))
                pe.wait_ge(emptied[st.slot], st.uses)
                wh, n = high_of(jb, st)
                wh, wl = (x.rearrange("p (c n) -> p c n", c=2) for x in (wh, w_low[:, st.slot, 0:n]))
                ah, al = jb.split(0)
                for q in range(4):
                    bk = proj_banks(i)[chJ.claim(pe)]
                    for m in range(2):
                        o = (2 * q + m) * P
                        for k in range(2):
                            for n_, (x, y) in enumerate(((wh, al), (wl, ah), (wh, ah))):
                                mm = pe.matmul(bk[:, m * T:(m + 1) * T], x[:, k, o:o + P], y[:, k, :],
                                               start=(k == 0 and n_ == 0), stop=(k == 1 and n_ == 2))
                    mm.then_inc(chJ.full, 1)
                pe.wait_ge(chJ.full, chJ.put)
                pe.sem_inc(multiplied, 1)

            def all_left(name):
                last = by_name[name].first + by_name[name].panels
                for k in range(RING):
                    pe.wait_ge(emptied[k], (last - 1 - k) // RING + 1)

            def turn(pieces):
                chP.claim(pe)
                for o, src in pieces:
                    n, m = src.shape[0], src.shape[1]
                    mm = pe.transpose(psP[0:m, o:o + n], src, ident[0:n, 0:n])
                mm.then_inc(chP.full, 1)

            def norm_sum(name):
                n, src, dst, g, c = norms[name]
                if name in late:
                    pe.wait_ge(squared_v, n + 1)
                    pe.wait_ge(squared_s, squares_by_act(name))
                    chP.claim(pe)
                    for k in range(c):
                        mm = pe.matmul(psP[:, 0:T], ones[:, :], squares[:, k * T:(k + 1) * T], start=(k == 0), stop=(k == c - 1))
                else:
                    e, after_job, width = early[name]
                    pe.wait_ge(early_sum, e + 1)
                    chP.claim(pe)
                    for k in range(width):
                        pe.matmul(psP[:, 0:T], ones[:, :], squares[:, k * T:(k + 1) * T], start=(k == 0), stop=False)
                    pe.wait_ge(squared_v, n + 1)
                    for k in range(width):
                        mm = pe.matmul(psP[:, 0:T], ones[:, :], squares[:, 1024 + k * T:1024 + (k + 1) * T], start=False,
                                       stop=(k == width - 1))
                mm.then_inc(chP.full, 1)

            def attention(key):
                base, us = unit_base[key]
                n = len(us)
                for s in range(n + LAG):
                    if s < n:
                        u = us[s]
                        ps = psS[chS.claim(pe)]
                        half = u["width"] - T
                        for t, (lo, hi) in enumerate(((0, half), (half, u["width"]))):
                            for k, (ql, kr) in enumerate(zip(u["lhs"], u["rhs"])):
                                mm = pe.matmul(ps[:, lo:hi], ql[:, t * P:(t + 1) * P], kr[:, 0:hi - lo],
                                               start=(k == 0), stop=(k == len(u["lhs"]) - 1))
                        mm.then_inc(chS.full, 1)
                    if 2 <= s < n + 2:
                        gu, w = base + s - 2, us[s - 2]["width"]
                        pe.wait_ge(exped, gu + 1)
                        turn([(o, prob[:, gu % LAG, o:o + P]) for o in range(0, w, P)])
                    if s >= LAG:
                        gu, u = base + s - LAG, us[s - LAG]
                        pe.wait_ge(probs_up, gu + 1)
                        lo = chO.claim(pe) * T
                        dv = u["v"][0].shape[1]
                        for t, pieces in SEGS[u["width"]]:
                            for k, (c, kt) in enumerate(pieces):
                                mm = pe.matmul(psO[:, lo + t * dv:lo + (t + 1) * dv], probT[:, gu % LAG, c * P:(c + 1) * P],
                                               u["v"][kt], start=(k == 0), stop=(k == len(pieces) - 1))
                        mm.then_inc(chO.full, 1)

            def rows_to_T(src, blocks):
                for t in range(TT):
                    for q in range(blocks // 4):
                        turn([(j * P, src[:, t, (4 * q + j) * P:(4 * q + j + 1) * P]) for j in range(4)])

            pe.wait_ge(sem("consts"), 1)
            pe.wait_ge(sem("x_in"), 16)
            rows_to_T(x_in, 8)
            norm_sum("mix")
            pe.wait_ge(sem("gains_in"), 16 * len(GAINS))
            turn([(0, rows_in[0:N_GAINS, :])])
            pe.wait_ge(sem("pe_in"), 32)
            turn([(0, pe_in[0:32, :])])
            pe.wait_ge(sem("mem_in"), 16)
            rows_to_T(mem_in, 8)
            pe.wait_ge(sem("rel_in"), 32)
            chP.claim(pe)
            pe.matmul(psP[0:NSA_HEADS, 0:T], rel[0:BUCKETS, :], hot[0:BUCKETS, :], start=True, stop=True).then_inc(chP.full, 1)
            products("kv", pairs_ready=(norm_pair, PAIRS * whole["mix"]))
            norm_sum("mem")
            products("q")
            products("gate_nsa")
            products("qx")
            products("pool")
            products("kx", (normed, norms["mem"][0] + 1))
            products("vx")
            pe.wait_ge(sem("consts"), 2)
            pe.wait_ge(sem("blocks"), 2)
            pe.wait_ge(sem("cmp_in"), 32)
            chP.claim(pe)
            for l in range(LP):
                mm = pe.matmul(psP[0:HEAD, 0:4 * N_CMP], w_cmp[:, 0, l, :], blkk[:, l, :, 0:N_CMP], start=(l == 0), stop=(l == LP - 1))
            mm.then_inc(chP.full, 1)
            chP.claim(pe)
            for l in range(LP):
                mm = pe.matmul(psP[:, 0:HEAD], blkv[:, l].rearrange("p g c -> p (g c)"), w_cmp[:, 1, l, :],
                               start=(l == 0), stop=(l == LP - 1))
            mm.then_inc(chP.full, 1)
            pe.wait_ge(sem("kc_ready"), 1)
            all_left("vx")
            for par in range(2):
                ps = psS[chS.claim(pe)]
                lo = HEAD * par
                for t in range(TT):
                    for g in (par, par + 2):
                        for r in range(HEADS_PER_GROUP):
                            o = (t * NSA_HEADS + g * HEADS_PER_GROUP + r) * 16
                            mm = pe.matmul(ps[:, o:o + N_CMP], qT[lo:lo + HEAD, (g // 2) * 4 + r, t * P:(t + 1) * P],
                                           kcT[lo:lo + HEAD, g // 2, :], start=True, stop=True)
                mm.then_inc(chS.full, 1)
            pe.wait_ge(sem("cmp_probs"), 1)
            for t in range(TT):
                turn([(r * P, pcmp[:, t, r].rearrange("p g c -> p (g c)")) for r in range(4)])
            pe.wait_ge(sem("pcmp_T"), 1)
            for g in range(NSA_GROUPS):
                ps = psS[chS.claim(pe)]
                lo = CMP_SLOT * g
                for t in range(TT):
                    for r in range(HEADS_PER_GROUP):
                        o = t * T + r * HEAD
                        mm = pe.matmul(ps[:, o:o + HEAD], pcmpT[lo:lo + N_CMP, t, r, :], vc[lo:lo + N_CMP, :],
                                       start=True, stop=True)
                mm.then_inc(chS.full, 1)
            pe.wait_ge(sem("pooled"), 1)
            pe.wait_ge(sem("grp_in"), 16)
            for half in range(2):
                ps = psS[chS.claim(pe)]
                for g in (2 * half, 2 * half + 1):
                    mm = pe.matmul(ps[:, (g % 2) * T:(g % 2 + 1) * T], w_grp[:, g, :], uT[:, g, :], start=True, stop=True)
                mm.then_inc(chS.full, 1)
            pe.wait_ge(sem("bias_in"), 32)
            attention("nsa")
            attention("x")
            pe.wait_ge(sem("attended"), 1)
            rows_to_T(o_x, 4)
            products("merge", (sem("merge_low"), PAIRS))
            rows_to_T(o_nsa, 8)
            products("pool_out", (sem("mix_low"), 1))
            products("x_out", (sem("o_low"), 2))
            products("nsa_out", (sem("o_low"), 6))
            products("w_o", pairs_ready=(sem("m_low"), 0))
            norm_sum("peer")
            q_first = by_name["peer_q"].first

            def key_scores(t, pair):
                ps = psS[chS.claim(pe)]
                for j in range(4):
                    c = 4 * pair + j
                    mm = pe.matmul(ps[:, j * P:(j + 1) * P], qpT[:, c, t * P:(t + 1) * P], subT[:, c, :], start=True, stop=True)
                mm.then_inc(chS.full, 1)

            def queries_left(pair):
                for n in (q_first + 2 * pair, q_first + 2 * pair + 1):
                    pe.wait_ge(emptied[n % RING], n // RING + 1)

            pe.wait_ge(sem("sub_in"), 16)
            for q in range(4):
                turn([(j * P, sub_in[:, 4 * q + j, :]) for j in range(4)])
            products("peer_q", None, range(2), (norm_pair, PAIRS * whole["peer"]))
            pe.wait_ge(sem("sub_T"), 1)
            queries_left(0)
            key_scores(0, 0)
            for t in range(TT):
                for q in range(2):
                    turn([(j * P, nT[:, 4 * q + j, t * P:(t + 1) * P]) for j in range(4)])
            for pair in range(1, PEER_HEADS // 2):
                products("peer_q", None, range(2 * pair, 2 * pair + 2))
                queries_left(pair)
                key_scores(0, pair)
            for pair in range(2):
                key_scores(1, pair)
            pe.sem_inc(sem("pe_rows"), len(BY_PE))

            def row_sum(lhs, rhs, start, stop):
                for q in range(2):
                    mm = pe.matmul(bank[q][:, :], lhs, rhs[:, 512 * q:512 * q + 512] if rhs.shape[-1] > 512 else rhs,
                                   start=start, stop=stop)
                return mm

            row_sum(zeros[:, 0:P], zeros[:, :], True, False)
            ROUNDS = SLOTS // GATHERS
            for pair in range(PEER_HEADS // 2):
                done = pair * ROUNDS // 4
                with pe.Fori(0, ROUNDS // 4) as i:
                    for n, k in enumerate(BY_PE):
                        pe.wait_ge(sem(f"rows_in{k}"), i * 16 + 16 * (ROUNDS + done + 1))
                        pe.wait_ge(sem("diagonal"), i * len(BY_PE) + (done * len(BY_PE) + n + 1))
                        row_sum(diag[:, n, :], gath[:, k, :], False, False).then_inc(sem("pe_rows"), 1)
                if pair < 2:
                    key_scores(1, pair + 2)
            row_sum(zeros[:, 0:P], zeros[:, :], False, True).then_inc(sem("pe_sum"), 1)
            for t in range(TT):
                pe.wait_ge(sem("experts_done"), t + 1)
                for q in range(2):
                    ps = psS[chS.claim(pe)]
                    for j in range(4):
                        mm = pe.transpose(ps[:, j * P:(j + 1) * P], yacc[:, t, (4 * q + j) * P:(4 * q + j + 1) * P], ident[:, :])
                    mm.then_inc(chS.full, 1)
                pe.wait_ge(squared_s, squares_by_act("first") - 1 + t)
                if t == 0:
                    chP.claim(pe)
                for k in range(DC):
                    if t == TT - 1 and k == 4:
                        pe.wait_ge(squared_v, norms["first"][0] + 1)
                    mm = pe.matmul(psP[:, t * P:(t + 1) * P], ones[:, :], squares[:, k * T + t * P:k * T + (t + 1) * P],
                                   start=(k == 0), stop=(k == DC - 1))
            mm.then_inc(chP.full, 1)

            def ffn(i, s):
                n = f"ffn{i}{s}"
                norm_sum(n)
                products(f"ffn_in{i}{s}", pairs_ready=(sem("n_low"), PAIRS * split_norms.index(n)))
                products(f"ffn_out{i}{s}", pairs_ready=(sem("h_low"), (2 * i + s) * (FC // 2)))

            ffn(0, 0)
            norm_sum("mix0")
            products("cq", pairs_ready=(norm_pair, PAIRS * whole["mix0"]))
            products("ckv")
            norm_sum("cq")
            norm_sum("ckv")
            products("uq", (normed, norms["cq"][0] + 1))
            products("ukv", (normed, norms["ckv"][0] + 1))

            all_left("ukv")
            pe.wait_ge(sem("rope_go"), 2 + MLA_HEADS)
            pe.wait_ge(sem("p_in"), 32)
            for i in L:
                turn([(c * T + t * P, p_in[:, i, t, c * P:(c + 1) * P]) for c in range(2) for t in range(TT)])
            attention("mla")
            pe.wait_ge(sem("attended"), 2)
            rows_to_T(o2, 8)
            products("mla_o", (sem("o_low"), 10))
            ffn(0, 1)
            norm_sum("ple0")
            pe.wait_ge(sem("p_low"), 2)
            projections(0)
            products("ple0", pairs_ready=(sem("n_low"), PAIRS * split_norms.index("ple0")))
            ffn(1, 0)
            norm_sum("mix1")
            products("fq", pairs_ready=(sem("n_low"), PAIRS * split_norms.index("mix1")))
            products("fk")
            products("fv")
            products("ff")
            pe.wait_ge(sem("forget"), 3)
            ps = psS[chS.claim(pe)]
            for t in range(TT):
                for j in range(t + 1):
                    mm = pe.matmul(ps[:, t * FOX_HEADS:(t + 1) * FOX_HEADS], tri[:, j, t * P:(t + 1) * P], logf[:, j, :],
                                   start=(j == 0), stop=(j == t))
            mm.then_inc(chS.full, 1)
            pe.wait_ge(sem("forget"), 4)
            for h2 in range(FOX_HEADS // 2):
                ps = psS[chS.claim(pe)]
                for j in range(2):
                    h = 2 * h2 + j
                    for t in range(TT):
                        mm = pe.matmul(ps[:, j * T:(j + 1) * T], logf_wide[:, t, h * P:(h + 1) * P], tri[:, t, :],
                                       start=(t == 0), stop=(t == TT - 1))
                mm.then_inc(chS.full, 1)
            all_left("ff")
            attention("fox")
            pe.wait_ge(sem("attended"), 3)
            rows_to_T(o2, 8)
            products("fox_o", (sem("o_low"), 14))
            ffn(1, 1)
            norm_sum("ple1")
            projections(1)
            products("ple1", pairs_ready=(sem("n_low"), PAIRS * split_norms.index("ple1")))
            norm_sum("final")
            pe.wait_ge(normed, norms["final"][0] + 1)
            for t in range(TT):
                for q in range(2):
                    turn([(j * P, xT[:, 4 * q + j, t * P:(t + 1) * P]) for j in range(4)])

        @block.vector
        def _(dve):
            chain = [0]

            def link(ins):
                ins.then_inc(sem("dve_chain"), 1)
                chain[0] += 1
                dve.wait_ge(sem("dve_chain"), chain[0])

            def tt(o, x, y, op):
                return dve.tensor_tensor(o, x, y, op)

            def ts(o, x, s1, op0, s2=None, op1=None):
                return dve.tensor_scalar(o, x, s1, s2, op0, op1) if op1 is not None else dve.tensor_scalar(o, x, s1, None, op0)

            def stt(o, x, s, y, op0, op1):
                return dve.scalar_tensor_tensor(out=o, in0=x, scalar=s, in1=y, op0=op0, op1=op1)

            def do_norm(name):
                n, src, dst, g, c = norms[name]
                sq = squares[:, 0:c * T].rearrange("p (c t) -> p c t", c=c)
                if name == "first":
                    dve.sem_inc(src_ready, 1)
                    tt(sq[:, 4:8, P:T], src[:, 4:8, P:T], src[:, 4:8, P:T], ALU.mult).then_inc(squared_v, 1)
                elif name in late:
                    dve.sem_inc(src_ready, 1)
                    tt(sq[:, :, 0:P], src[:, 0:c, 0:P], src[:, 0:c, 0:P], ALU.mult).then_inc(squared_v, 1)
                else:
                    width = early[name][2]
                    x_ = src[:, c - width:c, :]
                    tt(squares[:, 1024:1024 + width * T].rearrange("p (c t) -> p c t", c=width), x_, x_, ALU.mult)\
                        .then_inc(squared_v, 1)
                dve.wait_ge(rooted, n + 1)
                link(dve.reciprocal(rstd[:, :], root[:, :]))
                if name == "mix":
                    dve.wait_ge(sem("gains_T"), 1)

                def low_half(q):
                    lows[0] += 1
                    dve.wait_ge(sem("n_high"), lows[0])
                    h_ = slice(2 * q, 2 * q + 2)
                    tt(n_low[:, h_, :], nT[:, h_, :], n_high[:, h_, :].bitcast(F32), ALU.subtract).then_inc(sem("n_low"), 1)

                for k in range(c):
                    ins = stt(dst[:, k, :], src[:, k, :], gains[:, g + k:g + k + 1], rstd[:, :], ALU.mult, ALU.mult)
                    if c == DC and k % 2 and k < c - 1:
                        ins.then_inc(norm_pair, 1)
                    if name in split_norms and k % 2 and k > 1:
                        low_half(k // 2 - 1)
                ins.then_inc(normed, 1)
                dve.wait_ge(normed, n + 1)
                if c == DC:
                    dve.sem_inc(norm_pair, 1)
                if name in split_norms:
                    low_half(PAIRS - 1)

            lows = [0]

            def low_part(jb, st):
                wh, n = high_of(jb, st)
                dve.wait_ge(high, split_no(jb, st) + 1)
                tt(w_low[:, st.slot, 0:n], ring[:, st.slot, 0:n], wh.bitcast(F32), ALU.subtract).then_inc(low, 1)

            def low_ahead(jb, st):
                target = two_on(jb, st)
                if target:
                    low_part(*target)

            def low_after(name):
                low_ahead(by_name[name], Step(by_name[name].first, by_name[name].panels - 1, 0, False))

            def o_low(n, high, whole=nT, low_=n_low):
                for t in range(TT):
                    for h in range(whole.shape[1] // 4):
                        n += 1
                        dve.wait_ge(chP.free, turned_back[n - 1])
                        x_ = (slice(0, P), slice(4 * h, 4 * h + 4), slice(t * P, (t + 1) * P))
                        tt(low_[x_], whole[x_], high[x_].bitcast(F32), ALU.subtract).then_inc(sem("o_low"), 1)

            def empties(name, body):
                jb = by_name[name]

                def one(st):
                    if jb.split and st.j < jb.panels - 1:
                        low_ahead(jb, st)
                    dve.wait_ge(multiplied, st.number + 1)
                    body(st, bank[st.slot]).then_inc(emptied[st.slot], 1)
                panels_of(dve, jb, one, ahead=2 if jb.split else 0)

            def settle(name):
                last = by_name[name].first + by_name[name].panels
                for k in range(RING):
                    dve.wait_ge(emptied[k], (last - 1 - k) // RING + 1)

            def halves(ap):
                return ap.rearrange("p (c t) -> p c t", c=2)

            def attention(key):
                base, us = unit_base[key]
                n = len(us)
                for s in range(n + LAG):
                    if s >= LAG:
                        gu, u = base + s - LAG, us[s - LAG]
                        sl = gu % LAG
                        dve.wait_ge(exped, gu + 1)
                        link(dve.reciprocal(inv[:, sl, :], sums[:, sl, :]))
                        scal = inv
                        if u["kind"] == "gated":
                            link(tt(coef[:, sl, :], inv[:, sl, :], u["extra"], ALU.mult))
                            scal = coef
                    if s < n:
                        v, gv, w = us[s], base + s, us[s]["width"]
                        sl = gv % LAG
                        ps = psS[chS.take(dve)]
                        stt(soft[:, sl, 0:w], ps[:, 0:w], v["scale"], v["mask"][:, 0:w], ALU.mult, ALU.add).then_inc(chS.free, 1)
                        dve.wait_ge(chS.free, chS.got)
                        half = w - T
                        segs = ((0, half), (half, w))
                        if v["kind"] == "fox":
                            for t, (lo, hi) in enumerate(segs):
                                ins = stt(soft[:, sl, lo:hi], soft[:, sl, lo:hi], v["extra"][:, t:t + 1], causal[:, lo:hi],
                                          ALU.add, ALU.add)
                            link(ins)
                        for t, (lo, hi) in enumerate(segs):
                            ins = dve.tensor_reduce(nmax[:, sl, t:t + 1], soft[:, sl, lo:hi], AX_X, ALU.max, negate=True)
                        ins.then_inc(biased, 1)
                    if s >= LAG:
                        sl = gu % LAG
                        lo = chO.take(dve) * T
                        dv = u["v"][0].shape[1]
                        for t in range(TT):
                            src = psO[:, lo + t * dv:lo + (t + 1) * dv]
                            if u["kind"] == "gated":
                                ins = stt(u["outs"][t], src, scal[:, sl, t:t + 1], u["outs"][t], ALU.mult, ALU.add)
                            else:
                                ins = ts(u["outs"][t], src, scal[:, sl, t:t + 1], ALU.mult)
                        ins.then_inc(chO.free, 1)
                dve.wait_ge(chO.free, chO.got)

            link(dve.memset(rstd[:, 0:1], 0.0))
            dve.sem_inc(sem("sgate_free"), 2)
            dve.sem_inc(sem("rows_used"), GATHERS)
            dve.wait_ge(sem("inputs_T"), 1)
            do_norm("mix")

            dve.wait_ge(multiplied, 1)
            for k, (tok_, blk) in enumerate(((tokk, blkk), (tokv, blkv))):
                dve.wait_ge(emptied[k], 1)
                if k == 0:
                    dve.wait_ge(sem("consts"), 2)
                for g in range(NSA_GROUPS):
                    src = tok_[:, g, :]
                    win = bass.AP(src.tensor, src.offset, [list(src.ap[0]), [2, LP], [CMP_STRIDE, N_CMP]])
                    pe_ = peT[:, 16 * k:16 * k + 16]
                    peb = bass.AP(pe_.tensor, pe_.offset, [list(pe_.ap[0]), [1, LP], [0, N_CMP]])
                    ins = tt(blk[:, :, g, 0:N_CMP], win, peb, ALU.add)
                ins.then_inc(sem("blocks"), 1)

            dve.wait_ge(sem("inputs_T"), 2)
            do_norm("mem")

            last = by_name["pool"]
            dve.wait_ge(emptied[(last.first) % RING], last.first // RING + 1)
            dve.wait_ge(emptied[(last.first + 1) % RING], (last.first + 1) // RING + 1)
            link(dve.reciprocal(icount, icount))
            for g, win in enumerate((2, 4, 8, 16)):
                src, step = uT[:, g, :], 1
                bufs = (mixT[:, 0, :], mixT[:, 1, :])
                n = 0
                while step < win:
                    dst = bufs[n % 2]
                    tt(dst[:, step:T], src[:, step:T], src[:, 0:T - step], ALU.add)
                    link(dve.tensor_copy(dst[:, 0:step], src[:, 0:step]))
                    src, step, n = dst, 2 * step, n + 1
                link(tt(mixT[:, 2, 0:win], src[:, 0:win], icount[:, 0:win], ALU.mult))
                tt(uT[:, g, 0:win], mixT[:, 2, 0:win], uT[:, g, 0:win], ALU.subtract)
                link(stt(uT[:, g, win:T], src[:, win:T], 1.0 / win, uT[:, g, win:T], ALU.mult, ALU.subtract))
            dve.sem_inc(sem("pooled"), 1)

            dve.wait_ge(sem("bias_in"), 32)
            b = bcmp.rearrange("p (t h) c -> p t h c", t=TT)
            dve.tensor_copy(b[:, 0, :, 0:7], bias[:, :, CMP_LEN - 1:P:CMP_STRIDE])
            link(dve.tensor_copy(b[:, 1, :, 0:N_CMP], bias[:, :, P + CMP_LEN - 1:3 * P:CMP_STRIDE]))
            for par in range(2):
                def mine(ap, c):
                    return ap.rearrange("p (n e r) c -> p n e r c", e=2, r=4)[:, :, par, :, 0:c]
                ps = psS[chS.take(dve)]
                tt(mine(scmp, N_CMP), mine(ps[:, :].rearrange("p (n c) -> p n c", c=16), N_CMP), mine(bcmp, N_CMP),
                   ALU.add).then_inc(chS.free, 1)
            dve.wait_ge(chS.free, chS.got)
            link(dve.tensor_reduce(cstat[:, 0], scmp, AX_X, ALU.max))

            def over_c(ap):
                return bass.AP(ap.tensor, ap.offset, [list(ap.ap[0]), [1, 32], [0, N_CMP]])

            tt(scmp, scmp, over_c(cstat[:, 0]), ALU.subtract).then_inc(sem("cmp_scores"), 1)
            dve.wait_ge(sem("cmp_exp"), 1)
            link(dve.tensor_reduce(cstat[:, 1], scmp, AX_X, ALU.add))
            link(dve.reciprocal(cstat[:, 2], cstat[:, 1]))
            c2 = cstat[:, 2].rearrange("p (t h) -> p t h", t=TT)
            c3 = cstat[:, 3].rearrange("p (t h) -> p t h", t=TT)
            g_last = by_name["gate_nsa"].first
            dve.wait_ge(emptied[g_last % RING], g_last // RING + 1)
            link(tt(c3, c2, gate_nsa[:, :, 0:NSA_HEADS], ALU.mult))
            link(ts(c3[:, 0], c3[:, 0], has[:, 0:1], ALU.mult))
            link(tt(scmp, scmp, over_c(cstat[:, 3]), ALU.mult))
            s5 = scmp.rearrange("p (t g r) c -> p t g r c", t=TT, g=4)
            for t in range(TT):
                for r in range(4):
                    ins = dve.tensor_copy(pcmp[:, t, r, :, 0:N_CMP], s5[:, t, :, r, :])
            ins.then_inc(sem("cmp_probs"), 1)
            for g in range(NSA_GROUPS):
                ps = psS[chS.take(dve)]
                dve.tensor_copy(o_nsa[:, :, 256 * g:256 * g + 256], halves(ps[:, :])).then_inc(chS.free, 1)
            for half in range(2):
                ps = psS[chS.take(dve)]
                for g in (2 * half, 2 * half + 1):
                    at_ = GAIN_AT["pool_scale"] + g
                    ins = ts(mixT[:, g, :], ps[:, (g % 2) * T:(g % 2 + 1) * T], gains[:, at_:at_ + 1], ALU.mult)
                ins.then_inc(chS.free, 1)
            dve.wait_ge(chS.free, chS.got)
            attention("nsa")
            attention("x")
            dve.sem_inc(sem("attended"), 1)

            def by_gate(branch):
                def body(st, bk):
                    return tt(merge[:, 8 * branch + 2 * st.j:8 * branch + 2 * st.j + 2, :], halves(bk[:, :]),
                              merge[:, 8 * branch + 2 * st.j:8 * branch + 2 * st.j + 2, :], ALU.mult)
                return body

            o_low(0, ox_high, oxT, ox_low)
            panels_of(dve, by_name["merge"], lambda st: low_ahead(by_name["merge"], st), ahead=2)
            o_low(2, n_high1)
            m_last = by_name["merge"].first + 11
            for k in range(RING):
                dve.wait_ge(emptied[k], (m_last - k) // RING + 1)
            empties("pool_out", by_gate(0))
            low_after("pool_out")
            empties("x_out", by_gate(2))
            settle("x_out")
            tt(merge[:, 0:8, :], merge[:, 0:8, :], merge[:, 16:24, :], ALU.add).then_inc(sem("two_merged"), 1)
            dve.wait_ge(sem("two_merged"), 1)
            low_after("x_out")

            def m_part(j):
                dve.wait_ge(sem("m_high"), j + 1)
                h_ = slice(2 * j, 2 * j + 2)
                tt(m_low[:, h_, :], merge[:, h_, :], n_high2[:, h_, :].bitcast(F32), ALU.subtract).then_inc(sem("m_low"), 1)

            for j in range(4):
                st = Step(by_name["nsa_out"].first, j, 0, False)
                if j < 3:
                    low_ahead(by_name["nsa_out"], st)
                dve.wait_ge(multiplied, st.number + 1)
                by_gate(1)(st, bank[st.slot]).then_inc(emptied[st.slot], 1)
                dve.wait_ge(emptied[st.slot], st.uses + 1)
                h_ = slice(2 * j, 2 * j + 2)
                tt(merge[:, h_, :], merge[:, h_, :], merge[:, 8 + 2 * j:10 + 2 * j, :], ALU.add).then_inc(sem("merged"), 1)
                if j:
                    m_part(j - 1)
            m_part(3)
            low_after("nsa_out")

            def add_pair(scale):
                def body(st, bk):
                    x_ = xT[:, 2 * st.j:2 * st.j + 2, :]
                    return stt(x_, halves(bk[:, :]), scale, x_, ALU.mult, ALU.add)
                return body

            empties("w_o", add_pair(1.0))
            settle("w_o")
            do_norm("peer")

            it = iota16

            key_bank = [None]

            def choose(t, h, between=None):
                steps = [0]

                def link(ins):
                    ins.then_inc(sem("dve_chain"), 1)
                    chain[0] += 1
                    written = chain[0]
                    if between:
                        between(steps[0])
                    steps[0] += 1
                    dve.wait_ge(sem("dve_chain"), written)

                if h % 2 == 0:
                    key_bank[0] = psS[chS.take(dve)]
                sides = range(2)
                row = [key_bank[0][:, (2 * (h % 2) + s) * P:(2 * (h % 2) + s + 1) * P] for s in sides]
                rest = [stop_[:, s * P:(s + 1) * P] for s in sides]
                first, second = slice(0, 8), slice(8, 16)
                dve.max(ktop[:, h, 0, first], row[0])
                link(dve.max(ktop[:, h, 1, first], row[1]))
                for s in sides:
                    dve.max_index(kidx[:, h, s, first].bitcast(U32), ktop[:, h, s, first], row[s])
                dve.match_replace(rest[0], ktop[:, h, 0, first], row[0], -3.0e38)
                ins = dve.match_replace(rest[1], ktop[:, h, 1, first], row[1], -3.0e38)
                link(ins)
                if h % 2:
                    dve.sem_inc(chS.free, 1)
                dve.max(ktop[:, h, 0, second], rest[0])
                link(dve.max(ktop[:, h, 1, second], rest[1]))
                x0, x1 = ktop[:, h, 0, :], ktop[:, h, 1, :]
                ap0 = bass.AP(x0.tensor, x0.offset, [list(x0.ap[0]), [1, 16], [0, 16]])
                ap1 = bass.AP(x1.tensor, x1.offset, [list(x1.ap[0]), [0, 16], [1, 16]])
                tt(cand[:, h], ap0, ap1, ALU.add)
                dve.max_index(kidx[:, h, 0, second].bitcast(U32), ktop[:, h, 0, second], rest[0])
                link(dve.max_index(kidx[:, h, 1, second].bitcast(U32), ktop[:, h, 1, second], rest[1]))
                sums_ = cand[:, h].rearrange("p a b -> p (a b)")
                dve.tensor_copy(kidf[:, h], kidx[:, h].bitcast(U32))
                link(dve.max(best[:, h, first], sums_))
                dve.max_index(bpos[:, h, first].bitcast(U32), best[:, h, first], sums_)
                link(dve.match_replace(cand2[:, h], best[:, h, first], sums_, -3.0e38))
                link(dve.max(best[:, h, second], cand2[:, h]))
                link(dve.max_index(bpos[:, h, second].bitcast(U32), best[:, h, second], cand2[:, h]))
                bp = bpos[:, h, :].bitcast(U32)
                mine_ = slice(h * TOPK, (h + 1) * TOPK)
                ts(bhalf[:, 0, mine_].bitcast(U32), bp, 4, ALU.logical_shift_right)
                link(ts(bhalf[:, 1, mine_].bitcast(U32), bp, 15, ALU.bitwise_and))
                link(dve.tensor_copy(bhalff[:, :, mine_], bhalf[:, :, mine_].bitcast(U32)))
                e4 = eq[:, 0:2 * TOPK * TOPK].rearrange("p (s k c) -> p s k c", s=2, k=TOPK)
                x_, k_ = bhalff[:, :, mine_], kidf[:, h]
                pos_b = bass.AP(x_.tensor, x_.offset, [list(x_.ap[0]), [P, 2], [1, TOPK], [0, TOPK]])
                io_b = bass.AP(it.tensor, it.offset, [list(it.ap[0]), [0, 2], [0, TOPK], [1, TOPK]])
                num_b = bass.AP(k_.tensor, k_.offset, [list(k_.ap[0]), [TOPK, 2], [0, TOPK], [1, TOPK]])
                link(tt(e4, pos_b, io_b, ALU.is_equal))
                link(tt(e4, e4, num_b, ALU.mult))
                link(dve.tensor_reduce(which[:, :, mine_], e4, AX_X, ALU.add))
                link(stt(idf[:, mine_], which[:, 0, mine_], float(KEYS), which[:, 1, mine_], ALU.mult, ALU.add))
                dve.tensor_copy(ids[:, t, mine_].bitcast(U32), idf[:, mine_]).then_inc(sem("ids_ready"), 1)
                return steps[0]

            def gates_of(t):
                g3 = gate[:, t].rearrange("p (h k) -> p h k", h=8)
                b0 = best[:, :, 0:1]
                top_b = bass.AP(b0.tensor, b0.offset, [list(b0.ap[0]), [16, 8], [0, 16]])
                tt(g3, best, top_b, ALU.subtract).then_inc(sem("best_ready"), 1)
                dve.wait_ge(sem("gate_exp"), t + 1)
                link(dve.tensor_reduce(gsum, g3, AX_X, ALU.add))
                link(dve.reciprocal(gsum, gsum))
                gs_b = bass.AP(gsum.tensor, gsum.offset, [list(gsum.ap[0]), [1, 8], [0, 16]])
                link(tt(g3, g3, gs_b, ALU.mult))

            ROUNDS = SLOTS // GATHERS
            PER_HEAD = TOPK // GATHERS

            def dot_rows(t, lo, rounds):
                before = 2 * t * ROUNDS + lo
                with dve.Fori(0, rounds) as i:
                    for k in range(GATHERS):
                        dve.wait_ge(sem(f"rows_in{k}"), i * 16 + 16 * (before + 1))
                        dve.tensor_tensor_reduce(gath[:, k, :], gath[:, k, :], hrow[:, t, :], 1.0, 0.0, ALU.mult, ALU.add,
                                                 dcol[:, k:k + 1]).then_inc(sem("rows_used"), 1)
                    dve.wait_ge(sem("rows_used"), i * GATHERS + (before + 2) * GATHERS)
                    dve.tensor_copy(dots[:, t, bass.ds(i * GATHERS + lo * GATHERS, GATHERS)], dcol).then_inc(sem("dots_part"), 1)
                    dve.wait_ge(sem("dots_part"), i + (lo + 1))

            def dot_row(t, h, row):
                if row >= TOPK:
                    return
                n = h * TOPK + row
                k = n % GATHERS
                dve.wait_ge(sem(f"rows_in{k}"), 16 * (2 * t * ROUNDS + n // GATHERS + 1))
                dve.tensor_tensor_reduce(gath[:, k, :], gath[:, k, :], hrow[:, t, :], 1.0, 0.0, ALU.mult, ALU.add,
                                         dots[:, t, n:n + 1]).then_inc(sem("rows_used"), 1)

            def sum_rows(t, lo, rounds, others=(), odd=None):
                before = (2 * t + 1) * ROUNDS + lo
                with dve.Fori(0, rounds) as i:
                    for k in range(GATHERS):
                        if k in others:
                            dve.sem_inc(sem("rows_used"), 1)
                            continue
                        dve.wait_ge(sem(f"rows_in{k}"), i * 16 + 16 * (before + 1))
                        y_ = yacc[:, t, :] if odd is None or k % 2 == 0 else odd
                        stt(y_, gath[:, k, :], wgt[:, t, bass.ds(i * GATHERS + (lo * GATHERS + k), 1)], y_,
                            ALU.mult, ALU.add).then_inc(sem("rows_used"), 1)
                        dve.wait_ge(sem("rows_used"), i * GATHERS + ((before + 1) * GATHERS + k + (odd is None)))

            AHEAD = 2
            for h in range(AHEAD):
                choose(0, h)
            dve.wait_ge(sem("hrow_T"), 1)
            for t in range(TT):
                if t == 0:
                    for h in range(PEER_HEADS):
                        done = 0
                        if h + AHEAD < PEER_HEADS:
                            for done in range(2):
                                dot_row(t, h, done)
                            done = 2 + choose(t, h + AHEAD, lambda n: dot_row(t, h, n + 2))
                        for row in range(done, TOPK):
                            dot_row(t, h, row)
                    dve.wait_ge(sem("rows_used"), SLOTS + GATHERS)
                else:
                    dot_rows(t, 0, ROUNDS)
                dve.sem_inc(sem("dots_ready"), 1)
                gates_of(t)
                dve.wait_ge(sem("gelu_done"), t + 1)
                link(tt(wgt[:, t], wgt[:, t], gate[:, t], ALU.mult))
                dve.sem_inc(sem("weights"), 1)
                link(dve.memset(yacc[:, t], 0.0))
                if t == 0:
                    for h in range(PEER_HEADS):
                        choose(1, h)
                        sum_rows(t, h * PER_HEAD, PER_HEAD, BY_PE)
                    dve.wait_ge(sem("pe_sum"), 1)
                    for q in range(2):
                        y_ = yacc[:, t, 512 * q:512 * q + 512]
                        link(tt(y_, bank[q][:, :], y_, ALU.add))
                else:
                    odd = cand.rearrange("p h a b -> p (h a b)")[:, 0:D]
                    link(dve.memset(odd, 0.0))
                    sum_rows(t, 0, ROUNDS, odd=odd)
                    dve.wait_ge(sem("rows_used"), (4 * ROUNDS + 1) * GATHERS)
                    link(tt(yacc[:, t, :], yacc[:, t, :], odd, ALU.add))
                dve.sem_inc(sem("experts_done"), 1)
                for q in range(2):
                    ps = psS[chS.take(dve)]
                    x_ = xT[:, 4 * q:4 * q + 4, t * P:(t + 1) * P]
                    tt(x_, ps[:, :].rearrange("p (c t) -> p c t", c=4), x_, ALU.add).then_inc(chS.free, 1)
                    dve.wait_ge(chS.free, chS.got)
                    dve.sem_inc(sem("added"), 1)
            do_norm("first")

            pairs_done = [0]

            def ffn(i, s):
                jb, jo = by_name[f"ffn_in{i}{s}"], by_name[f"ffn_out{i}{s}"]
                k0 = pairs_done[0]
                pairs_done[0] += FC // 2
                h0 = (2 * i + s) * (FC // 2)

                def ahead(st):
                    low_ahead(jb, st)

                def one(st):
                    if st.j % 2 == 0:
                        ahead(st)
                        return
                    gate_slot = (st.slot - 1) % RING
                    g_uses = (jb.first + st.j - 1) // RING + 1
                    more = st.turn * 2 if st.per else 0
                    dve.wait_ge(emptied[gate_slot], st.turn + g_uses)
                    dve.wait_ge(multiplied, st.number + 1)
                    sg = halves(sgate[:, (st.j // 2 + k0) % 2, :])
                    tt(sg, halves(bank[st.slot][:, :]), sg, ALU.mult).then_inc(emptied[st.slot], 1)
                    dve.wait_ge(emptied[st.slot], st.uses + 1)
                    dve.sem_inc(sem("hidden_pair"), 1)
                    ahead(st)
                    at_ = st.at(lambda j: 2 * (j // 2))
                    both = slice(at_, at_ + 2) if not st.per else bass.ds(at_, 2)
                    dve.wait_ge(sem("h_high"), h0 + st.j // 2 + 1 + more)
                    tt(h_low[:, both, :], sg, h_high[:, both, :].bitcast(F32), ALU.subtract).then_inc(sem("h_low"), 1)
                    dve.wait_ge(sem("h_low"), h0 + st.j // 2 + 1 + more)
                    dve.sem_inc(sem("sgate_free"), 1)
                panels_of(dve, jb, one, ahead=2)

                for j in range(DC):
                    st = Step(jo.first, j, 0, False)
                    if j < DC - 1:
                        low_ahead(jo, st)
                    dve.wait_ge(multiplied, st.number + 1)
                    stt(xT[:, j, :], bank[st.slot][:, 0:T], 0.5, xT[:, j, :], ALU.mult, ALU.add).then_inc(emptied[st.slot], 1)
                settle(f"ffn_out{i}{s}")

            def ple(i):
                jp, jb = by_name[f"proj{i}"], by_name[f"ple{i}"]
                k0 = pairs_done[0]
                pairs_done[0] += 4
                low_ahead(jp, Step(jp.first, 0, 0, False))
                dve.wait_ge(chJ.free, 4 * (i + 1))
                for j in range(4):
                    st = Step(jb.first, j, 0, False)
                    if j < 3:
                        low_ahead(jb, st)
                    dve.wait_ge(emptied[st.slot], st.uses + 1)
                    sg = sgate[:, (j + k0) % 2, :]
                    link(tt(sg, projected[:, 512 * j:512 * j + 512], sg, ALU.mult))
                    x_ = xT[:, 2 * j:2 * j + 2, :]
                    tt(x_, x_, halves(sg), ALU.add).then_inc(sem("sgate_free"), 1)
                dve.wait_ge(sem("sgate_free"), pairs_done[0] + 2)

            do_norm("ffn00")
            ffn(0, 0)
            do_norm("mix0")
            dve.wait_ge(sem("pos_in"), 48)
            R = slice(0, ROPE)
            link(dve.tensor_copy(posf[R, :], posi[R, :].bitcast(I32)))
            link(ts(ang[R, 0], posf[R, :], freq[R, 0:1], ALU.mult))
            link(ts(ang[R, 1], ang[R, 0], INV_TWO_PI, ALU.mult))
            link(ts(ang[R, 1], ang[R, 1], MAGIC, ALU.add))
            link(ts(ang[R, 1], ang[R, 1], -MAGIC, ALU.add))
            for part_ in TWO_PI_PARTS:
                link(stt(ang[R, 0], ang[R, 1], -part_, ang[R, 0], ALU.mult, ALU.add))
            link(ts(ang[R, 0], ang[R, 0], 3.1415925, ALU.min, -3.1415925, ALU.max))
            dve.sem_inc(sem("angles"), 1)
            dve.wait_ge(sem("sines"), 2)
            link(tt(cosT[R, :], cosT[R, :], cosT[R, :], ALU.mult))
            ts(cosT[R, :], cosT[R, :], -2.0, ALU.mult, 1.0, ALU.add)
            link(ts(sinT[0:32, :], sinT[0:32, :], -1.0, ALU.mult))
            for name, dst in (("cq", cqT), ("ckv", None)):
                st = Step(by_name[name].first, 0, 0, False)
                dve.wait_ge(multiplied, st.number + 1)
                bk = bank[st.slot]
                if dst is not None:
                    link2 = dve.tensor_copy(dst, halves(bk[:, :]))
                else:
                    dve.tensor_copy(ckvT, bk[:, 0:T].rearrange("p (c t) -> p c t", c=1))
                    link2 = dve.tensor_copy(krT[R, :], bk[R, T:2 * T])
                link2.then_inc(emptied[st.slot], 1)
                dve.wait_ge(emptied[st.slot], st.uses + 1)
            do_norm("cq")
            do_norm("ckv")

            def rotate(dst, src):
                link(tt(rope_sw[R, :], rope_sw[R, :], sinT[R, :], ALU.mult))
                link(tt(src, src, cosT[R, :], ALU.mult))
                link(tt(dst, src, rope_sw[R, :], ALU.add))
                dve.sem_inc(sem("rope_go"), 1)

            dve.sem_inc(sem("rope_go"), 1)
            dve.wait_ge(sem("swapped"), 1)
            rotate(krT[R, :], krT[R, :])
            for h in range(MLA_HEADS):
                st = Step(by_name["uq"].first, h, 0, False)
                dve.wait_ge(emptied[st.slot], st.uses + 1)
                rotate(qrT[R, h, :], rope_in[R, :])
            for i in L:
                dve.wait_ge(sem("p_high"), i + 1)
                tt(p_low[:, i], pT[:, i], p_high[:, i].bitcast(F32), ALU.subtract).then_inc(sem("p_low"), 1)
            attention("mla")
            dve.sem_inc(sem("attended"), 1)
            o_low(6, n_high)
            empties("mla_o", add_pair(1.0))
            settle("mla_o")
            do_norm("ffn01")
            low_after("mla_o")
            ffn(0, 1)
            do_norm("ple0")
            ple(0)
            do_norm("ffn10")
            low_after("ple0")
            ffn(1, 0)
            do_norm("mix1")
            low_after("ffn_out10")
            for name in ("fq", "fk", "fv", "ff"):
                panels_of(dve, by_name[name], lambda st: low_ahead(by_name[name], st), ahead=2)
            st = Step(by_name["ff"].first, 0, 0, False)
            dve.wait_ge(multiplied, st.number + 1)
            f3 = [ftmp[:, k].rearrange("p (t h) -> p t h", t=TT) for k in range(6)]
            fb = bass.AP(fbias.tensor, fbias.offset, [list(fbias.ap[0]), [0, TT], [1, FOX_HEADS]])
            tt(f3[0], bank[st.slot][:, :].rearrange("p (t n) -> p t n", t=TT)[:, :, 0:FOX_HEADS], fb, ALU.add)\
                .then_inc(emptied[st.slot], 1)
            dve.wait_ge(emptied[st.slot], st.uses + 1)
            link(stt(f3[1], f3[0], -1.0, f3[0], ALU.mult, ALU.max))
            dve.sem_inc(sem("forget"), 1)
            dve.wait_ge(sem("fexp"), 1)
            link(ts(f3[2], f3[1], 1.0, ALU.add))
            dve.sem_inc(sem("forget"), 1)
            link(ts(f3[3], f3[0], 0.0, ALU.min))
            dve.wait_ge(sem("fexp"), 2)
            link(tt(logf, f3[3], f3[2], ALU.subtract))
            dve.sem_inc(sem("forget"), 1)
            for t in range(TT):
                l_ = logf[:, t, :]
                lb = bass.AP(l_.tensor, l_.offset, [list(l_.ap[0]), [1, FOX_HEADS], [0, P]])
                link(dve.tensor_copy(logf_wide[:, t].rearrange("p (h q) -> p h q", h=8), lb))
            dve.sem_inc(sem("forget"), 1)
            ps = psS[chS.take(dve)]
            dve.tensor_copy(cumq, ps[:, 0:16].rearrange("p (t h) -> p t h", t=TT)).then_inc(chS.free, 1)
            for h2 in range(FOX_HEADS // 2):
                ps = psS[chS.take(dve)]
                ts(ncum[:, 2 * h2:2 * h2 + 2, P:3 * P], halves(ps[:, :]), -1.0, ALU.mult)
                ts(ncum[:, 2 * h2:2 * h2 + 2, 0:P], halves(ps[:, :])[:, :, 0:P], -1.0, ALU.mult).then_inc(chS.free, 1)
            dve.wait_ge(chS.free, chS.got)
            attention("fox")
            dve.sem_inc(sem("attended"), 1)
            o_low(10, n_high)
            empties("fox_o", add_pair(1.0))
            settle("fox_o")
            do_norm("ffn11")
            low_after("fox_o")
            ffn(1, 1)
            do_norm("ple1")
            ple(1)
            do_norm("final")


NAMES = ["x", "mem", "rel_bias", "g_mix", "w_in", "w_pool_grp", "pool_scale", "w_pool_out", "w_cmp_k", "w_cmp_v", "pe_k",
         "pe_v", "w_nsa_out", "g_mem", "w_mem_kv", "w_x_out", "w_o", "g_ffn", "w_peer_q", "peer_sub_keys", "peer_u",
         "peer_v", "g_final", "p_2", "positions_2", "ffn_norm_2", "ffn_w_in_2", "ffn_w_out_2", "mix_norm_2",
         "mla_w_down_2", "mla_q_norm_2", "mla_w_uq_2", "mla_kv_norm_2", "mla_w_ukv_2", "mla_w_o_2", "fox_w_in_2",
         "fox_b_f_2", "fox_w_o_2", "ple_norm_2", "ple_w_gate_2", "ple_w_proj_2", "final_norm_2"]


def kernel(**inputs):
    import numpy as np
    import concourse.bacc as bacc
    from concourse.bass_utils import run_bass_kernel_spmd

    n = np.arange(T)[::-1]
    large = 16 + (np.log(np.maximum(n, 1).astype(np.float32) / np.float32(16)) / np.float32(math.log(8)) * np.float32(16)).astype(np.int32)
    bucket = np.where(n < 16, n, np.minimum(large, BUCKETS - 1))
    onehot = (np.arange(BUCKETS)[:, None] == bucket[None, :]).astype(np.float32)
    half = (10000.0 ** (-np.arange(0, ROPE, 2, dtype=np.float64) / ROPE)).astype(np.float32)
    freq = np.concatenate([half, half])[:, None]

    nc = bacc.Bacc("TRN2", target_bir_lowering=False, num_devices=1)
    arrays, aps = {}, {}
    for name in NAMES:
        arr = np.ascontiguousarray(inputs[name])
        arrays[name + "_in"] = arr
        aps[name] = nc.dram_tensor(name + "_in", arr.shape, mybir.dt.from_np(arr.dtype), kind="ExternalInput").ap()
    arrays["onehot_in"], arrays["freq_in"] = onehot, freq
    hot = nc.dram_tensor("onehot_in", onehot.shape, F32, kind="ExternalInput").ap()
    fr = nc.dram_tensor("freq_in", freq.shape, F32, kind="ExternalInput").ap()
    out = nc.dram_tensor("out", (1, T, D), F32, kind="ExternalOutput").ap()
    build(nc, aps, out, hot, fr)
    r = run_bass_kernel_spmd(nc, [arrays], core_ids=[0])
    return r.results[0]["out"]
```
